# Optimizing a Trainium2 kernel written in Bass

```python
import jax, jax.numpy as jnp
from jax import lax
import numpy as np

D_MODEL = 1024
BATCH = 1
SEQ = 1024
DEPTH = 1

CHUNK = 64
HEAD_DIM = 64
RWKV_HEADS = 8
D_RWKV = RWKV_HEADS * HEAD_DIM
SB_HEADS = 8
D_SB = SB_HEADS * HEAD_DIM
DECAY_LORA = 64
AAA_LORA = 64
GATE_LORA = 128
D_FF = 4 * D_MODEL
Q_BLOCK = 128
DEEPNORM_ALPHA = (2.0 * DEPTH) ** 0.25
DEEPNORM_BETA = (8.0 * DEPTH) ** -0.25
LN_EPS = 1e-5
ADALN_EPS = 1e-6
GN_EPS = 64e-5
RW_SIZES = (D_RWKV, D_RWKV, D_RWKV, DECAY_LORA, AAA_LORA, GATE_LORA)
REST_SIZES = (D_SB, D_SB, D_SB, D_MODEL, D_MODEL)
D_SHIFT = sum(RW_SIZES)
D_IN = D_SHIFT + sum(REST_SIZES)

kernel_name = 'rwkv7_stickbreaking_hybrid_deepnorm_adaln'

def _split(t, sizes):
    return jnp.split(t, np.cumsum(sizes)[:-1].tolist(), axis=-1)

def _layernorm(x, g, b):
    x32 = x.astype(jnp.float32)
    mu = jnp.mean(x32, axis=-1, keepdims=True)
    var = jnp.mean(jnp.square(x32 - mu), axis=-1, keepdims=True)
    return (x32 - mu) * lax.rsqrt(var + LN_EPS) * g + b

def _modulate(x, shift, scale):
    x32 = x.astype(jnp.float32)
    mu = jnp.mean(x32, axis=-1, keepdims=True)
    var = jnp.mean(jnp.square(x32 - mu), axis=-1, keepdims=True)
    return (x32 - mu) * lax.rsqrt(var + ADALN_EPS) * (1.0 + scale) + shift

def _rwkv7_scan(r, w, k, v, a, b):
    def step(state, inp):
        r_t, w_t, k_t, v_t, a_t, b_t = inp
        sa = jnp.einsum('bhvk,bhk->bhv', state, a_t)
        state = (state * w_t[:, :, None, :] + sa[..., None] * b_t[:, :, None, :]
                 + v_t[..., None] * k_t[:, :, None, :])
        return state, jnp.einsum('bhvk,bhk->bhv', state, r_t)
    bsz, _, nh, n = r.shape
    xs = tuple(jnp.moveaxis(t, 1, 0) for t in (r, w, k, v, a, b))
    _, y = lax.scan(step, jnp.zeros((bsz, nh, n, n), jnp.float32), xs)
    return jnp.moveaxis(y, 0, 1)

def _stick_breaking(q, k, v):
    bsz, s_len, nh, d = q.shape
    nb = s_len // Q_BLOCK
    scale = d ** -0.5
    qh = q.astype(jnp.float32).transpose(0, 2, 1, 3)
    kh = k.astype(jnp.float32).transpose(0, 2, 1, 3)
    vh = v.astype(jnp.float32).transpose(0, 2, 1, 3)
    qb = qh.reshape(bsz, nh, nb, Q_BLOCK, d).transpose(2, 0, 1, 3, 4)
    key_pos = jnp.arange(s_len)

    def block(args):
        q_blk, i = args
        q_pos = i * Q_BLOCK + jnp.arange(Q_BLOCK)
        mask = key_pos[None, :] < q_pos[:, None]
        z = jnp.einsum('bhqd,bhkd->bhqk', q_blk, kh) * scale
        log_beta = jax.nn.log_sigmoid(z)
        log_1m = jnp.where(mask, jax.nn.log_sigmoid(-z), 0.0)
        between = lax.cumsum(log_1m, axis=3, reverse=True) - log_1m
        att = jnp.where(mask, jnp.exp(log_beta + between), 0.0)
        return jnp.einsum('bhqk,bhkd->bhqd', att, vh)

    o = lax.map(block, (qb, jnp.arange(nb)))
    return o.transpose(1, 0, 3, 2, 4).reshape(bsz, s_len, nh * d)

def _group_norm(y, g, b):
    mu = jnp.mean(y, axis=-1, keepdims=True)
    var = jnp.mean(jnp.square(y - mu), axis=-1, keepdims=True)
    return (y - mu) * lax.rsqrt(var + GN_EPS) * g.reshape(RWKV_HEADS, HEAD_DIM) + b.reshape(RWKV_HEADS, HEAD_DIM)

def _time_mix(h, w_in, mu_shift, rw_w0, rw_w2, rw_a0, rw_a2, rw_g2, rw_kk, rw_ka, rw_rk,
              rw_gn_g, rw_gn_b, w_branch_a, w_branch_b, w_out):
    bsz, s_len, _ = h.shape
    z = h @ w_in
    z_rw, z_rest = z[..., :D_SHIFT], z[..., D_SHIFT:]
    z_prev = jnp.pad(z_rw, ((0, 0), (1, 0), (0, 0)))[:, :s_len]
    z_rw = z_rw + mu_shift * (z_prev - z_rw)
    r, k, v, zw, za, zg = _split(z_rw, RW_SIZES)
    q_sb, k_sb, v_sb, gate_a, gate_b = _split(z_rest, REST_SIZES)

    heads = lambda t: t.reshape(bsz, s_len, RWKV_HEADS, HEAD_DIM).astype(jnp.float32)
    w_log = -jax.nn.softplus(-(rw_w0 + jnp.tanh(zw) @ rw_w2)) - 0.5
    decay = jnp.exp(-jnp.exp(w_log.astype(jnp.float32)))
    a_rate = jax.nn.sigmoid(rw_a0 + za @ rw_a2)
    g = jax.nn.sigmoid(zg) @ rw_g2
    kk = heads(k * rw_kk)
    kk = kk / jnp.maximum(jnp.sqrt(jnp.sum(kk * kk, axis=-1, keepdims=True)), 1e-12)
    k = k * (1.0 + (a_rate - 1.0) * rw_ka)
    rh, kh, vh, ah = heads(r), heads(k), heads(v), heads(a_rate)
    y = _rwkv7_scan(rh, heads(decay), kh, vh, -kk, kk * ah)
    y = _group_norm(y, rw_gn_g, rw_gn_b)
    y = y + jnp.sum(rh * kh * rw_rk, axis=-1, keepdims=True) * vh
    y_a = (y.reshape(bsz, s_len, D_RWKV) * g) @ w_branch_a

    sb_heads = lambda t: t.reshape(bsz, s_len, SB_HEADS, HEAD_DIM)
    o = _stick_breaking(sb_heads(q_sb), sb_heads(k_sb), sb_heads(v_sb))
    y_b = o @ w_branch_b

    merged = jax.nn.sigmoid(gate_a) * y_a + jax.nn.sigmoid(gate_b) * y_b
    return merged @ w_out

def _layer(x, c, w_ada, b_ada, w_in, mu_shift, rw_w0, rw_w2, rw_a0, rw_a2, rw_g2, rw_kk, rw_ka,
           rw_rk, rw_gn_g, rw_gn_b, w_branch_a, w_branch_b, w_out, ln1_g, ln1_b,
           w_ff1, b_ff1, w_ff2, b_ff2, ln2_g, ln2_b):
    ada = jax.nn.silu(c) @ w_ada + b_ada
    sh1, sc1, g1, sh2, sc2, g2 = jnp.split(ada[:, None, :], 6, axis=-1)
    h = _modulate(x, sh1, sc1)
    mix = _time_mix(h, w_in, mu_shift, rw_w0, rw_w2, rw_a0, rw_a2, rw_g2, rw_kk, rw_ka, rw_rk,
                    rw_gn_g, rw_gn_b, w_branch_a, w_branch_b, w_out)
    x = _layernorm(DEEPNORM_ALPHA * x + g1 * mix, ln1_g, ln1_b)
    h = _modulate(x, sh2, sc2)
    ff = jnp.square(jax.nn.relu(h @ w_ff1 + b_ff1)) @ w_ff2 + b_ff2
    return _layernorm(DEEPNORM_ALPHA * x + g2 * ff, ln2_g, ln2_b)

def setup_inputs(seed: int = 0) -> dict:
    key = jax.random.key(seed)
    ks = jax.random.split(key, 28)
    nrm = lambda i, shape, s: jax.random.normal(ks[i], shape, jnp.float32) * s
    L = DEPTH
    beta = DEEPNORM_BETA
    col_scale = jnp.concatenate([
        jnp.ones((2 * D_RWKV,), jnp.float32), jnp.full((D_RWKV,), beta, jnp.float32),
        jnp.ones((DECAY_LORA + AAA_LORA + GATE_LORA + 2 * D_SB,), jnp.float32),
        jnp.full((D_SB,), beta, jnp.float32), jnp.ones((2 * D_MODEL,), jnp.float32)])
    return {
        'x': nrm(0, (BATCH, SEQ, D_MODEL), 1.0),
        'c': nrm(1, (BATCH, D_MODEL), 1.0),
        'w_ada': nrm(2, (L, D_MODEL, 6 * D_MODEL), D_MODEL ** -0.5),
        'b_ada': nrm(3, (L, 6 * D_MODEL), 0.02),
        'w_in': nrm(4, (L, D_MODEL, D_IN), D_MODEL ** -0.5) * col_scale,
        'mu_shift': jax.random.uniform(ks[5], (L, D_SHIFT), jnp.float32),
        'rw_w0': jax.random.uniform(ks[6], (L, D_RWKV), jnp.float32, -6.0, 1.0),
        'rw_w2': nrm(7, (L, DECAY_LORA, D_RWKV), 0.1 * DECAY_LORA ** -0.5),
        'rw_a0': nrm(8, (L, D_RWKV), 0.5),
        'rw_a2': nrm(9, (L, AAA_LORA, D_RWKV), 0.5 * AAA_LORA ** -0.5),
        'rw_g2': nrm(10, (L, GATE_LORA, D_RWKV), GATE_LORA ** -0.5),
        'rw_kk': 0.85 + nrm(11, (L, D_RWKV), 0.05),
        'rw_ka': 1.0 + nrm(12, (L, D_RWKV), 0.05),
        'rw_rk': nrm(13, (L, RWKV_HEADS, HEAD_DIM), 0.1),
        'rw_gn_g': 1.0 + nrm(14, (L, D_RWKV), 0.05),
        'rw_gn_b': nrm(15, (L, D_RWKV), 0.02),
        'w_branch_a': nrm(16, (L, D_RWKV, D_MODEL), beta * D_RWKV ** -0.5),
        'w_branch_b': nrm(17, (L, D_SB, D_MODEL), beta * D_SB ** -0.5),
        'w_out': nrm(18, (L, D_MODEL, D_MODEL), beta * D_MODEL ** -0.5),
        'ln1_g': 1.0 + nrm(19, (L, D_MODEL), 0.05),
        'ln1_b': nrm(20, (L, D_MODEL), 0.02),
        'w_ff1': nrm(21, (L, D_MODEL, D_FF), beta * D_MODEL ** -0.5),
        'b_ff1': nrm(22, (L, D_FF), 0.02),
        'w_ff2': nrm(23, (L, D_FF, D_MODEL), beta * D_FF ** -0.5),
        'b_ff2': nrm(24, (L, D_MODEL), 0.02),
        'ln2_g': 1.0 + nrm(25, (L, D_MODEL), 0.05),
        'ln2_b': nrm(26, (L, D_MODEL), 0.02),
    }

def reference(x, c, w_ada, b_ada, w_in, mu_shift, rw_w0, rw_w2, rw_a0, rw_a2, rw_g2, rw_kk, rw_ka,
              rw_rk, rw_gn_g, rw_gn_b, w_branch_a, w_branch_b, w_out, ln1_g, ln1_b,
              w_ff1, b_ff1, w_ff2, b_ff2, ln2_g, ln2_b):
    in_dtype = x.dtype
    layer_params = (w_ada, b_ada, w_in, mu_shift, rw_w0, rw_w2, rw_a0, rw_a2, rw_g2, rw_kk, rw_ka,
                    rw_rk, rw_gn_g, rw_gn_b, w_branch_a, w_branch_b, w_out, ln1_g, ln1_b,
                    w_ff1, b_ff1, w_ff2, b_ff2, ln2_g, ln2_b)
    for l in range(DEPTH):
        x = _layer(x, c, *[p[l] for p in layer_params])
    return x.astype(in_dtype)


_drawn_inputs = setup_inputs


def setup_inputs(seed=0):
    import zlib

    import numpy as np

    out = dict(_drawn_inputs(seed))
    spreads = {}
    factors = {'b_ada': 5.811,
     'rw_w2': 8.0,
     'rw_a0': 5.136,
     'rw_a2': 4.366,
     'rw_kk': 5.751,
     'rw_ka': 5.86,
     'rw_rk': 2.719,
     'rw_gn_g': 22.148,
     'rw_gn_b': 61.392,
     'ln1_b': 2.959,
     'b_ff1': 8.0,
     'b_ff2': 5.849,
     'ln2_b': 2.806}
    for name, (base, spread) in spreads.items():
        noise = np.random.default_rng([zlib.crc32(name.encode()), seed]).standard_normal(out[name].shape)
        drawn = base * np.exp(spread * noise) if base else spread * noise
        out[name] = __import__('jax').numpy.asarray(drawn.astype(out[name].dtype))
    for name, factor in factors.items():
        out[name] = (out[name] * factor).astype(out[name].dtype)
    return out
```

```python
from contextlib import ExitStack

import numpy as np

import concourse.bass as bass
from concourse import mybir

F32 = mybir.dt.float32
BF16 = mybir.dt.bfloat16
ALU = mybir.AluOpType
ACT = mybir.ActivationFunctionType
ds = bass.ds

P = 128
SEQ = 1024
D = 1024
KT = D // P
TT = SEQ // P
HALF = 512
DR = 512
PAIRS = DR // P
HD = 64
DFF = 4 * D
LORA_W, LORA_A, LORA_G = 64, 64, 128
D_SHIFT = 3 * DR + LORA_W + LORA_A + LORA_G
NSH = D_SHIFT // P
COL_Q, COL_K, COL_V = D_SHIFT, D_SHIFT + DR, D_SHIFT + 2 * DR
COL_GA, COL_GB = D_SHIFT + 3 * DR, D_SHIFT + 3 * DR + D
CH = 64
ALPHA = 2.0 ** 0.25
LN_EPS, ADALN_EPS, GN_EPS = 1e-5, 1e-6, 64e-5
DECAY = float(np.exp(-0.5))
LEVELS = (2, 4, 8, 16)

ROWS = {}
_at = 0
for _name, _n in (("mu", NSH), ("w0", 4), ("a0", 4), ("kk", 4), ("ka", 4), ("rk", 4), ("gng", 4), ("gnb", 4),
                  ("bff1", DFF // P), ("sh1", KT), ("sc1", KT), ("sh2", KT), ("sc2", KT), ("c", KT)):
    ROWS[_name] = (_at, _n)
    _at += _n
NROWS = _at

CT = {n: i for i, n in enumerate(("ident", "strictT", "inclT", "pairT", "m2", "m4", "m8", "m16", "bones", "neg", "misc"))}


def constants():
    i, j = np.meshgrid(np.arange(P), np.arange(P), indexing="ij")
    same = i // CH == j // CH
    t = np.zeros((P, len(CT), P), np.float32)
    t[:, CT["ident"]] = i == j
    t[:, CT["strictT"]] = same & (i < j)
    t[:, CT["inclT"]] = same & (i <= j)
    t[:, CT["pairT"]] = (i // 2 == j // 2) & (i < j)
    for s in LEVELS:
        t[:, CT[f"m{s}"]] = (i // (2 * s) == j // (2 * s)) & (i % (2 * s) >= s) & (j % (2 * s) < s)
    t[:, CT["bones"]] = i // HD == j // HD
    t[:, CT["neg"]] = np.where(j >= i, np.float32(-1e30), 0)
    t[:, CT["misc"], 0] = i[:, 0] % CH < CH // 2
    t[:, CT["misc"], 1] = i[:, 0] % CH >= CH // 2
    t[:, CT["misc"], 2] = ADALN_EPS
    t[:, CT["misc"], 3] = LN_EPS
    t[:, CT["misc"], 4] = GN_EPS
    reset = np.ones((P, HALF), np.float32)
    reset[:, ::CH] = 0
    return t, reset


def credit(eng, sems):
    for s in sems:
        eng.sem_inc(s, 1)


class Net:
    pass


def split_stream(es, nc, tag, count, units, source, w_used):
    stage = [es.enter_context(nc.sbuf_tensor(f"{tag}_stage{u}", [P, KT, P], F32)) for u in range(units)]
    hi = [es.enter_context(nc.sbuf_tensor(f"{tag}_whi{u}", [P, KT, P], BF16)) for u in range(units)]
    lo = [es.enter_context(nc.sbuf_tensor(f"{tag}_wlo{u}", [P, KT, P], BF16)) for u in range(units)]
    loaded = [nc.alloc_semaphore(f"{tag}_loaded{u}") for u in range(units)]
    hi_ready = [nc.alloc_semaphore(f"{tag}_hi_ready{u}") for u in range(units)]
    lo_ready = [nc.alloc_semaphore(f"{tag}_lo_ready{u}") for u in range(units)]

    def load(sp):
        with sp.Fori(0, count) as i:
            col = sp.snap(i * P)
            for u in range(units):
                for w in {0: (0,), 1: range(1, units)}.get(u, ()):
                    sp.wait_ge(lo_ready[w], i + 1)
                parts = source(u, col)
                for dst, src in parts:
                    sp.dma_start(stage[u][:, dst, :], src).then_inc(loaded[u], 16)

    def split_hi(act, i, u):
        act.wait_ge(loaded[u], (i + 1) * (16 * len(source(u, 0))))
        act.wait_ge(w_used[u], i + 1)
        act.activation(hi[u][:], stage[u][:], ACT.Copy).then_inc(hi_ready[u], 1)

    def cut_lo(pool, i, u):
        pool.wait_ge(hi_ready[u], i + 1)
        pool.tensor_tensor(lo[u][:], stage[u][:], hi[u][:], ALU.subtract).then_inc(lo_ready[u], 1)

    def split_lo(pool):
        credit(pool, lo_ready)
        with pool.Fori(0, count) as i:
            for u in range(units):
                cut_lo(pool, i, u)

    st = Net()
    st.stage, st.hi, st.lo, st.loaded, st.hi_ready, st.lo_ready = stage, hi, lo, loaded, hi_ready, lo_ready
    st.load, st.split_hi, st.split_lo, st.cut_lo = load, split_hi, split_lo, cut_lo
    return st


def gemm_rows(pe, out, whi, wlo, act_hi, act_lo, kts, slots):
    n = len(kts)
    for x, (kt, slot) in enumerate(zip(kts, slots)):
        for y, (w, a) in enumerate(((whi, act_hi), (whi, act_lo), (wlo, act_hi))):
            for h in range(2):
                last = pe.matmul(out[:, h * HALF:(h + 1) * HALF], w[:, kt, :], a[:, slot, h * HALF:(h + 1) * HALF],
                                 start=(x == 0 and y == 0), stop=(x == n - 1 and y == 2))
    return last


def phase_params(nc, g, a):
    with ExitStack() as es:
        rows = es.enter_context(nc.sbuf_tensor("rows", [P, P], F32))
        ps = es.enter_context(nc.psum_tensor("par_ps", [P, HALF], F32))
        s_in = nc.alloc_semaphore("par_in")
        s_tr = nc.alloc_semaphore("par_tr")
        s_z = nc.alloc_semaphore("par_zero")
        s_d = nc.alloc_semaphore("par_dve")
        vecs = {"mu": a["mu_shift"][0], "w0": a["rw_w0"][0], "a0": a["rw_a0"][0], "kk": a["rw_kk"][0], "ka": a["rw_ka"][0],
                "rk": a["rw_rk"][0].rearrange("h d -> (h d)"), "gng": a["rw_gn_g"][0], "gnb": a["rw_gn_b"][0], "bff1": a["b_ff1"][0],
                "sh1": a["b_ada"][0][0:D], "sc1": a["b_ada"][0][D:2 * D], "sh2": a["b_ada"][0][3 * D:4 * D],
                "sc2": a["b_ada"][0][4 * D:5 * D], "c": a["c"][0]}
        n_in = 16 * (len(vecs) + 2)
        block = es.enter_context(nc.Block())

        @block.sync
        def _(sp):
            sp.dma_start(g.const[:], a["const_tiles"]).then_inc(s_in, 16)
            sp.dma_start(g.reset[:], a["const_reset"]).then_inc(s_in, 16)
            sp.wait_ge(s_z, 1)
            for name, v in vecs.items():
                at, n = ROWS[name]
                sp.dma_start(rows[at:at + n, :], v.rearrange("(t p) -> t p", p=P)).then_inc(s_in, 16)

        @block.tensor
        def _(pe):
            pe.wait_ge(s_in, n_in)
            pe.transpose(ps[:, 0:P], rows[:], g.tile("ident")).then_inc(s_tr, 1)

        @block.vector
        def _(dve):
            dve.memset(rows[:], 0.0).then_inc(s_z, 1)
            dve.wait_ge(s_tr, 1)
            dve.tensor_copy(g.cols[:, 0:P], ps[:, 0:P]).then_inc(s_d, 1)
            dve.wait_ge(s_d, 1)
            ka, n = ROWS["ka"]
            dve.tensor_scalar(g.omka[:], g.cols[:, ka:ka + n], -1.0, 1.0, ALU.mult, ALU.add).then_inc(s_d, 1)
            dve.tensor_copy(g.idb[:], g.tile("ident")).then_inc(s_d, 1)
            dve.tensor_copy(g.negb[:], g.tile("neg")).then_inc(s_d, 1)


def phase_ada(nc, g, a):
    with ExitStack() as es:
        sb = lambda n, s, d=F32: es.enter_context(nc.sbuf_tensor(n, s, d))
        sem = lambda n: nc.alloc_semaphore(n)
        wst = [sb(f"ada_w{u}", [P, KT, HALF]) for u in range(2)]
        csig = sb("csig", [P, KT])
        csil = sb("csil", [P, KT])
        cb = sb("cb", [P, KT, P])
        brow = sb("ada_brow", [P, 2, D])
        ps_col = es.enter_context(nc.psum_tensor("ada_col", [P, HALF], F32))
        ps_row = [es.enter_context(nc.psum_tensor(f"ada_row{u}", [P, HALF], F32)) for u in range(2)]
        loaded = [sem(f"ada_loaded{u}") for u in range(2)]
        s_used = [sem(f"ada_used{u}") for u in range(2)]
        s_b, s_sig, s_sil, s_cb, s_row, s_rowe, s_col, s_d = (sem(f"ada_{n}") for n in "b sig sil cb row rowe col d".split())
        w = a["w_ada"][0].rearrange("(k p) n -> p k n", p=P)
        order = [("sh1", 0), ("sh1", 1), ("sc1", 0), ("sc1", 1), ("g1", 0), ("g1", 1),
                 ("sh2", 0), ("sh2", 1), ("sc2", 0), ("sc2", 1), ("g2", 0), ("g2", 1)]
        col_at = {"sh1": 0, "sc1": 8, "sh2": 16, "sc2": 24}
        cc, nc_ = ROWS["c"]
        block = es.enter_context(nc.Block())

        @block.sync
        def _(sp):
            for x in range(2):
                src = a["b_ada"][0][(2 + 3 * x) * D:(3 + 3 * x) * D]
                sp.dma_start(brow[:, x, :], src.partition_broadcast(P)).then_inc(s_b, 16)
            for n in range(len(order)):
                if n >= 2:
                    sp.wait_ge(s_used[n % 2], n // 2)
                sp.dma_start(wst[n % 2][:], w[:, :, n * HALF:(n + 1) * HALF]).then_inc(loaded[n % 2], 16)

        @block.scalar
        def _(act):
            act.activation(csig[:], g.cols[:, cc:cc + KT], ACT.Sigmoid).then_inc(s_sig, 1)

        @block.vector
        def _(dve):
            dve.wait_ge(s_sig, 1)
            dve.tensor_tensor(csil[:], csig[:], g.cols[:, cc:cc + KT], ALU.mult).then_inc(s_sil, 1)
            dve.wait_ge(s_sil, 1)
            dve.tensor_copy(cb[:], csil[:].unsqueeze(2).to_broadcast([P, KT, P])).then_inc(s_cb, 1)
            dve.wait_ge(s_b, 32)
            rows = [n for n, (name, _) in enumerate(order) if name[0] == "g"]
            for x, n in enumerate(rows):
                name, h = order[n]
                dve.wait_ge(s_row, x + 1)
                dst = (g.g1 if name == "g1" else g.g2)[:, h * HALF:(h + 1) * HALF]
                dve.tensor_tensor(dst, ps_row[x % 2][:], brow[:, int(name == "g2"), h * HALF:(h + 1) * HALF], ALU.add).then_inc(s_rowe, 1)
            dve.wait_ge(s_col, 1)
            for name in col_at:
                at, n = ROWS[name]
                src = ps_col[:, col_at[name]:col_at[name] + KT]
                dve.tensor_tensor(g.ada[:, col_at[name]:col_at[name] + KT], src, g.cols[:, at:at + KT], ALU.add).then_inc(s_d, 1)
            dve.wait_ge(s_d, 4)
            for name in ("sc1", "sc2"):
                v = g.ada[:, col_at[name]:col_at[name] + KT]
                dve.tensor_scalar(v, v, 1.0, None, ALU.add).then_inc(s_d, 1)

        @block.tensor
        def _(pe):
            pe.wait_ge(s_cb, 1)
            x = 0
            for n, (name, h) in enumerate(order):
                pe.wait_ge(loaded[n % 2], 16 * (n // 2 + 1))
                wt = wst[n % 2]
                if name[0] == "g":
                    if x >= 2:
                        pe.wait_ge(s_rowe, x - 1)
                    for kt in range(KT):
                        last = pe.matmul(ps_row[x % 2][:], cb[:, kt, :], wt[:, kt, :], start=(kt == 0), stop=(kt == KT - 1))
                        if kt == KT - 1:
                            last.then_inc(s_row, 1)
                    x += 1
                    pe.matmul(ps_col[:, 64:65], wt[:, 0, 0:P], csil[:, 0:1], start=True, stop=True, skip_group_check=True).then_inc(s_used[n % 2], 1)
                else:
                    for c in range(4):
                        col = col_at[name] + 4 * h + c
                        for kt in range(KT):
                            last = pe.matmul(ps_col[:, col:col + 1], wt[:, kt, c * P:(c + 1) * P], csil[:, kt:kt + 1],
                                             start=(kt == 0), stop=(kt == KT - 1))
                    last.then_inc(s_used[n % 2], 1)
            pe.matmul(ps_col[:, 65:66], g.tile("ident"), csil[:, 0:1], start=True, stop=True).then_inc(s_col, 1)


def modulate(nc, g, tag, src, from_dram, scale_at, shift_at, dst_hi, dst_lo):
    with ExitStack() as es:
        sb = lambda n, s, d=F32: es.enter_context(nc.sbuf_tensor(f"{tag}_{n}", s, d))
        sem = lambda n: nc.alloc_semaphore(f"{tag}_{n}")
        x = sb("x", [P, TT, D]) if from_dram is not None else src
        xn = x if from_dram is not None else sb("xn", [P, TT, D])
        st = sb("st", [P, TT, 2, 6]); mv = sb("mv", [P, TT, 2]); rs = sb("rs", [P, TT])
        hf = [sb(f"hf{u}", [P, HALF]) for u in range(2)]
        ps = [es.enter_context(nc.psum_tensor(f"{tag}_ps{u}", [P, HALF], F32)) for u in range(2)]
        s_x, s_st, s_mv, s_sd, s_rs, s_xn, s_tr, s_hf, s_hi, s_lo = (sem(n) for n in "in st mv sd rs xn tr hf hi lo".split())
        block = es.enter_context(nc.Block())

        if from_dram is not None:
            @block.sync
            def _(sp):
                for t in range(TT):
                    sp.dma_start(x[:, t, :], from_dram[t * P:(t + 1) * P, :]).then_inc(s_x, 16)

        @block.vector
        def _(dve):
            for t in range(TT):
                if from_dram is not None:
                    dve.wait_ge(s_x, 16 * TT)
                for h in range(2):
                    dve.bn_stats(st[:, t, h, :], x[:, t, h * HALF:(h + 1) * HALF]).then_inc(s_st, 1)
                dve.wait_ge(s_st, 2 * t + 2)
                dve.bn_aggr(mv[:, t, :], st[:, t, :, :].rearrange("p a b -> p (a b)")).then_inc(s_mv, 1)
            dve.wait_ge(s_sd, 1)
            dve.reciprocal(rs[:], rs[:]).then_inc(s_rs, 1)
            dve.wait_ge(s_rs, 1)
            for t in range(TT):
                dve.tensor_scalar(xn[:, t, :], x[:, t, :], mv[:, t, 0:1], rs[:, t:t + 1], ALU.subtract, ALU.mult).then_inc(s_xn, 1)
            for n in range(2 * KT):
                dve.wait_ge(s_hf, n + 1)
                kt, h = n % KT, n // KT
                dve.tensor_copy(dst_hi[:, kt, h * HALF:(h + 1) * HALF], hf[n % 2][:]).then_inc(s_hi, 1)

        @block.tensor
        def _(pe):
            for n in range(2 * KT):
                kt, h = n % KT, n // KT
                pe.wait_ge(s_xn, 4 * h + 4)
                if n >= 2:
                    pe.wait_ge(s_hf, n - 1)
                for j in range(4):
                    last = pe.transpose(ps[n % 2][:, j * P:(j + 1) * P], xn[:, 4 * h + j, kt * P:(kt + 1) * P], g.tile("ident"))
                last.then_inc(s_tr, 1)

        @block.scalar
        def _(act):
            act.wait_ge(s_mv, TT)
            act.activation(rs[:], mv[:, :, 1], ACT.Sqrt, bias=g.misc(2)).then_inc(s_sd, 1)
            for n in range(2 * KT):
                kt, h = n % KT, n // KT
                act.wait_ge(s_tr, n + 1)
                if n >= 2:
                    act.wait_ge(s_lo, n - 1)
                act.activation(hf[n % 2][:], ps[n % 2][:], ACT.Identity, bias=g.ada[:, shift_at + kt:shift_at + kt + 1],
                               scale=g.ada[:, scale_at + kt:scale_at + kt + 1]).then_inc(s_hf, 1)

        @block.gpsimd
        def _(pool):
            for n in range(2 * KT):
                kt, h = n % KT, n // KT
                pool.wait_ge(s_hi, n + 1)
                pool.tensor_tensor(dst_lo[:, kt, h * HALF:(h + 1) * HALF], hf[n % 2][:],
                                   dst_hi[:, kt, h * HALF:(h + 1) * HALF], ALU.subtract).then_inc(s_lo, 1)


def phase_shifted(nc, g, a):
    with ExitStack() as es:
        sem = lambda n: nc.alloc_semaphore(n)
        w_used = [sem(f"zs_used{u}") for u in range(2)]
        s_raw = [sem(f"zs_raw{u}") for u in range(2)]
        s_diff = [sem(f"zs_diff{u}") for u in range(2)]
        s_shift = [sem(f"zs_shift{u}") for u in range(2)]
        s_zero = sem("zs_zero")
        raw = [es.enter_context(nc.sbuf_tensor(f"zs_rawt{u}", [P, SEQ + 1], F32)) for u in range(2)]
        diff = [es.enter_context(nc.sbuf_tensor(f"zs_dift{u}", [P, SEQ], F32)) for u in range(2)]
        ps = [es.enter_context(nc.psum_tensor(f"zs_ps{u}", [P, SEQ], F32)) for u in range(2)]
        w = a["w_in"][0].rearrange("(k p) n -> p k n", p=P)
        steps = NSH // 2
        ws = split_stream(
            es, nc, "zs", steps, 2, lambda u, i: [(slice(0, KT), w[:, :, ds(i * 2 + u * P, P)])], w_used)
        block = es.enter_context(nc.Block())
        block.sync(ws.load)
        block.gpsimd(ws.split_lo)

        @block.tensor
        def _(pe):
            credit(pe, w_used)
            with pe.Fori(0, steps) as i:
                for u in range(2):
                    pe.wait_ge(ws.lo_ready[u], i + 2)
                    pe.wait_ge(s_raw[u], i + 1)
                    gemm_rows(pe, ps[u], ws.hi[u], ws.lo[u], g.a_hi, g.a_lo, range(KT), range(KT)).then_inc(w_used[u], 1)

        @block.scalar
        def _(act):
            credit(act, s_raw)
            for u in range(2):
                ws.split_hi(act, 0, u)
            act.wait_ge(s_zero, 2)
            with act.Fori(0, steps - 1) as i:
                for u in range(2):
                    act.wait_ge(w_used[u], i + 2)
                    act.wait_ge(s_shift[u], i + 1)
                    act.activation(raw[u][:, 1:SEQ + 1], ps[u][:], ACT.Copy).then_inc(s_raw[u], 1)
                    ws.split_hi(act, i + 1, u)
            for u in range(2):
                act.wait_ge(w_used[u], steps + 1)
                act.wait_ge(s_shift[u], steps)
                act.activation(raw[u][:, 1:SEQ + 1], ps[u][:], ACT.Copy).then_inc(s_raw[u], 1)

        @block.vector
        def _(dve):
            for u in range(2):
                dve.memset(raw[u][:, 0:1], 0.0).then_inc(s_zero, 1)
            mu = ROWS["mu"][0]
            credit(dve, s_shift)
            with dve.Fori(0, steps) as i:
                for u in range(2):
                    dve.wait_ge(s_raw[u], i + 2)
                    dve.tensor_tensor(diff[u][:], raw[u][:, 0:SEQ], raw[u][:, 1:SEQ + 1], ALU.subtract).then_inc(s_diff[u], 1)
                    dve.wait_ge(s_diff[u], i + 1)
                    dve.scalar_tensor_tensor(g.z[:, ds(i * 2 + u, 1), :].rearrange("p a n -> p (a n)"), diff[u][:],
                                             g.cols[:, ds(i * 2 + (mu + u), 1)],
                                             raw[u][:, 1:SEQ + 1], ALU.mult, ALU.add).then_inc(s_shift[u], 1)


def gemm_tokens(pe, out, act_hi, act_lo, at, whi, wlo, n, slots):
    k = len(slots)
    for x, slot in enumerate(slots):
        for y, (a, w) in enumerate(((act_hi, whi), (act_hi, wlo), (act_lo, whi))):
            last = pe.matmul(out, a[:, slot, at], w[:, x, n], start=(x == 0 and y == 0), stop=(x == k - 1 and y == 2))
    return last


def phase_values(nc, g, a):
    with ExitStack() as es:
        sb = lambda n, s, d=F32: es.enter_context(nc.sbuf_tensor(n, s, d))
        sem = lambda n: nc.alloc_semaphore(n)
        w = a["w_in"][0].rearrange("(k p) n -> p k n", p=P)
        stage, hi, lo = sb("v_stage", [P, KT, DR]), sb("v_whi", [P, KT, DR], BF16), sb("v_wlo", [P, KT, DR], BF16)
        ps = [es.enter_context(nc.psum_tensor(f"v_ps{u}", [P, DR], F32)) for u in range(2)]
        s_w, s_hi, s_lo = sem("v_in"), sem("v_hi"), sem("v_lo")
        s_mm = [sem(f"v_mm{u}") for u in range(2)]
        s_out = [sem(f"v_out{u}") for u in range(2)]
        block = es.enter_context(nc.Block())

        @block.sync
        def _(sp):
            sp.dma_start(stage[:], w[:, :, COL_V:COL_V + DR]).then_inc(s_w, 16)

        @block.scalar
        def _(act):
            act.wait_ge(s_w, 16)
            for kt in range(KT):
                act.activation(hi[:, kt, :], stage[:, kt, :], ACT.Copy).then_inc(s_hi, 1)
            credit(act, s_out)
            with act.Fori(0, TT // 2) as i:
                for u in range(2):
                    act.wait_ge(s_mm[u], i + 1)
                    act.activation(g.v[:, ds(i * 2 + u, 1), :].rearrange("p a n -> p (a n)"), ps[u][:], ACT.Copy).then_inc(s_out[u], 1)

        @block.gpsimd
        def _(pool):
            for kt in range(KT):
                pool.wait_ge(s_hi, kt + 1)
                pool.tensor_tensor(lo[:, kt, :], stage[:, kt, :], hi[:, kt, :], ALU.subtract).then_inc(s_lo, 1)

        @block.tensor
        def _(pe):
            pe.wait_ge(s_lo, KT)
            with pe.Fori(0, TT // 2) as i:
                for u in range(2):
                    pe.wait_ge(s_out[u], i + 1)
                    gemm_tokens(pe, ps[u][:], g.a_hi, g.a_lo, ds(i * (2 * P) + u * P, P), hi, lo,
                                slice(0, DR), range(KT)).then_inc(s_mm[u], 1)


def phase_stick(nc, g, a):
    with ExitStack() as es:
        sb = lambda n, s, d=F32: es.enter_context(nc.sbuf_tensor(n, s, d))
        sem = lambda n: nc.alloc_semaphore(n)
        w = a["w_in"][0].rearrange("(k p) n -> p k n", p=P)
        qk = [sb("qs", [P, SEQ]), sb("ks", [P, SEQ])]
        vs = sb("vs", [P, TT, P])
        att = [sb(f"att{b}", [P, SEQ]) for b in range(3)]
        rest = [sb(f"rest{b}", [P, SEQ]) for b in range(3)]
        prod = [sb(f"prod{b}", [P, SEQ + 1]) for b in range(2)]
        attT = [sb(f"attT{b}", [P, TT, P]) for b in range(2)]
        zps = [es.enter_context(nc.psum_tensor(f"z_ps{b}", [P, SEQ], F32)) for b in range(2)]
        trps = [es.enter_context(nc.psum_tensor(f"tr_ps{b}", [P, HALF], F32)) for b in range(2)]
        ops = es.enter_context(nc.psum_tensor("o_ps", [P, SEQ], F32))
        w_used = [sem(f"sb_used{u}") for u in range(2)]
        s_one, s_qk, s_vs, s_z, s_sig, s_scan, s_att, s_tr, s_pv, s_ohi, s_olo = (
            sem(f"sb_{n}") for n in "one qk vs z sig scan att tr pv ohi olo".split())
        s_tre = [sem(f"sb_tre{b}") for b in range(2)]
        units = [(e, i) for e in range(2) for i in range(TT)]
        NU = len(units)
        groups = [(n, k0, min(k0 + 4, units[n][1] + 1)) for n in range(NU) for k0 in range(0, units[n][1] + 1, 4)]
        NG = len(groups)
        assert NG % 2 == 0
        of_unit = [[x for x, gr in enumerate(groups) if gr[0] == n] for n in range(NU)]
        ws = split_stream(
            es, nc, "sb", PAIRS, 2, lambda u, i: [(slice(0, KT), w[:, :, ds(i + (COL_Q, COL_K)[u], P)])], w_used)
        block = es.enter_context(nc.Block())
        block.sync(ws.load)

        @block.gpsimd
        def _(pool):
            credit(pool, ws.lo_ready + [s_att])
            with pool.Fori(0, PAIRS) as p:
                for u in range(2):
                    ws.cut_lo(pool, p, u)
                pool.wait_ge(s_pv, p * NU + 1)
                pool.tensor_copy(vs[:], g.v[:, :, ds(p * P, P)]).then_inc(s_vs, 1)
                for n, (e, i) in enumerate(units):
                    nk = (i + 1) * P
                    pool.wait_ge(s_scan, p * NU + n + 1)
                    pool.tensor_tensor(att[n % 3][:, 0:nk], att[n % 3][:, 0:nk], prod[n % 2][:, SEQ - nk + 1:SEQ + 1],
                                       ALU.mult).then_inc(s_att, 1)

        @block.tensor
        def _(pe):
            credit(pe, w_used + [s_pv])
            with pe.Fori(0, PAIRS) as p:
                for u in range(2):
                    pe.wait_ge(ws.lo_ready[u], p + 2)
                    pe.wait_ge(s_sig, p * NU + 1)
                    gemm_rows(pe, zps[u], ws.hi[u], ws.lo[u], g.a_hi, g.a_lo, range(KT), range(KT)).then_inc(w_used[u], 1)

                def scores(n):
                    e, i = units[n]
                    nk = (i + 1) * P
                    if n >= 2:
                        pe.wait_ge(s_sig, p * NU + n)
                    q = qk[0][HD * e:HD * e + HD, i * P:(i + 1) * P]
                    for b in range(0, nk, HALF):
                        b1 = min(nk, b + HALF)
                        pe.matmul(zps[n % 2][:, b:b1], q, qk[1][HD * e:HD * e + HD, b:b1], start=True, stop=True)
                    pe.matmul(zps[n % 2][:, i * P:nk], g.idb[:], g.negb[:], start=False, stop=True, skip_group_check=True).then_inc(s_z, 1)

                def turn(n):
                    e, i = units[n]
                    pe.wait_ge(s_att, p * NU + n + 2)
                    for x in of_unit[n]:
                        _, k0, k1 = groups[x]
                        pe.wait_ge(s_tre[x % 2], p * (NG // 2) + (x // 2 + 1))
                        for kt in range(k0, k1):
                            last = pe.transpose(trps[x % 2][:, (kt - k0) * P:(kt - k0 + 1) * P], att[n % 3][:, kt * P:(kt + 1) * P], g.tile("ident"))
                        last.then_inc(s_tr, 1)

                def values(n):
                    e, i = units[n]
                    for x in of_unit[n]:
                        pe.wait_ge(s_tre[x % 2], p * (NG // 2) + (x // 2 + 2))
                    for kt in range(i + 1):
                        last = pe.matmul(ops[HD * e:HD * e + HD, i * P:(i + 1) * P], vs[:, kt, HD * e:HD * e + HD],
                                         attT[n % 2][:, kt, :], start=(kt == 0), stop=(kt == i))
                    last.then_inc(s_pv, 1)

                pe.wait_ge(s_qk, p * 2 + 2)
                scores(0)
                scores(1)
                pe.wait_ge(s_vs, p + 1)
                pe.wait_ge(s_olo, p + 1)
                for n in range(NU):
                    if n + 2 < NU:
                        scores(n + 2)
                    turn(n)
                    if n >= 1:
                        values(n - 1)
                values(NU - 1)

        def evacuate(eng, p, n, x):
            _, k0, k1 = groups[x]
            eng.wait_ge(s_tr, p * NG + x + 1)
            eng.wait_ge(s_pv, p * NU + max(n, 1))
            dst = attT[n % 2][:, k0:k1, :].rearrange("p a n -> p (a n)")
            src = trps[x % 2][:, 0:(k1 - k0) * P]
            if x % 2:
                eng.activation(dst, src, ACT.Copy).then_inc(s_tre[1], 1)
            else:
                eng.tensor_copy(dst, src).then_inc(s_tre[0], 1)

        @block.scalar
        def _(act):
            def sigmoids(p, n):
                e, i = units[n]
                nk = (i + 1) * P
                act.wait_ge(s_z, p * NU + n + 1)
                if n >= 3:
                    act.wait_ge(s_tr, p * NG + of_unit[n - 3][-1] + 1)
                    act.wait_ge(s_scan, p * NU + n - 2)
                act.activation(att[n % 3][:, 0:nk], zps[n % 2][:, 0:nk], ACT.Sigmoid, scale=HD ** -0.5)
                act.activation(rest[n % 3][:, 0:nk], zps[n % 2][:, 0:nk], ACT.Sigmoid, scale=-HD ** -0.5).then_inc(s_sig, 1)

            credit(act, [s_sig, s_tre[1]])
            with act.Fori(0, PAIRS) as p:
                for u in range(2):
                    ws.split_hi(act, p, u)
                for u in range(2):
                    act.wait_ge(w_used[u], p + 2)
                    act.activation(qk[u][:], zps[u][:], ACT.Copy).then_inc(s_qk, 1)
                sigmoids(p, 0)
                sigmoids(p, 1)
                for n in range(NU):
                    if n + 2 < NU:
                        sigmoids(p, n + 2)
                    for x in of_unit[n]:
                        if x % 2:
                            evacuate(act, p, n, x)
                act.wait_ge(s_pv, p * NU + (NU + 1))
                act.activation(g.c_hi[:, ds(p + PAIRS, 1), :].rearrange("p a n -> p (a n)"), ops[:], ACT.Copy).then_inc(s_ohi, 1)

        @block.vector
        def _(dve):
            for b in range(2):
                dve.memset(prod[b][:, SEQ:SEQ + 1], 1.0).then_inc(s_one, 1)
            dve.wait_ge(s_one, 2)
            credit(dve, [s_tre[0], s_olo])

            def scan(p, n):
                e, i = units[n]
                nk = (i + 1) * P
                dve.wait_ge(s_sig, p * NU + n + 2)
                dve.wait_ge(s_att, p * NU + max(n, 1))
                m = rest[n % 3][:, 0:nk][:, ::-1]
                dve.tensor_tensor_scan(prod[n % 2][:, SEQ - nk:SEQ][:, ::-1], m, m, 1.0, ALU.mult, ALU.bypass).then_inc(s_scan, 1)

            with dve.Fori(0, PAIRS) as p:
                scan(p, 0)
                for n in range(NU):
                    if n + 1 < NU:
                        scan(p, n + 1)
                    for x in of_unit[n]:
                        if x % 2 == 0:
                            evacuate(dve, p, n, x)
                dve.wait_ge(s_ohi, p + 1)
                dve.tensor_tensor(g.c_lo[:, ds(p + PAIRS, 1), :].rearrange("p a n -> p (a n)"), ops[:],
                                  g.c_hi[:, ds(p + PAIRS, 1), :].rearrange("p a n -> p (a n)"), ALU.subtract).then_inc(s_olo, 1)


def phase_recurrence(nc, g, a):
    with ExitStack() as es:
        sb = lambda n, s=(P, HALF), d=F32: es.enter_context(nc.sbuf_tensor(f"rec_{n}", list(s), d))
        sem = lambda n: nc.alloc_semaphore(f"rws_{n}")
        NB, NT, NC = 8, 4, 8
        lora_wa, lora_g = sb("lora_wa", (P, DR)), sb("lora_g", (P, DR))
        wa_s, g_s, pc = sb("wa_s", (P, P)), sb("g_s", (P, P)), sb("pc", (P, 8))
        th, zgs = g.z[:, NSH - 2, :], g.z[:, NSH - 1, :]
        sg, av, gv, cum, cumE, eI, eN = (sb(n) for n in "sg av gv cum cumE eI eN".split())
        eE = zt = cumE
        kkr, tmp, k2, kk = (sb(n) for n in "kkr tmp k2 kk".split())
        ar = sb("ar", (P, NT, 2, P))
        vt = sb("vt")
        X, T = sb("X", (P, NB, P)), sb("T", (P, NB, P))
        flat = lambda t, x: t[:].rearrange("p b n -> p (b n)")[:, x * HALF:(x + 1) * HALF]
        bt, kt_, bh, kh = flat(X, 0), flat(X, 1), flat(T, 0), flat(T, 1)
        bn, kn, vn = (sb(n, (P, NT, P)) for n in "bn kn vn".split())
        rhs = sb("rhs", (P, NB, P))
        ma, mk = (t[:, PAIRS:KT, :].rearrange("p a n -> p (a n)").bitcast(F32).rearrange("p (b x n) -> p b x n", x=2, n=P)
                  for t in (g.c_hi, g.c_lo))
        TTr, st = sb("TT", (P, NB, P)), sb("st", (P, NC + 1, P))
        gt = sb("gt", (P, NC, P))
        sst = sb("sst", (P, PAIRS, P))
        bonus = sb("bonus")
        B = [es.enter_context(nc.psum_tensor(f"rw_ps{b}", [P, HALF], F32)) for b in range(8)]
        names = ("in th zg zero wst lora sg a g kkr sq ss bonusv rk bo cum cumE t k2 ssm rt rn kk kka eI eN eE AT RT VT BT KT BhT KhT "
                 "M1 M1e pair TT0 M2 M2e nat natE mv mvE T1 T1e X Xe TX T Tt Tte u ue nu wm tw pq Z ze G ge H S ch Y ysb mean yc sqy var sd ri "
                 "y1 y2 y3 y4 yhi ylo end").split()
        s = {n: sem(n) for n in names}
        U, Um, Wm, PQ = rhs, T, X, rhs
        block = es.enter_context(nc.Block())
        IT = lambda p, f, k, j: p * k + (4 * f * k + j)
        wcb = eI[:, CH - 1::CH].unsqueeze(2).to_broadcast([P, NC, CH])
        c8 = lambda t: t.rearrange("p (c n) -> p c n", n=CH)
        c4 = lambda t: t[:].rearrange("p (j n) -> p j n", n=P)
        bank = lambda b: B[b][:].rearrange("p (j n) -> p j n", n=P)
        col = lambda n: pc[:, n:n + 1]
        W0, A0, KK, KA, RK, GG, GB, OMKA = range(8)
        zs = lambda off, p, f: g.z[:, ds(p + off, 1), f * HALF:(f + 1) * HALF].rearrange("p a n -> p (a n)")

        @block.sync
        def _(sp):
            sp.dma_start(lora_wa[0:LORA_W, :], a["rw_w2"][0]).then_inc(s["in"], 16)
            sp.dma_start(lora_wa[LORA_W:P, :], a["rw_a2"][0]).then_inc(s["in"], 16)
            sp.dma_start(lora_g[:], a["rw_g2"][0]).then_inc(s["in"], 16)

        @block.gpsimd
        def _(pool):
            pool.memset(gt[:], 0.0).then_inc(s["zero"], 1)
            pool.memset(st[:], 0.0).then_inc(s["zero"], 1)
            pool.memset(sst[:], 0.0).then_inc(s["zero"], 1)
            credit(pool, [s["end"]])
            pool.wait_ge(s["in"], 48)
            pool.wait_ge(s["zero"], 3)
            at, _ = ROWS["w0"]
            for f in range(2):
                with pool.Fori(0, PAIRS) as p:
                    v = lambda k, j: IT(p, f, k, j)
                    pool.wait_ge(s["end"], v(1, 1))
                    pool.tensor_copy(wa_s[:], lora_wa[:, ds(p * P, P)]).then_inc(s["wst"], 1)
                    pool.tensor_copy(g_s[:], lora_g[:, ds(p * P, P)]).then_inc(s["wst"], 1)
                    for x in range(7):
                        pool.tensor_copy(pc[:, x:x + 1], g.cols[:, ds(p + (at + 4 * x), 1)]).then_inc(s["wst"], 1)
                    pool.tensor_copy(pc[:, OMKA:OMKA + 1], g.omka[:, ds(p, 1)]).then_inc(s["wst"], 1)
                    pool.tensor_copy(st[:, 0, :], sst[:, ds(p, 1), :].rearrange("p a n -> p (a n)")).then_inc(s["wst"], 1)
                    pool.tensor_copy(vt[:], zs(8, p, f)).then_inc(s["VT"], 1)
                    pool.wait_ge(s["cum"], v(1, 1))
                    pool.tensor_tensor(cumE[:], cum[:], sg[:], ALU.subtract).then_inc(s["cumE"], 1)
                    pool.wait_ge(s["eI"], v(1, 1))
                    pool.tensor_tensor(ar[:, :, 1, :], zs(0, p, f).rearrange("p (j n) -> p j n", n=P), c4(eI), ALU.mult).then_inc(s["RT"], 1)
                    pool.wait_ge(s["yhi"], v(1, 1))
                    pool.tensor_tensor(g.c_lo[:, ds(p, 1), f * HALF:(f + 1) * HALF].rearrange("p a n -> p (a n)"), tmp[:],
                                       g.c_hi[:, ds(p, 1), f * HALF:(f + 1) * HALF].rearrange("p a n -> p (a n)"),
                                       ALU.subtract).then_inc(s["ylo"], 1)
                    pool.tensor_copy(sst[:, ds(p, 1), :].rearrange("p a n -> p (a n)"), st[:, NC, :]).then_inc(s["end"], 1)

        @block.scalar
        def _(act):
            act.activation(th[0:LORA_W, :], th[0:LORA_W, :], ACT.Tanh).then_inc(s["th"], 1)
            act.activation(zgs, zgs, ACT.Sigmoid).then_inc(s["th"], 1)
            for f in range(2):
                with act.Fori(0, PAIRS) as p:
                    v = lambda k, j: IT(p, f, k, j)
                    act.wait_ge(s["end"], v(1, 1))
                    act.wait_ge(s["wst"], v(11, 11))
                    act.wait_ge(s["lora"], v(3, 1))
                    act.activation(sg[:], B[0][:], ACT.Sigmoid, bias=col(W0)).then_inc(s["sg"], 1)
                    act.wait_ge(s["lora"], v(3, 2))
                    act.activation(av[:], B[1][:], ACT.Sigmoid, bias=col(A0)).then_inc(s["a"], 1)
                    act.wait_ge(s["lora"], v(3, 3))
                    act.activation(gv[:], B[2][:], ACT.Copy).then_inc(s["g"], 1)
                    act.wait_ge(s["ssm"], v(1, 1))
                    act.activation(kk[:], tmp[:], ACT.Sqrt).then_inc(s["rt"], 1)
                    act.wait_ge(s["cum"], v(1, 1))
                    act.activation(eI[:], cum[:], ACT.Exp, scale=-DECAY).then_inc(s["eI"], 1)
                    act.activation(eN[:], cum[:], ACT.Exp, scale=DECAY).then_inc(s["eN"], 1)
                    act.wait_ge(s["cumE"], v(1, 1))
                    act.activation(eE[:], cumE[:], ACT.Exp, scale=-DECAY).then_inc(s["eE"], 1)
                    act.wait_ge(s["nat"], v(4, 1))
                    act.activation(rhs[:].rearrange("p (e j) n -> p e j n", e=2)[:, :, :, 0:HD],
                                   B[0][:].rearrange("p (j e n) -> p e j n", e=2, n=HD), ACT.Copy).then_inc(s["natE"], 1)
                    for x, (b, dst) in enumerate(((1, bn), (2, kn), (5, vn))):
                        act.wait_ge(s["nat"], v(4, x + 2))
                        act.activation(dst[:].rearrange("p j n -> p (j n)"), B[b][:], ACT.Copy).then_inc(s["natE"], 1)
                    for h in range(2):
                        act.wait_ge(s["T1"], v(2, h + 1))
                        act.activation(T[:, 4 * h:4 * h + 4, :], bank(6 + h), ACT.Copy).then_inc(s["T1e"], 1)
                    act.wait_ge(s["mv"], v(1, 1))
                    act.activation(rhs[:, :, HD:P], B[2][:].rearrange("p (b n) -> p b n", n=HD), ACT.Copy).then_inc(s["mvE"], 1)
                    for lv in range(len(LEVELS)):
                        for h in range(2):
                            act.wait_ge(s["Tt"], v(8, 2 * lv + h + 1))
                            act.activation(TTr[:, 4 * h:4 * h + 4, :], bank(h), ACT.Copy).then_inc(s["Tte"], 1)
                    for h in range(2):
                        act.wait_ge(s["u"], v(2, h + 1))
                        act.activation(U[:, 4 * h:4 * h + 4, :], bank(3 + h), ACT.Copy).then_inc(s["ue"], 1)
                        act.activation(Um[:, 4 * h:4 * h + 4, :], bank(3 + h), ACT.Copy, scale=g.misc(0)).then_inc(s["ue"], 1)
                    for h in range(2):
                        act.wait_ge(s["nu"], v(2, h + 1))
                        act.activation(Wm[:, 4 * h:4 * h + 4, :], bank(6 + h), ACT.Copy, scale=g.misc(1)).then_inc(s["wm"], 1)
                    act.wait_ge(s["G"], v(1, 1))
                    for h in range(2):
                        for e in range(2):
                            r = slice(HD * e, HD * e + HD)
                            act.activation(gt[r, h::2, r], B[h][r, 0:4 * HD].rearrange("p (j n) -> p j n", n=HD), ACT.Copy).then_inc(s["ge"], 1)
                    act.wait_ge(s["Y"], v(1, 1))
                    act.activation(kkr[:], B[2][:], ACT.Copy).then_inc(s["ysb"], 1)
                    act.wait_ge(s["yc"], v(1, 1))
                    act.activation(k2[:], kk[:], ACT.Square).then_inc(s["sqy"], 1)
                    act.wait_ge(s["var"], v(1, 1))
                    act.activation(tmp[:], B[4][:], ACT.Sqrt, bias=g.misc(4), scale=1.0 / HD).then_inc(s["sd"], 1)
                    act.wait_ge(s["y4"], v(1, 1))
                    act.activation(g.c_hi[:, ds(p, 1), f * HALF:(f + 1) * HALF].rearrange("p a n -> p (a n)"), tmp[:], ACT.Copy).then_inc(s["yhi"], 1)

        @block.vector
        def _(dve):
            for f in range(2):
                with dve.Fori(0, PAIRS) as p:
                    v = lambda k, j: IT(p, f, k, j)
                    r_, k_ = zs(0, p, f), zs(4, p, f)
                    dve.wait_ge(s["end"], v(1, 1))
                    dve.wait_ge(s["wst"], v(11, 11))
                    dve.tensor_scalar(kkr[:], k_, col(KK), None, ALU.mult).then_inc(s["kkr"], 1)
                    dve.wait_ge(s["kkr"], v(1, 1))
                    dve.tensor_tensor(tmp[:], kkr[:], kkr[:], ALU.mult).then_inc(s["sq"], 1)
                    dve.wait_ge(s["sg"], v(1, 1))
                    dve.tensor_tensor_scan(cum[:], g.reset[:], sg[:], 0.0, ALU.mult, ALU.add).then_inc(s["cum"], 1)
                    dve.wait_ge(s["a"], v(1, 1))
                    dve.tensor_scalar(k2[:], av[:], col(KA), col(OMKA), ALU.mult, ALU.add).then_inc(s["t"], 1)
                    dve.wait_ge(s["t"], v(1, 1))
                    dve.tensor_tensor(k2[:], k2[:], k_, ALU.mult).then_inc(s["k2"], 1)
                    dve.wait_ge(s["ss"], v(1, 1))
                    dve.tensor_scalar(tmp[:], B[3][:], 1e-24, None, ALU.max).then_inc(s["ssm"], 1)
                    dve.wait_ge(s["k2"], v(1, 1))
                    dve.scalar_tensor_tensor(bonus[:], r_, col(RK), k2[:], ALU.mult, ALU.mult).then_inc(s["rk"], 1)
                    dve.wait_ge(s["rt"], v(1, 1))
                    dve.reciprocal(kk[:], kk[:]).then_inc(s["rn"], 1)
                    dve.wait_ge(s["rn"], v(1, 1))
                    dve.tensor_tensor(kk[:], kkr[:], kk[:], ALU.mult).then_inc(s["kk"], 1)
                    dve.wait_ge(s["eN"], v(1, 1))
                    dve.tensor_tensor(kt_, k2[:], eN[:], ALU.mult).then_inc(s["KT"], 1)
                    dve.wait_ge(s["kk"], v(1, 1))
                    dve.tensor_tensor(tmp[:], kk[:], av[:], ALU.mult).then_inc(s["kka"], 1)
                    dve.wait_ge(s["bo"], v(1, 1))
                    dve.wait_ge(s["VT"], v(1, 1))
                    dve.tensor_tensor(bonus[:], B[4][:], vt[:], ALU.mult).then_inc(s["bonusv"], 1)
                    dve.wait_ge(s["kka"], v(1, 1))
                    dve.tensor_tensor(bt, tmp[:], eN[:], ALU.mult).then_inc(s["BT"], 1)
                    dve.wait_ge(s["eE"], v(1, 1))
                    dve.scalar_tensor_tensor(ar[:, :, 0, :], c4(kk), -1.0, c4(eE), ALU.mult, ALU.mult).then_inc(s["AT"], 1)
                    dve.wait_ge(s["BT"], v(1, 1))
                    dve.tensor_tensor(c8(bh), c8(bt), wcb, ALU.mult).then_inc(s["BhT"], 1)
                    dve.tensor_tensor(c8(kh), c8(kt_), wcb, ALU.mult).then_inc(s["KhT"], 1)
                    masks = g.const[:, CT["strictT"]:CT["strictT"] + 2, :].unsqueeze(1).to_broadcast([P, 2, 2, P])
                    for x, (b, blk) in enumerate(((3, 0), (6, 4), (4, 2), (7, 6))):
                        dve.wait_ge(s["M1"], v(4, x + 1))
                        dve.tensor_tensor(ma[:, blk:blk + 2, :, :], B[b][:].rearrange("p (j x n) -> p j x n", x=2, n=P), masks, ALU.mult).then_inc(s["M1e"], 1)
                    dve.wait_ge(s["M1e"], v(4, 4))
                    full = lambda n, w: g.tile(n).unsqueeze(1).to_broadcast([P, w, P])
                    dve.tensor_tensor(TTr[:], ma[:, :, 0, :], full("pairT", NB), ALU.mult).then_inc(s["pair"], 1)
                    dve.wait_ge(s["pair"], v(1, 1))
                    dve.tensor_tensor(TTr[:], TTr[:], full("ident", NB), ALU.add).then_inc(s["TT0"], 1)
                    for x, (b, blk) in enumerate(((0, 0), (2, 4), (1, 2), (5, 6))):
                        dve.wait_ge(s["M2"], v(4, x + 1))
                        dve.tensor_tensor(mk[:, blk:blk + 2, :, :], B[b][:].rearrange("p (j x n) -> p j x n", x=2, n=P), masks, ALU.mult).then_inc(s["M2e"], 1)
                    for lv, size in enumerate(LEVELS):
                        for h in range(2):
                            dve.wait_ge(s["X"], v(8, 2 * lv + h + 1))
                            dve.tensor_tensor(X[:, 4 * h:4 * h + 4, :], bank(3 + h), full(f"m{size}", 4), ALU.mult).then_inc(s["Xe"], 1)
                        for h in range(2):
                            dve.wait_ge(s["TX"], v(8, 2 * lv + h + 1))
                            dve.tensor_tensor(T[:, 4 * h:4 * h + 4, :], bank(6 + h), T[:, 4 * h:4 * h + 4, :], ALU.add).then_inc(s["T"], 1)
                    for h in range(2):
                        dve.wait_ge(s["tw"], v(2, h + 1))
                        dve.tensor_tensor(PQ[:, 4 * h:4 * h + 4, :], bank(3 + h), U[:, 4 * h:4 * h + 4, :], ALU.add).then_inc(s["pq"], 1)
                    dve.wait_ge(s["Z"], v(1, 1))
                    dve.tensor_tensor(c4(zt), bank(5), ar[:, :, 1, :], ALU.add).then_inc(s["ze"], 1)
                    for c in range(NC):
                        dve.wait_ge(s["ch"], v(NC, c + 1))
                        e = CH * c + CH - 1
                        dve.scalar_tensor_tensor(st[:, c + 1, :], st[:, c, :], eI[:, e:e + 1], bank(6 + c % 2)[:, c // 2, :],
                                                 ALU.mult, ALU.add).then_inc(s["S"], 1)
                    dve.wait_ge(s["mean"], v(1, 1))
                    dve.scalar_tensor_tensor(kk[:], B[3][:], -1.0 / HD, kkr[:], ALU.mult, ALU.add).then_inc(s["yc"], 1)
                    dve.wait_ge(s["sd"], v(1, 1))
                    dve.reciprocal(tmp[:], tmp[:]).then_inc(s["ri"], 1)
                    dve.wait_ge(s["ri"], v(1, 1))
                    dve.tensor_tensor(tmp[:], kk[:], tmp[:], ALU.mult).then_inc(s["y1"], 1)
                    dve.wait_ge(s["y1"], v(1, 1))
                    dve.tensor_scalar(tmp[:], tmp[:], col(GG), col(GB), ALU.mult, ALU.add).then_inc(s["y2"], 1)
                    dve.wait_ge(s["y2"], v(1, 1))
                    dve.tensor_tensor(tmp[:], tmp[:], bonus[:], ALU.add).then_inc(s["y3"], 1)
                    dve.wait_ge(s["y3"], v(1, 1))
                    dve.tensor_tensor(tmp[:], tmp[:], gv[:], ALU.mult).then_inc(s["y4"], 1)

        @block.tensor
        def _(pe):
            ident, bones = g.tile("ident"), g.tile("bones")
            pe.wait_ge(s["th"], 2)
            jobs = [(jp, e) for jp in range(2) for e in range(2)]
            for f in range(2):
                with pe.Fori(0, PAIRS) as p:
                    v = lambda k, j: IT(p, f, k, j)
                    tok = slice(f * HALF, (f + 1) * HALF)
                    pe.wait_ge(s["end"], v(1, 1))
                    pe.wait_ge(s["wst"], v(11, 2))
                    pe.matmul(B[0][:], wa_s[0:LORA_W, :], th[0:LORA_W, tok], start=True, stop=True).then_inc(s["lora"], 1)
                    pe.matmul(B[1][:], wa_s[LORA_W:P, :], g.z[LORA_W:P, NSH - 2, tok], start=True, stop=True).then_inc(s["lora"], 1)
                    pe.matmul(B[2][:], g_s[:], zgs[:, tok], start=True, stop=True).then_inc(s["lora"], 1)
                    pe.wait_ge(s["sq"], v(1, 1))
                    pe.matmul(B[3][:], bones, tmp[:], start=True, stop=True).then_inc(s["ss"], 1)
                    pe.wait_ge(s["rk"], v(1, 1))
                    pe.matmul(B[4][:], bones, bonus[:], start=True, stop=True).then_inc(s["bo"], 1)
                    for left, ready, banks, done in ((bt, ("BT", "AT", "RT", "ssm", "bonusv"), ((3, 4), (6, 7)), "M1"),
                                                     (kt_, ("KT", "sg", "a", "g"), ((0, 1), (2, 5)), "M2")):
                        for n in ready:
                            pe.wait_ge(s[n], v(1, 1))
                        for jp, e in jobs:
                            rows = slice(HD * e, HD * e + HD)
                            for j in (2 * jp, 2 * jp + 1):
                                last = pe.matmul(B[banks[e][jp]][:, (j % 2) * 2 * P:(j % 2 + 1) * 2 * P], left[rows, j * P:(j + 1) * P],
                                                 ar[rows, j, :, :].rearrange("p x n -> p (x n)"), start=True, stop=True)
                            last.then_inc(s[done], 1)
                    pe.wait_ge(s["TT0"], v(1, 1))
                    for h in range(2):
                        for b in range(4):
                            last = pe.transpose(B[6 + h][:, b * P:(b + 1) * P], TTr[:, 4 * h + b, :], ident)
                        last.then_inc(s["T1"], 1)
                    pe.wait_ge(s["M2e"], v(4, 4))
                    for src, n, b in ((None, "AT", 0), (bh, "BhT", 1), (kh, "KhT", 2), (vt, "VT", 5)):
                        pe.wait_ge(s[n], v(1, 1))
                        for j in range(NT):
                            blk = ar[:, j, 0, :] if src is None else src[:, j * P:(j + 1) * P]
                            last = pe.transpose(B[b][:, j * P:(j + 1) * P], blk, ident)
                        last.then_inc(s["nat"], 1)
                    pe.wait_ge(s["natE"], v(4, 4))
                    for b in range(NB):
                        last = pe.matmul(B[2][:, b * HD:(b + 1) * HD], mk[:, b, 0, :], vn[:, b % 4, HD * (b // 4):HD * (b // 4) + HD],
                                         start=True, stop=True)
                    last.then_inc(s["mv"], 1)

                    def product(left, right, b0, done):
                        def half(h):
                            for b in range(4):
                                last = pe.matmul(B[b0 + h][:, b * P:(b + 1) * P], left(4 * h + b), right(4 * h + b), start=True, stop=True)
                            last.then_inc(s[done], 1)
                        return half

                    nT = lambda b: ma[:, b, 0, :]
                    blk = lambda t: lambda b: t[:, b, :]
                    for lv in range(len(LEVELS)):
                        x = product(nT, blk(T), 3, "X")
                        for h in range(2):
                            if lv == 0:
                                pe.wait_ge(s["T1e"], v(2, h + 1))
                            else:
                                pe.wait_ge(s["T"], v(8, 2 * lv - 1 + h))
                            x(h)
                        x = product(blk(TTr), blk(X), 6, "TX")
                        for h in range(2):
                            if lv:
                                pe.wait_ge(s["Tte"], v(8, 2 * lv - 1 + h))
                            pe.wait_ge(s["Xe"], v(8, 2 * lv + h + 1))
                            x(h)
                        for h in range(2):
                            pe.wait_ge(s["T"], v(8, 2 * lv + h + 1))
                            for b in range(4):
                                last = pe.transpose(B[h][:, b * P:(b + 1) * P], T[:, 4 * h + b, :], ident)
                            last.then_inc(s["Tt"], 1)
                    pe.wait_ge(s["mvE"], v(1, 1))
                    x = product(blk(TTr), blk(rhs), 3, "u")
                    for h in range(2):
                        pe.wait_ge(s["Tte"], v(8, 7 + h))
                        x(h)
                    x = product(nT, blk(Um), 6, "nu")
                    for h in range(2):
                        pe.wait_ge(s["ue"], v(4, 2 * h + 2))
                        x(h)
                    x = product(blk(TTr), blk(Wm), 3, "tw")
                    for h in range(2):
                        pe.wait_ge(s["wm"], v(2, h + 1))
                        x(h)
                    pe.wait_ge(s["pq"], v(2, 2))
                    for b in range(NB):
                        e, j = b // 4, b % 4
                        last = pe.matmul(B[5][HD * e:HD * e + HD, j * P:(j + 1) * P], PQ[:, b, 0:HD], ma[:, b, 1, :], start=True, stop=True)
                    last.then_inc(s["Z"], 1)
                    for h in range(2):
                        rows = slice(CH * h, CH * h + CH)
                        for b in range(NB):
                            e, j = b // 4, b % 4
                            r = slice(HD * e, HD * e + HD)
                            last = pe.matmul(B[h][r, j * HD:(j + 1) * HD], PQ[rows, b, 0:HD], bn[rows, j, r], start=True, stop=True)
                    last.then_inc(s["G"], 1)
                    for h in range(2):
                        rows = slice(CH * h, CH * h + CH)
                        for b in range(NB):
                            e, j = b // 4, b % 4
                            r = slice(HD * e, HD * e + HD)
                            o = B[6 + h][r, j * P + HD * e:j * P + HD * e + HD]
                            pe.matmul(o, bn[rows, j, r], PQ[rows, b, HD:P], start=(j == 0), stop=False, skip_group_check=True)
                            pe.matmul(o, kn[rows, j, r], vn[rows, j, r], start=False, stop=False, skip_group_check=True)
                    for b in range(NB):
                        e, j = b // 4, b % 4
                        r = slice(HD * e, HD * e + HD)
                        o = B[2][r, j * P:(j + 1) * P]
                        pe.matmul(o, PQ[:, b, HD:P], ma[:, b, 1, :], start=(j == 0), stop=False, skip_group_check=True)
                        pe.matmul(o, vn[:, j, r], mk[:, b, 1, :], start=False, stop=False, skip_group_check=True)
                    pe.wait_ge(s["ge"], v(4, 4))
                    pe.wait_ge(s["ze"], v(1, 1))
                    for c in range(NC):
                        if c:
                            pe.wait_ge(s["S"], v(NC, c))
                        else:
                            pe.wait_ge(s["wst"], v(11, 11))
                        pe.matmul(B[6 + c % 2][:, (c // 2) * P:(c // 2 + 1) * P], gt[:, c, :], st[:, c, :], start=False, stop=True,
                                  skip_group_check=True).then_inc(s["ch"], 1)
                        last = pe.matmul(B[2][:, c * CH:(c + 1) * CH], st[:, c, :], zt[:, c * CH:(c + 1) * CH], start=False, stop=True,
                                         skip_group_check=True)
                    last.then_inc(s["Y"], 1)
                    pe.wait_ge(s["ysb"], v(1, 1))
                    pe.matmul(B[3][:], bones, kkr[:], start=True, stop=True).then_inc(s["mean"], 1)
                    pe.wait_ge(s["sqy"], v(1, 1))
                    pe.matmul(B[4][:], bones, k2[:], start=True, stop=True).then_inc(s["var"], 1)


def phase_merge(nc, g, a):
    with ExitStack() as es:
        sb = lambda n, s, d=F32: es.enter_context(nc.sbuf_tensor(f"mg_{n}", s, d))
        sem = lambda n: nc.alloc_semaphore(f"mgs_{n}")
        w = a["w_in"][0].rearrange("(k p) n -> p k n", p=P)
        wa = a["w_branch_a"][0].rearrange("(k p) n -> p k n", p=P)
        wb = a["w_branch_b"][0].rearrange("(k p) n -> p k n", p=P)
        w_used = [sem(f"used{u}") for u in range(3)]
        s_ya, s_sa, s_sb, s_pa, s_pb, s_m, s_hi, s_lo = (sem(n) for n in "ya sa sb pa pb m hi lo".split())
        ga, gb, m = sb("ga", [P, SEQ]), sb("gb", [P, SEQ]), sb("m", [P, SEQ])
        ps = [es.enter_context(nc.psum_tensor(f"mg_ps{u}", [P, SEQ], F32)) for u in range(4)]

        def source(u, i):
            if u < 2:
                return [(slice(0, KT), w[:, :, ds(i + (COL_GA, COL_GB)[u], P)])]
            return [(slice(0, PAIRS), wa[:, :, ds(i, P)]), (slice(PAIRS, KT), wb[:, :, ds(i, P)])]

        ws = split_stream(es, nc, "mg", KT, 3, source, w_used)
        block = es.enter_context(nc.Block())
        block.sync(ws.load)

        @block.gpsimd
        def _(pool):
            credit(pool, ws.lo_ready + [s_lo])
            for u in range(3):
                ws.cut_lo(pool, 0, u)

            def finish(i):
                pool.wait_ge(s_hi, i + 1)
                pool.tensor_tensor(g.b_lo[:, ds(i, 1), :].rearrange("p a n -> p (a n)"), m[:],
                                   g.b_hi[:, ds(i, 1), :].rearrange("p a n -> p (a n)"), ALU.subtract).then_inc(s_lo, 1)

            with pool.Fori(0, KT - 1) as i:
                for u in range(3):
                    ws.cut_lo(pool, i + 1, u)
                finish(i)
            finish(KT - 1)

        @block.tensor
        def _(pe):
            credit(pe, w_used)
            with pe.Fori(0, KT) as i:
                for u in range(2):
                    pe.wait_ge(ws.lo_ready[u], i + 2)
                    pe.wait_ge((s_sa, s_sb)[u], i + 1)
                    gemm_rows(pe, ps[u], ws.hi[u], ws.lo[u], g.a_hi, g.a_lo, range(KT), range(KT)).then_inc(w_used[u], 1)
                pe.wait_ge(ws.lo_ready[2], i + 2)
                pe.wait_ge(s_pa, i + 1)
                gemm_rows(pe, ps[2], ws.hi[2], ws.lo[2], g.c_hi, g.c_lo, range(PAIRS), range(PAIRS)).then_inc(s_ya, 1)
                pe.wait_ge(s_pb, i + 1)
                gemm_rows(pe, ps[3], ws.hi[2], ws.lo[2], g.c_hi, g.c_lo, range(PAIRS, KT), range(PAIRS, KT)).then_inc(w_used[2], 1)

        @block.scalar
        def _(act):
            credit(act, [s_sa, s_sb])
            for u in range(3):
                ws.split_hi(act, 0, u)

            def step(i, last):
                for u, (gate, ready, free) in enumerate(((ga, s_sa, s_pa), (gb, s_sb, s_pb))):
                    act.wait_ge(w_used[u], i + 2)
                    act.wait_ge(free, i + 1)
                    act.activation(gate[:], ps[u][:], ACT.Sigmoid).then_inc(ready, 1)
                    if not last:
                        ws.split_hi(act, i + 1, u)
                act.wait_ge(s_m, i + 1)
                act.activation(g.b_hi[:, ds(i, 1), :].rearrange("p a n -> p (a n)"), m[:], ACT.Copy).then_inc(s_hi, 1)
                if not last:
                    ws.split_hi(act, i + 1, 2)

            with act.Fori(0, KT - 1) as i:
                step(i, False)
            step(KT - 1, True)

        @block.vector
        def _(dve):
            credit(dve, [s_pa, s_pb])
            with dve.Fori(0, KT) as i:
                dve.wait_ge(s_sa, i + 2)
                dve.wait_ge(s_ya, i + 1)
                dve.tensor_tensor(ga[:], ga[:], ps[2][:], ALU.mult).then_inc(s_pa, 1)
                dve.wait_ge(s_sb, i + 2)
                dve.wait_ge(w_used[2], i + 2)
                dve.tensor_tensor(gb[:], gb[:], ps[3][:], ALU.mult).then_inc(s_pb, 1)
                dve.wait_ge(s_pb, i + 2)
                dve.wait_ge(s_pa, i + 2)
                dve.wait_ge(s_lo, i + 1)
                dve.tensor_tensor(m[:], ga[:], gb[:], ALU.add).then_inc(s_m, 1)


def phase_out(nc, g, a):
    with ExitStack() as es:
        sb = lambda n, s, d=F32: es.enter_context(nc.sbuf_tensor(f"ou_{n}", s, d))
        sem = lambda n: nc.alloc_semaphore(f"ous_{n}")
        w = a["w_out"][0].rearrange("(k p) n -> p k n", p=P)
        x = a["x"][0].rearrange("(t p) n -> p t n", p=P)
        stage = sb("stage", [P, KT, HALF])
        hi, lo = sb("whi", [P, KT, HALF], BF16), sb("wlo", [P, KT, HALF], BF16)
        xt = [sb(f"x{u}", [P, HALF]) for u in range(2)]
        gm = [sb(f"gm{u}", [P, HALF]) for u in range(2)]
        ps = [es.enter_context(nc.psum_tensor(f"ou_ps{u}", [P, HALF], F32)) for u in range(2)]
        s_w, s_hi, s_lo = (sem(n) for n in "w hi lo".split())
        s_x, s_mm, s_gm, s_done = ([sem(f"{n}{u}") for u in range(2)] for n in "x mm gm done".split())
        steps = TT // 2
        block = es.enter_context(nc.Block())

        @block.sync
        def _(sp):
            for n in range(2):
                if n:
                    sp.wait_ge(s_lo, KT)
                sp.dma_start(stage[:], w[:, :, n * HALF:(n + 1) * HALF]).then_inc(s_w, 16)
                with sp.Fori(0, steps) as i:
                    for u in range(2):
                        sp.wait_ge(s_done[u], i + (n * steps + 1))
                        sp.dma_start(xt[u][:], x[:, ds(i * 2 + u, 1), n * HALF:(n + 1) * HALF].rearrange("p a n -> p (a n)")).then_inc(s_x[u], 16)

        @block.scalar
        def _(act):
            for n in range(2):
                act.wait_ge(s_w, 16 * (n + 1))
                if n:
                    for u in range(2):
                        act.wait_ge(s_mm[u], steps)
                for kt in range(KT):
                    act.activation(hi[:, kt, :], stage[:, kt, :], ACT.Copy).then_inc(s_hi, 1)

        @block.gpsimd
        def _(pool):
            for n in range(2 * KT):
                pool.wait_ge(s_hi, n + 1)
                pool.tensor_tensor(lo[:, n % KT, :], stage[:, n % KT, :], hi[:, n % KT, :], ALU.subtract).then_inc(s_lo, 1)

        @block.tensor
        def _(pe):
            for n in range(2):
                pe.wait_ge(s_lo, KT * (n + 1))
                with pe.Fori(0, steps) as i:
                    for u in range(2):
                        pe.wait_ge(s_gm[u], i + (n * steps + 1))
                        gemm_tokens(pe, ps[u][:], g.b_hi, g.b_lo, ds(i * (2 * P) + u * P, P), hi, lo,
                                    slice(0, HALF), range(KT)).then_inc(s_mm[u], 1)

        @block.vector
        def _(dve):
            credit(dve, s_gm + s_done)
            for n in range(2):
                with dve.Fori(0, steps) as i:
                    for u in range(2):
                        at = n * steps
                        dve.wait_ge(s_mm[u], i + (at + 1))
                        dve.wait_ge(s_done[u], i + (at + 1))
                        dve.tensor_tensor(gm[u][:], ps[u][:], g.g1[:, n * HALF:(n + 1) * HALF], ALU.mult).then_inc(s_gm[u], 1)
                        dve.wait_ge(s_gm[u], i + (at + 2))
                        dve.wait_ge(s_x[u], i * 16 + 16 * (at + 1))
                        dve.scalar_tensor_tensor(g.x1[:, ds(i * 2 + u, 1), n * HALF:(n + 1) * HALF].rearrange("p a n -> p (a n)"),
                                                 xt[u][:], ALPHA, gm[u][:], ALU.mult, ALU.add).then_inc(s_done[u], 1)


def norm_affine(nc, g, tag, gain, bias, to_dram):
    with ExitStack() as es:
        sb = lambda n, s, d=F32: es.enter_context(nc.sbuf_tensor(f"{tag}_{n}", s, d))
        sem = lambda n: nc.alloc_semaphore(f"{tag}s_{n}")
        rows = sb("rows", [P, 2, D])
        st, mv, rs = sb("st", [P, TT, 2, 6]), sb("mv", [P, TT, 2]), sb("rs", [P, TT])
        s_in, s_st, s_mv, s_sd, s_rs, s_xn, s_g, s_b, s_out = (sem(n) for n in "in st mv sd rs xn g b out".split())
        block = es.enter_context(nc.Block())

        @block.sync
        def _(sp):
            for x, v in enumerate((gain, bias)):
                sp.dma_start(rows[:, x, :], v.partition_broadcast(P)).then_inc(s_in, 16)
            if to_dram is not None:
                for t in range(TT):
                    sp.wait_ge(s_b, t + 1)
                    sp.dma_start(to_dram[t * P:(t + 1) * P, :], g.x1[:, t, :]).then_inc(s_out, 16)
                sp.wait_ge(s_out, 16 * TT)

        @block.vector
        def _(dve):
            for t in range(TT):
                for h in range(2):
                    dve.bn_stats(st[:, t, h, :], g.x1[:, t, h * HALF:(h + 1) * HALF]).then_inc(s_st, 1)
                dve.wait_ge(s_st, 2 * t + 2)
                dve.bn_aggr(mv[:, t, :], st[:, t, :, :].rearrange("p a b -> p (a b)")).then_inc(s_mv, 1)
            dve.wait_ge(s_sd, 1)
            dve.reciprocal(rs[:], rs[:]).then_inc(s_rs, 1)
            dve.wait_ge(s_rs, 1)
            dve.wait_ge(s_in, 32)
            for t in range(TT):
                dve.tensor_scalar(g.x1[:, t, :], g.x1[:, t, :], mv[:, t, 0:1], rs[:, t:t + 1], ALU.subtract, ALU.mult).then_inc(s_xn, 1)
                if t:
                    dve.wait_ge(s_xn, t)
                    dve.tensor_tensor(g.x1[:, t - 1, :], g.x1[:, t - 1, :], rows[:, 0, :], ALU.mult).then_inc(s_g, 1)
            dve.wait_ge(s_xn, TT)
            dve.tensor_tensor(g.x1[:, TT - 1, :], g.x1[:, TT - 1, :], rows[:, 0, :], ALU.mult).then_inc(s_g, 1)

        @block.scalar
        def _(act):
            act.wait_ge(s_mv, TT)
            act.activation(rs[:], mv[:, :, 1], ACT.Sqrt, bias=g.misc(3)).then_inc(s_sd, 1)

        @block.gpsimd
        def _(pool):
            for t in range(TT):
                pool.wait_ge(s_g, t + 1)
                pool.tensor_tensor(g.x1[:, t, :], g.x1[:, t, :], rows[:, 1, :], ALU.add).then_inc(s_b, 1)


def phase_mlp(nc, g, a):
    with ExitStack() as es:
        sb = lambda n, s, d=F32: es.enter_context(nc.sbuf_tensor(f"ff_{n}", s, d))
        sem = lambda n: nc.alloc_semaphore(f"ffs_{n}")
        GT = 4
        NGR = DFF // P // GT
        w1 = a["w_ff1"][0].rearrange("(k p) n -> p k n", p=P)
        w2 = a["w_ff2"][0].rearrange("(g k p) n -> p (g k) n", p=P, k=GT)
        st1 = [sb(f"st1_{u}", [P, KT, P]) for u in range(2)]
        hi1 = [sb(f"hi1_{u}", [P, KT, P], BF16) for u in range(2)]
        lo1 = [sb(f"lo1_{u}", [P, KT, P], BF16) for u in range(2)]
        st2, hi2, lo2 = sb("st2", [P, GT, D]), sb("hi2", [P, GT, D], BF16), sb("lo2", [P, GT, D], BF16)
        r = [sb(f"r{u}", [P, SEQ]) for u in range(2)]
        brow = sb("brow", [P, D])
        ps1 = [es.enter_context(nc.psum_tensor(f"ff_ps1_{u}", [P, SEQ], F32)) for u in range(2)]
        ps2 = [es.enter_context(nc.psum_tensor(f"ff_ps2_{u}", [P, HALF], F32)) for u in range(4)]
        s_l1, s_h1, s_o1, s_used1, s_relu, s_sq, s_uhi, s_ulo = (
            [sem(f"{n}{u}") for u in range(2)] for n in "l1 h1 o1 used1 relu sq uhi ulo".split())
        s_l2, s_m2, s_h2, s_o2, s_mm2, s_acc, s_b, s_bg, s_init = (sem(n) for n in "l2 m2 h2 o2 mm2 acc b bg init".split())
        NO = 2 * TT
        block = es.enter_context(nc.Block())

        def steps(eng, first, step):
            first()
            with eng.Fori(0, (NGR - 2) // 2) as r_:
                for par in range(2):
                    step(r_ * 2 + par, par, False)
            step(NGR - 2, 0, False)
            step(NGR - 1, 1, True)

        @block.sync
        def _(sp):
            sp.dma_start(brow[:], a["b_ff2"][0].partition_broadcast(P)).then_inc(s_b, 16)
            with sp.Fori(0, NGR) as gr:
                for t in range(GT):
                    sp.wait_ge(s_o1[t % 2], gr * 2 + (t // 2 + 1))
                    sp.dma_start(st1[t % 2][:], w1[:, :, ds(gr * (GT * P) + t * P, P)]).then_inc(s_l1[t % 2], 16)
                sp.wait_ge(s_o2, gr * GT + 1)
                sp.dma_start(st2[:], w2[:, ds(gr * GT, GT), :]).then_inc(s_l2, 16)

        @block.scalar
        def _(act):
            b1 = ROWS["bff1"][0]

            def split1(m, u):
                act.wait_ge(s_l1[u], m * 16 + 16)
                act.wait_ge(s_used1[u], m + 1)
                act.activation(hi1[u][:], st1[u][:], ACT.Copy).then_inc(s_h1[u], 1)

            def group(gr, par, last):
                for t in range(GT):
                    u, m = t % 2, gr * 2 + t // 2
                    act.wait_ge(s_used1[u], m + 2)
                    act.wait_ge(s_ulo[u], m + 1)
                    act.activation(r[u][:], ps1[u][:], ACT.Relu, bias=g.cols[:, ds(gr * GT + (b1 + t), 1)]).then_inc(s_relu[u], 1)
                    if not (last and t >= 2):
                        split1(m + 1, u)
                    act.wait_ge(s_sq[u], m + 1)
                    act.activation(g.c_hi[:, GT * par + t, :], r[u][:], ACT.Copy).then_inc(s_uhi[u], 1)

            def split2(gr):
                act.wait_ge(s_m2, gr * GT + GT)
                for k in range(GT):
                    act.activation(hi2[:, k, :], st2[:, k, :], ACT.Copy).then_inc(s_h2, 1)

            def first():
                for u in range(2):
                    split1(0, u)
                group(0, 0, False)
                split2(0)

            def step(i, par, last):
                if not last:
                    group(i + 1, 1 - par, isinstance(i, int))
                    act.wait_ge(s_mm2, i * NO + NO)
                    split2(i + 1)

            credit(act, s_relu)
            steps(act, first, step)

        @block.gpsimd
        def _(pool):
            credit(pool, s_o1 + s_ulo + [s_o2])

            def split1(m, u):
                pool.wait_ge(s_h1[u], m + 1)
                pool.tensor_tensor(lo1[u][:], st1[u][:], hi1[u][:], ALU.subtract).then_inc(s_o1[u], 1)

            def group(gr, par, last):
                for t in range(GT):
                    u, m = t % 2, gr * 2 + t // 2
                    if not (last and t >= 2):
                        split1(m + 1, u)
                    pool.wait_ge(s_uhi[u], m + 1)
                    pool.tensor_tensor(g.c_lo[:, GT * par + t, :], r[u][:], g.c_hi[:, GT * par + t, :], ALU.subtract).then_inc(s_ulo[u], 1)

            def split2(gr):
                for k in range(GT):
                    pool.wait_ge(s_h2, gr * GT + k + 1)
                    pool.tensor_tensor(lo2[:, k, :], st2[:, k, :], hi2[:, k, :], ALU.subtract).then_inc(s_o2, 1)

            def first():
                for u in range(2):
                    split1(0, u)
                group(0, 0, False)
                split2(0)

            def step(i, par, last):
                if not last:
                    group(i + 1, 1 - par, isinstance(i, int))
                    split2(i + 1)

            steps(pool, first, step)

        @block.vector
        def _(dve):
            dve.wait_ge(s_b, 16)
            dve.tensor_tensor(brow[:], brow[:], g.g2[:], ALU.mult).then_inc(s_bg, 1)
            dve.wait_ge(s_bg, 1)
            for t in range(TT):
                dve.scalar_tensor_tensor(g.x1[:, t, :], g.x1[:, t, :], ALPHA, brow[:], ALU.mult, ALU.add).then_inc(s_init, 1)
            dve.wait_ge(s_init, TT)
            credit(dve, [s_acc])

            def scale2(gr):
                dve.wait_ge(s_l2, gr * 16 + 16)
                for k in range(GT):
                    dve.tensor_tensor(st2[:, k, :], st2[:, k, :], g.g2[:], ALU.mult).then_inc(s_m2, 1)

            def group(gr):
                for t in range(GT):
                    u, m = t % 2, gr * 2 + t // 2
                    dve.wait_ge(s_relu[u], m + 2)
                    dve.tensor_tensor(r[u][:], r[u][:], r[u][:], ALU.mult).then_inc(s_sq[u], 1)

            def first():
                scale2(0)
                group(0)

            def step(i, par, last):
                if not last:
                    scale2(i + 1)
                    group(i + 1)
                for x in range(NO):
                    t, h = x // 2, x % 2
                    dve.wait_ge(s_mm2, i * NO + x + 1)
                    acc = g.x1[:, t, h * HALF:(h + 1) * HALF]
                    dve.tensor_tensor(acc, ps2[x % 4][:], acc, ALU.add).then_inc(s_acc, 1)

            steps(dve, first, step)

        @block.tensor
        def _(pe):
            credit(pe, s_used1)

            def group(gr):
                for t in range(GT):
                    u, m = t % 2, gr * 2 + t // 2
                    pe.wait_ge(s_o1[u], m + 2)
                    pe.wait_ge(s_relu[u], m + 1)
                    gemm_rows(pe, ps1[u], hi1[u], lo1[u], g.a_hi, g.a_lo, range(KT), range(KT)).then_inc(s_used1[u], 1)

            def second(i, par):
                pe.wait_ge(s_o2, i * GT + GT + 1)
                for u in range(2):
                    pe.wait_ge(s_ulo[u], i * 2 + 3)
                for x in range(NO):
                    t, h = x // 2, x % 2
                    pe.wait_ge(s_acc, i * NO + (x - 3 if x > 3 else 0) + 1)
                    gemm_tokens(pe, ps2[x % 4][:], g.c_hi, g.c_lo, slice(t * P, (t + 1) * P), hi2, lo2,
                                slice(h * HALF, (h + 1) * HALF), range(GT * par, GT * par + GT)).then_inc(s_mm2, 1)

            def step(i, par, last):
                if not last:
                    group(i + 1)
                second(i, par)

            steps(pe, lambda: group(0), step)


def setup(nc, es):
    g = Net()
    sb = lambda n, s, d=F32: es.enter_context(nc.sbuf_tensor(n, s, d))
    g.const = sb("const", [P, len(CT), P])
    g.tile = lambda n: g.const[:, CT[n], :]
    g.misc = lambda n: g.const[:, CT["misc"], n:n + 1]
    g.reset = sb("reset", [P, HALF])
    g.cols = sb("cols", [P, P])
    g.omka = sb("omka", [P, PAIRS])
    g.idb = sb("idb", [P, P], BF16)
    g.negb = sb("negb", [P, P], BF16)
    g.ada = sb("ada", [P, 4 * KT])
    g.g1 = sb("g1", [P, D])
    g.g2 = sb("g2", [P, D])
    g.a_hi = sb("a_hi", [P, KT, SEQ], BF16)
    g.a_lo = sb("a_lo", [P, KT, SEQ], BF16)
    g.c_hi = sb("c_hi", [P, KT, SEQ], BF16)
    g.c_lo = sb("c_lo", [P, KT, SEQ], BF16)
    return g


def build(nc, a, out):
    with ExitStack() as es:
        g = setup(nc, es)
        with nc.cleanup_on_exit(), ExitStack() as scope:
            phase_params(nc, g, a)
            phase_ada(nc, g, a)
            modulate(nc, g, "m1", None, a["x"][0], 8, 0, g.a_hi, g.a_lo)
            g.z = scope.enter_context(nc.sbuf_tensor("z", [P, NSH, SEQ], F32))
            phase_shifted(nc, g, a)
            phase_recurrence(nc, g, a)
        with nc.cleanup_on_exit(), ExitStack() as scope:
            g.v = scope.enter_context(nc.sbuf_tensor("v", [P, TT, DR], F32))
            phase_values(nc, g, a)
            phase_stick(nc, g, a)
        g.x1 = es.enter_context(nc.sbuf_tensor("x1", [P, TT, D], F32))
        with nc.cleanup_on_exit():
            with ExitStack() as scope:
                g.b_hi, g.b_lo = (scope.enter_context(nc.sbuf_tensor(n, [P, KT, SEQ], BF16)) for n in ("b_hi", "b_lo"))
                phase_merge(nc, g, a)
                phase_out(nc, g, a)
            norm_affine(nc, g, "n1", a["ln1_g"][0], a["ln1_b"][0], None)
            modulate(nc, g, "m2", g.x1, None, 24, 16, g.a_hi, g.a_lo)
            phase_mlp(nc, g, a)
            norm_affine(nc, g, "n2", a["ln2_g"][0], a["ln2_b"][0], out[0])


_INS = ["x", "c", "w_ada", "b_ada", "w_in", "mu_shift", "rw_w0", "rw_w2", "rw_a0", "rw_a2", "rw_g2", "rw_kk", "rw_ka", "rw_rk",
        "rw_gn_g", "rw_gn_b", "w_branch_a", "w_branch_b", "w_out", "ln1_g", "ln1_b", "w_ff1", "b_ff1", "w_ff2", "b_ff2",
        "ln2_g", "ln2_b"]


def kernel(**inputs):
    import concourse.bacc as bacc
    from concourse.bass_utils import run_bass_kernel_spmd

    nc = bacc.Bacc("TRN2", target_bir_lowering=False, num_devices=1)
    tiles, reset = constants()
    arrays = {n: np.ascontiguousarray(inputs[n]) for n in _INS} | {"const_tiles": tiles, "const_reset": reset}
    aps = {n: nc.dram_tensor(n, v.shape, mybir.dt.from_np(v.dtype), kind="ExternalInput").ap() for n, v in arrays.items()}
    out = nc.dram_tensor("out", [1, SEQ, D], F32, kind="ExternalOutput").ap()
    build(nc, aps, out)
    r = run_bass_kernel_spmd(nc, [arrays], core_ids=[0])
    return r.results[0]["out"]
```

```python
from contextlib import ExitStack

import numpy as np

import concourse.bass as bass
from concourse import mybir

F32 = mybir.dt.float32
BF16 = mybir.dt.bfloat16
ALU = mybir.AluOpType
ACT = mybir.ActivationFunctionType
ds = bass.ds

P = 128
SEQ = 1024
D = 1024
KT = D // P
TT = SEQ // P
HALF = 512
DR = 512
PAIRS = DR // P
HD = 64
DFF = 4 * D
LORA_W, LORA_A, LORA_G = 64, 64, 128
D_SHIFT = 3 * DR + LORA_W + LORA_A + LORA_G
NSH = D_SHIFT // P
COL_Q, COL_K, COL_V = D_SHIFT, D_SHIFT + DR, D_SHIFT + 2 * DR
COL_GA, COL_GB = D_SHIFT + 3 * DR, D_SHIFT + 3 * DR + D
CH = 64
ALPHA = 2.0 ** 0.25
LN_EPS, ADALN_EPS, GN_EPS = 1e-5, 1e-6, 64e-5
DECAY = float(np.exp(-0.5))
LEVELS = (2, 4, 8, 16)

ROWS = {}
_at = 0
for _name, _n in (("mu", NSH), ("w0", 8 * PAIRS), ("bff1", DFF // P), ("bada", 6 * KT)):
    ROWS[_name] = (_at, _n)
    _at += _n
ROWS["c"] = (P, KT)
PAIR_ROWS = ("w0", "a0", "kk", "ka", "rk", "gng", "gnb")

CT = {n: i for i, n in enumerate(("ident", "strictT", "inclT", "pairT", "m2", "m4", "m8", "m16", "bones", "neg", "misc"))}


def constants():
    i, j = np.meshgrid(np.arange(P), np.arange(P), indexing="ij")
    same = i // CH == j // CH
    t = np.zeros((P, len(CT), P), np.float32)
    t[:, CT["ident"]] = i == j
    t[:, CT["strictT"]] = same & (i < j)
    t[:, CT["inclT"]] = same & (i <= j)
    t[:, CT["pairT"]] = (i // 2 == j // 2) & (i < j)
    for s in LEVELS:
        t[:, CT[f"m{s}"]] = (i // (2 * s) == j // (2 * s)) & (i % (2 * s) >= s) & (j % (2 * s) < s)
    t[:, CT["bones"]] = i // HD == j // HD
    t[:, CT["neg"]] = np.where(j >= i, np.float32(-1e30), 0)
    t[:, CT["misc"], 0] = i[:, 0] % CH < CH // 2
    t[:, CT["misc"], 1] = i[:, 0] % CH >= CH // 2
    t[:, CT["misc"], 2] = ADALN_EPS
    t[:, CT["misc"], 3] = LN_EPS
    t[:, CT["misc"], 4] = GN_EPS
    reset = np.ones((P, HALF), np.float32)
    reset[:, ::CH] = 0
    return t, reset


def credit(eng, sems):
    for s in sems:
        eng.sem_inc(s, 1)


class Net:
    pass


def split_stream(es, nc, tag, count, units, source, w_used):
    stage = [es.enter_context(nc.sbuf_tensor(f"{tag}_stage{u}", [P, KT, P], F32)) for u in range(units)]
    hi = [es.enter_context(nc.sbuf_tensor(f"{tag}_whi{u}", [P, KT, P], BF16)) for u in range(units)]
    lo = [es.enter_context(nc.sbuf_tensor(f"{tag}_wlo{u}", [P, KT, P], BF16)) for u in range(units)]
    loaded = [nc.alloc_semaphore(f"{tag}_loaded{u}") for u in range(units)]
    hi_ready = [nc.alloc_semaphore(f"{tag}_hi_ready{u}") for u in range(units)]
    lo_ready = [nc.alloc_semaphore(f"{tag}_lo_ready{u}") for u in range(units)]

    def load_step(sp, i):
        col = i * P if isinstance(i, int) else sp.snap(i * P)
        for u in range(units):
            for w in {0: (0,), 1: range(1, units)}.get(u, ()):
                sp.wait_ge(lo_ready[w], i + 1)
            parts = source(u, col)
            for dst, src in parts:
                sp.dma_start(stage[u][:, dst, :], src).then_inc(loaded[u], 16)

    def load(sp):
        with sp.Fori(0, count) as i:
            load_step(sp, i)

    def split_hi(act, i, u):
        act.wait_ge(loaded[u], (i + 1) * (16 * len(source(u, 0))))
        act.wait_ge(w_used[u], i + 1)
        act.activation(hi[u][:], stage[u][:], ACT.Copy).then_inc(hi_ready[u], 1)

    def cut_lo(pool, i, u):
        pool.wait_ge(hi_ready[u], i + 1)
        pool.tensor_tensor(lo[u][:], stage[u][:], hi[u][:], ALU.subtract).then_inc(lo_ready[u], 1)

    def split_lo(pool, first=True):
        if first:
            credit(pool, lo_ready)
        with pool.Fori(0, count) as i:
            for u in range(units):
                cut_lo(pool, i, u)

    st = Net()
    st.stage, st.hi, st.lo, st.loaded, st.hi_ready, st.lo_ready = stage, hi, lo, loaded, hi_ready, lo_ready
    st.load_step = load_step
    st.load, st.split_hi, st.split_lo, st.cut_lo = load, split_hi, split_lo, cut_lo
    return st


def gemm_rows(pe, out, whi, wlo, act_hi, act_lo, kts, slots):
    n = len(kts)
    for x, (kt, slot) in enumerate(zip(kts, slots)):
        for y, (w, a) in enumerate(((whi, act_hi), (whi, act_lo), (wlo, act_hi))):
            for h in range(2):
                last = pe.matmul(out[:, h * HALF:(h + 1) * HALF], w[:, kt, :], a[:, slot, h * HALF:(h + 1) * HALF],
                                 start=(x == 0 and y == 0), stop=(x == n - 1 and y == 2))
    return last


ADA = {n: i * KT for i, n in enumerate(("sh1", "sc1", "g1", "sh2", "sc2", "g2"))}
ADA_PARTS = 6 * D // HALF
CPH = HALF // P


def phase_start(nc, g, a):
    with ExitStack() as es:
        sb = lambda n, s, d=F32: es.enter_context(nc.sbuf_tensor(n, s, d))
        psum = lambda n, w=HALF: es.enter_context(nc.psum_tensor(n, [P, w], F32))
        sem = lambda n: nc.alloc_semaphore(n)
        rows, crows = sb("rows", [P, P]), sb("crows", [KT, P])
        s_in, s_tr, s_zero, s_one, s_cols, s_tab = (sem(f"par_{n}") for n in "in tr zero one cols tab".split())
        pair_vecs = {"w0": a["rw_w0"][0], "a0": a["rw_a0"][0], "kk": a["rw_kk"][0], "ka": a["rw_ka"][0],
                     "rk": a["rw_rk"][0].rearrange("h d -> (h d)"), "gng": a["rw_gn_g"][0], "gnb": a["rw_gn_b"][0]}
        vecs = {"mu": a["mu_shift"][0], "bff1": a["b_ff1"][0], "bada": a["b_ada"][0]}
        n_in = 16 * (len(vecs) + len(pair_vecs) + 3)
        at8 = ROWS["w0"][0]
        steps = NSH // 2
        early = ADA_PARTS - steps
        csig = sb("csig", [P, KT])
        wst, acc = [sb(f"ada_w{u}", [P, KT, HALF]) for u in range(2)], [sb(f"ada_acc{u}", [P, HALF]) for u in range(2)]
        ada_ps = [psum(f"ada_ps{u}") for u in range(2)]
        s_wada, s_acc, s_sum = ([sem(f"ada_{n}{u}") for u in range(2)] for n in "in acc sum".split())
        s_sig, s_sil, s_step, s_ada, s_wlate, s_late, s_lstep, s_lsum, s_lada = (
            sem(f"ada_{n}") for n in "sig sil step ada wlate late lstep lsum lada".split())
        w_ada = a["w_ada"][0].rearrange("(k p) n -> p k n", p=P)
        b_at = ROWS["bada"][0]
        NB = 4
        x = [(g.c_hi, g.c_lo)[t // 4][:].rearrange("p a n -> p (a n)").bitcast(F32)[:, (t % 4) * D:(t % 4 + 1) * D] for t in range(TT)]
        st, mv, rs = sb("st", [P, TT, 2, 6]), sb("mv", [P, TT, 2]), sb("rs", [P, TT])
        hf = [sb(f"hf{u}", [P, HALF]) for u in range(NB)]
        s_x = [sem(f"h_x{t}") for t in range(TT)]
        s_st, s_mv, s_sd, s_rs, s_xn, s_turn, s_hf, s_hi, s_lo0, s_lo1 = (
            sem(f"h_{n}") for n in "st mv sd rs xn turn hf hi lo0 lo1".split())
        NH = 2 * KT
        w_used, s_raw, s_diff, s_shift = ([sem(f"zs_{n}{u}") for u in range(2)] for n in "used raw diff shift".split())
        s_pad = sem("zs_pad")
        raw = [sb(f"zs_rawt{u}", [P, SEQ + 1]) for u in range(2)]
        diff = [sb(f"zs_dift{u}", [P, SEQ]) for u in range(2)]
        ps = [psum(f"zs_ps{u}", SEQ) for u in range(2)]
        h_ps = [psum(f"h_ps{u}")[:] for u in range(2)] + [ps[1][:, h * HALF:(h + 1) * HALF] for h in range(2)]
        w = a["w_in"][0].rearrange("(k p) n -> p k n", p=P)
        ws = split_stream(
            es, nc, "zs", steps, 2, lambda u, i: [(slice(0, KT), w[:, :, ds(i * 2 + u * P, P)])], w_used)
        block = es.enter_context(nc.Block())

        @block.sync
        def _(sp):
            sp.dma_start(g.const[:], a["const_tiles"]).then_inc(s_in, 16)
            sp.dma_start(g.reset[:], a["const_reset"]).then_inc(s_in, 16)
            sp.dma_start(crows[:], a["c"][0].rearrange("(t p) -> t p", p=P)).then_inc(s_in, 16)
            sp.wait_ge(s_zero, 1)
            for name, v in vecs.items():
                at, n = ROWS[name]
                sp.dma_start(rows[at:at + n, :], v.rearrange("(t p) -> t p", p=P)).then_inc(s_in, 16)
            for y, name in enumerate(PAIR_ROWS):
                sp.dma_start(rows[at8 + y:at8 + 8 * PAIRS:8, :], pair_vecs[name].rearrange("(t p) -> t p", p=P)).then_inc(s_in, 16)

            def chunk(n):
                if n >= 2:
                    sp.wait_ge(s_acc[n % 2], n // 2)
                sp.dma_start(wst[n % 2][:], w_ada[:, :, n * HALF:(n + 1) * HALF]).then_inc(s_wada[n % 2], 16)

            for n in range(early - 1):
                chunk(n)
            for t in range(TT):
                sp.dma_start(x[t], a["x"][0][t * P:(t + 1) * P, :]).then_inc(s_x[t], 16)

            def late(i):
                sp.wait_ge(s_late, i + 1)
                sp.dma_start(wst[early % 2][:], w_ada[:, :, ds(i * HALF + early * HALF, HALF)]).then_inc(s_wlate, 16)

            ws.load_step(sp, 0)
            chunk(early - 1)
            sp.wait_ge(s_acc[early % 2], early // 2)
            late(0)
            with sp.Fori(1, steps) as i:
                ws.load_step(sp, i)
                late(i)

        @block.tensor
        def _(pe):
            pe.wait_ge(s_in, n_in)
            pe.transpose(ps[0][:, 0:P], rows[:], g.tile("ident"))
            pe.transpose(ps[0][:, P:P + KT], crows[:], g.const[0:KT, CT["ident"], 0:KT]).then_inc(s_tr, 1)

            def columns(u):
                for c in range(CPH):
                    last = pe.matmul(ada_ps[u][:, c:c + 1], acc[u][:, c * P:(c + 1) * P], g.ones[:, 0:1], start=True, stop=True)
                return last

            def turn(n):
                kt, h = n % KT, n // KT
                pe.wait_ge(s_xn, 4 * h + 4)
                if n >= NB:
                    pe.wait_ge(s_hf, n - NB + 1)
                for j in range(4):
                    last = pe.transpose(h_ps[n % NB][:, j * P:(j + 1) * P], x[4 * h + j][:, kt * P:(kt + 1) * P], g.tile("ident"))
                last.then_inc(s_turn, 1)

            pe.wait_ge(s_one, 1)
            credit(pe, w_used)

            def early_columns(n):
                pe.wait_ge(s_acc[n % 2], n // 2 + 1)
                if n >= 2:
                    pe.wait_ge(s_ada, n - 1)
                columns(n % 2).then_inc(s_sum[n % 2], 1)

            for n in range(early - 1):
                early_columns(n)
            for n in range(NH):
                turn(n)
            pe.wait_ge(s_lo0, KT)
            pe.wait_ge(s_lo1, KT)
            late = early % 2
            pe.wait_ge(s_cols, 1)
            with pe.Fori(0, steps) as i:
                for u in range(2):
                    pe.wait_ge(ws.lo_ready[u], i + 2)
                    pe.wait_ge(s_raw[u], i + 1)
                    gemm_rows(pe, ps[u], ws.hi[u], ws.lo[u], g.a_hi, g.a_lo, range(KT), range(KT)).then_inc(w_used[u], 1)
                    if u == 0:
                        pe.wait_ge(s_late, i + 2)
                        pe.wait_ge(s_lada, i + 1)
                        columns(late).then_inc(s_lsum, 1)
            early_columns(early - 1)

        @block.scalar
        def _(act):
            cc = ROWS["c"][0]
            act.wait_ge(s_cols, 1)
            act.activation(csig[:], g.cols[:, cc:cc + KT], ACT.Sigmoid).then_inc(s_sig, 1)
            for t in range(TT):
                act.wait_ge(s_mv, t + 1)
                act.activation(rs[:, t:t + 1], mv[:, t, 1:2], ACT.Sqrt, bias=g.misc(2)).then_inc(s_sd, 1)
            act.wait_ge(s_ada, 2 * 2 + 2)
            credit(act, s_raw)
            for n in range(NH):
                kt = n % KT
                if n == KT:
                    for u in range(2):
                        ws.split_hi(act, 0, u)
                act.wait_ge(s_turn, n + 1)
                if n >= NB:
                    act.wait_ge((s_lo0, s_lo1)[n % 2], n // 2 - 1)
                act.activation(hf[n % NB][:], h_ps[n % NB], ACT.Identity, bias=g.ada[:, ADA["sh1"] + kt:ADA["sh1"] + kt + 1],
                               scale=g.ada[:, ADA["sc1"] + kt:ADA["sc1"] + kt + 1]).then_inc(s_hf, 1)
            act.wait_ge(s_pad, 2)
            with act.Fori(0, steps - 1) as i:
                for u in range(2):
                    act.wait_ge(w_used[u], i + 2)
                    act.wait_ge(s_shift[u], i + 1)
                    act.activation(raw[u][:, 1:SEQ + 1], ps[u][:], ACT.Copy).then_inc(s_raw[u], 1)
                    ws.split_hi(act, i + 1, u)
            for u in range(2):
                act.wait_ge(w_used[u], steps + 1)
                act.wait_ge(s_shift[u], steps)
                act.activation(raw[u][:, 1:SEQ + 1], ps[u][:], ACT.Copy).then_inc(s_raw[u], 1)

        @block.vector
        def _(dve):
            dve.memset(rows[:], 0.0).then_inc(s_zero, 1)
            dve.memset(g.ones[:], 1.0).then_inc(s_one, 1)
            credit(dve, s_shift + [s_late, s_lada])
            for u in range(2):
                dve.memset(raw[u][:, 0:1], 0.0).then_inc(s_pad, 1)
            dve.wait_ge(s_tr, 1)
            dve.tensor_copy(g.cols[:], ps[0][:, 0:P + KT]).then_inc(s_cols, 1)
            dve.wait_ge(s_cols, 1)
            ka, cc = at8 + PAIR_ROWS.index("ka"), ROWS["c"][0]
            dve.tensor_scalar(g.cols[:, at8 + 7:at8 + 8 * PAIRS:8], g.cols[:, ka:at8 + 8 * PAIRS:8], -1.0, 1.0, ALU.mult, ALU.add).then_inc(s_tab, 1)
            dve.tensor_copy(g.idb[:], g.tile("ident")).then_inc(s_tab, 1)
            dve.tensor_copy(g.negb[:], g.tile("neg")).then_inc(s_tab, 1)
            dve.wait_ge(s_sig, 1)
            dve.tensor_tensor(g.csil[:], csig[:], g.cols[:, cc:cc + KT], ALU.mult).then_inc(s_sil, 1)
            dve.wait_ge(s_sil, 1)

            def accumulate(u, step, before, done):
                for kt in range(KT):
                    src, c = wst[u][:, kt, :], g.csil[:, kt:kt + 1]
                    if kt:
                        dve.wait_ge(step, before + kt)
                        op = dve.scalar_tensor_tensor(acc[u][:], src, c, acc[u][:], ALU.mult, ALU.add)
                    else:
                        op = dve.tensor_scalar(acc[u][:], src, c, None, ALU.mult)
                    op.then_inc(done if kt == KT - 1 else step, 1)

            def chunk(n):
                dve.wait_ge(s_wada[n % 2], 16 * (n // 2 + 1))
                if n >= 2:
                    dve.wait_ge(s_sum[n % 2], n // 2)
                accumulate(n % 2, s_step, n * (KT - 1), s_acc[n % 2])

            def finish(n):
                dve.wait_ge(s_sum[n % 2], n // 2 + 1)
                dve.tensor_tensor(g.ada[:, n * CPH:(n + 1) * CPH], ada_ps[n % 2][:, 0:CPH],
                                  g.cols[:, b_at + n * CPH:b_at + (n + 1) * CPH], ALU.add).then_inc(s_ada, 1)

            for n in range(early - 1):
                chunk(n)
                if n:
                    finish(n - 1)
            finish(early - 2)
            at = ADA["sc1"]
            dve.wait_ge(s_ada, early - 1)
            for c in range(2):
                v = g.ada[:, at + c * CPH:at + (c + 1) * CPH]
                dve.tensor_scalar(v, v, 1.0, None, ALU.add).then_inc(s_ada, 1)

            def normalise(t):
                dve.wait_ge(s_sd, t + 1)
                dve.reciprocal(rs[:, t:t + 1], rs[:, t:t + 1]).then_inc(s_rs, 1)
                dve.wait_ge(s_rs, t + 1)
                dve.tensor_scalar(x[t], x[t], mv[:, t, 0:1], rs[:, t:t + 1], ALU.subtract, ALU.mult).then_inc(s_xn, 1)

            for t in range(TT):
                dve.wait_ge(s_x[t], 16)
                for h in range(2):
                    dve.bn_stats(st[:, t, h, :], x[t][:, h * HALF:(h + 1) * HALF]).then_inc(s_st, 1)
                dve.wait_ge(s_st, 2 * t + 2)
                dve.bn_aggr(mv[:, t, :], st[:, t, :, :].rearrange("p a b -> p (a b)")).then_inc(s_mv, 1)
                if t:
                    normalise(t - 1)
            normalise(TT - 1)

            def low(n):
                kt, h = n % KT, n // KT
                dve.wait_ge(s_hi, n + 1)
                at = slice(h * HALF, (h + 1) * HALF)
                dve.tensor_tensor(g.a_lo[:, kt, at], hf[n % NB][:], g.a_hi[:, kt, at], ALU.subtract).then_inc(s_lo1, 1)

            for n in range(NH):
                kt, h = n % KT, n // KT
                dve.wait_ge(s_hf, n + 1)
                dve.tensor_copy(g.a_hi[:, kt, h * HALF:(h + 1) * HALF], hf[n % NB][:]).then_inc(s_hi, 1)
                if n % 2:
                    low(n)
            chunk(early - 1)
            mu = ROWS["mu"][0]
            with dve.Fori(0, steps) as i:
                dve.wait_ge(s_wlate, i * 16 + 16)
                dve.wait_ge(s_lada, i + 1)
                accumulate(early % 2, s_lstep, i * (KT - 1), s_late)
                for u in range(2):
                    dve.wait_ge(s_raw[u], i + 2)
                    dve.tensor_tensor(diff[u][:], raw[u][:, 0:SEQ], raw[u][:, 1:SEQ + 1], ALU.subtract).then_inc(s_diff[u], 1)
                    if u == 0:
                        dve.wait_ge(s_lsum, i + 1)
                        dve.tensor_tensor(g.ada[:, ds(i * CPH + early * CPH, CPH)], ada_ps[early % 2][:, 0:CPH],
                                          g.cols[:, ds(i * CPH + (b_at + early * CPH), CPH)], ALU.add).then_inc(s_lada, 1)
                    dve.wait_ge(s_diff[u], i + 1)
                    dve.scalar_tensor_tensor(g.z[:, ds(i * 2 + u, 1), :].rearrange("p a n -> p (a n)"), diff[u][:],
                                             g.cols[:, ds(i * 2 + (mu + u), 1)],
                                             raw[u][:, 1:SEQ + 1], ALU.mult, ALU.add).then_inc(s_shift[u], 1)
            finish(early - 1)
            dve.wait_ge(s_lada, steps + 1)
            v = g.ada[:, ADA["sc2"]:ADA["sc2"] + KT]
            dve.tensor_scalar(v, v, 1.0, None, ALU.add).then_inc(s_ada, 1)

        @block.gpsimd
        def _(pool):
            credit(pool, ws.lo_ready)
            for n in range(0, NH, 2):
                kt, h = n % KT, n // KT
                pool.wait_ge(s_hi, n + 1)
                at = slice(h * HALF, (h + 1) * HALF)
                pool.tensor_tensor(g.a_lo[:, kt, at], hf[n % NB][:], g.a_hi[:, kt, at], ALU.subtract).then_inc(s_lo0, 1)
            ws.split_lo(pool, False)


def modulate(nc, g, tag, src, from_dram, scale_at, shift_at, dst_hi, dst_lo):
    with ExitStack() as es:
        sb = lambda n, s, d=F32: es.enter_context(nc.sbuf_tensor(f"{tag}_{n}", s, d))
        sem = lambda n: nc.alloc_semaphore(f"{tag}_{n}")
        x = sb("x", [P, TT, D]) if from_dram is not None else src
        xn = x if from_dram is not None else sb("xn", [P, TT, D])
        st = sb("st", [P, TT, 2, 6]); mv = sb("mv", [P, TT, 2]); rs = sb("rs", [P, TT])
        hf = [sb(f"hf{u}", [P, HALF]) for u in range(2)]
        ps = [es.enter_context(nc.psum_tensor(f"{tag}_ps{u}", [P, HALF], F32)) for u in range(2)]
        s_x, s_st, s_mv, s_sd, s_rs, s_xn, s_tr, s_hf, s_hi, s_lo = (sem(n) for n in "in st mv sd rs xn tr hf hi lo".split())
        block = es.enter_context(nc.Block())

        if from_dram is not None:
            @block.sync
            def _(sp):
                for t in range(TT):
                    sp.dma_start(x[:, t, :], from_dram[t * P:(t + 1) * P, :]).then_inc(s_x, 16)

        @block.vector
        def _(dve):
            for t in range(TT):
                if from_dram is not None:
                    dve.wait_ge(s_x, 16 * TT)
                for h in range(2):
                    dve.bn_stats(st[:, t, h, :], x[:, t, h * HALF:(h + 1) * HALF]).then_inc(s_st, 1)
                dve.wait_ge(s_st, 2 * t + 2)
                dve.bn_aggr(mv[:, t, :], st[:, t, :, :].rearrange("p a b -> p (a b)")).then_inc(s_mv, 1)
            dve.wait_ge(s_sd, 1)
            dve.reciprocal(rs[:], rs[:]).then_inc(s_rs, 1)
            dve.wait_ge(s_rs, 1)
            for t in range(TT):
                dve.tensor_scalar(xn[:, t, :], x[:, t, :], mv[:, t, 0:1], rs[:, t:t + 1], ALU.subtract, ALU.mult).then_inc(s_xn, 1)
            for n in range(2 * KT):
                dve.wait_ge(s_hf, n + 1)
                kt, h = n % KT, n // KT
                dve.tensor_copy(dst_hi[:, kt, h * HALF:(h + 1) * HALF], hf[n % 2][:]).then_inc(s_hi, 1)

        @block.tensor
        def _(pe):
            for n in range(2 * KT):
                kt, h = n % KT, n // KT
                pe.wait_ge(s_xn, 4 * h + 4)
                if n >= 2:
                    pe.wait_ge(s_hf, n - 1)
                for j in range(4):
                    last = pe.transpose(ps[n % 2][:, j * P:(j + 1) * P], xn[:, 4 * h + j, kt * P:(kt + 1) * P], g.tile("ident"))
                last.then_inc(s_tr, 1)

        @block.scalar
        def _(act):
            act.wait_ge(s_mv, TT)
            act.activation(rs[:], mv[:, :, 1], ACT.Sqrt, bias=g.misc(2)).then_inc(s_sd, 1)
            for n in range(2 * KT):
                kt, h = n % KT, n // KT
                act.wait_ge(s_tr, n + 1)
                if n >= 2:
                    act.wait_ge(s_lo, n - 1)
                act.activation(hf[n % 2][:], ps[n % 2][:], ACT.Identity, bias=g.ada[:, shift_at + kt:shift_at + kt + 1],
                               scale=g.ada[:, scale_at + kt:scale_at + kt + 1]).then_inc(s_hf, 1)

        @block.gpsimd
        def _(pool):
            for n in range(2 * KT):
                kt, h = n % KT, n // KT
                pool.wait_ge(s_hi, n + 1)
                pool.tensor_tensor(dst_lo[:, kt, h * HALF:(h + 1) * HALF], hf[n % 2][:],
                                   dst_hi[:, kt, h * HALF:(h + 1) * HALF], ALU.subtract).then_inc(s_lo, 1)


def gemm_tokens(pe, out, act_hi, act_lo, at, whi, wlo, n, slots):
    k = len(slots)
    for x, slot in enumerate(slots):
        for y, (a, w) in enumerate(((act_hi, whi), (act_hi, wlo), (act_lo, whi))):
            last = pe.matmul(out, a[:, slot, at], w[:, x, n], start=(x == 0 and y == 0), stop=(x == k - 1 and y == 2))
    return last


def phase_values(nc, g, a):
    with ExitStack() as es:
        sb = lambda n, s, d=F32: es.enter_context(nc.sbuf_tensor(n, s, d))
        sem = lambda n: nc.alloc_semaphore(n)
        w = a["w_in"][0].rearrange("(k p) n -> p k n", p=P)
        stage, hi, lo = sb("v_stage", [P, KT, DR]), sb("v_whi", [P, KT, DR], BF16), sb("v_wlo", [P, KT, DR], BF16)
        ps = [es.enter_context(nc.psum_tensor(f"v_ps{u}", [P, DR], F32)) for u in range(2)]
        s_w, s_hi, s_lo = sem("v_in"), sem("v_hi"), sem("v_lo")
        s_mm = [sem(f"v_mm{u}") for u in range(2)]
        s_out = [sem(f"v_out{u}") for u in range(2)]
        block = es.enter_context(nc.Block())

        @block.sync
        def _(sp):
            sp.dma_start(stage[:], w[:, :, COL_V:COL_V + DR]).then_inc(s_w, 16)

        @block.scalar
        def _(act):
            act.wait_ge(s_w, 16)
            for kt in range(KT):
                act.activation(hi[:, kt, :], stage[:, kt, :], ACT.Copy).then_inc(s_hi, 1)
            credit(act, s_out)
            with act.Fori(0, TT // 2) as i:
                for u in range(2):
                    act.wait_ge(s_mm[u], i + 1)
                    act.activation(g.v[:, ds(i * 2 + u, 1), :].rearrange("p a n -> p (a n)"), ps[u][:], ACT.Copy).then_inc(s_out[u], 1)

        @block.gpsimd
        def _(pool):
            for kt in range(KT):
                pool.wait_ge(s_hi, kt + 1)
                pool.tensor_tensor(lo[:, kt, :], stage[:, kt, :], hi[:, kt, :], ALU.subtract).then_inc(s_lo, 1)

        @block.tensor
        def _(pe):
            pe.wait_ge(s_lo, KT)
            with pe.Fori(0, TT // 2) as i:
                for u in range(2):
                    pe.wait_ge(s_out[u], i + 1)
                    gemm_tokens(pe, ps[u][:], g.a_hi, g.a_lo, ds(i * (2 * P) + u * P, P), hi, lo,
                                slice(0, DR), range(KT)).then_inc(s_mm[u], 1)


def phase_stick(nc, g, a):
    with ExitStack() as es:
        sb = lambda n, s, d=F32: es.enter_context(nc.sbuf_tensor(n, s, d))
        sem = lambda n: nc.alloc_semaphore(n)
        w = a["w_in"][0].rearrange("(k p) n -> p k n", p=P)
        qk = [sb("qs", [P, SEQ]), sb("ks", [P, SEQ])]
        vs = sb("vs", [P, TT, P])
        att = [sb(f"att{b}", [P, SEQ]) for b in range(3)]
        rest = [sb(f"rest{b}", [P, SEQ]) for b in range(3)]
        prod = [sb(f"prod{b}", [P, SEQ + 1]) for b in range(2)]
        attT = [sb(f"attT{b}", [P, TT, P]) for b in range(2)]
        zps = [es.enter_context(nc.psum_tensor(f"z_ps{b}", [P, SEQ], F32)) for b in range(2)]
        trps = [es.enter_context(nc.psum_tensor(f"tr_ps{b}", [P, HALF], F32)) for b in range(2)]
        ops = es.enter_context(nc.psum_tensor("o_ps", [P, SEQ], F32))
        w_used = [sem(f"sb_used{u}") for u in range(2)]
        s_one, s_qk, s_vs, s_z, s_sig, s_scan, s_att, s_tr, s_pv, s_ohi, s_olo = (
            sem(f"sb_{n}") for n in "one qk vs z sig scan att tr pv ohi olo".split())
        s_tre = [sem(f"sb_tre{b}") for b in range(2)]
        units = [(e, i) for e in range(2) for i in range(TT)]
        NU = len(units)
        groups = [(n, k0, min(k0 + 4, units[n][1] + 1)) for n in range(NU) for k0 in range(0, units[n][1] + 1, 4)]
        NG = len(groups)
        assert NG % 2 == 0
        of_unit = [[x for x, gr in enumerate(groups) if gr[0] == n] for n in range(NU)]
        ws = split_stream(
            es, nc, "sb", PAIRS, 2, lambda u, i: [(slice(0, KT), w[:, :, ds(i + (COL_Q, COL_K)[u], P)])], w_used)
        block = es.enter_context(nc.Block())
        block.sync(ws.load)

        @block.gpsimd
        def _(pool):
            credit(pool, ws.lo_ready + [s_att])
            with pool.Fori(0, PAIRS) as p:
                for u in range(2):
                    ws.cut_lo(pool, p, u)
                pool.wait_ge(s_pv, p * NU + 1)
                pool.tensor_copy(vs[:], g.v[:, :, ds(p * P, P)]).then_inc(s_vs, 1)
                for n, (e, i) in enumerate(units):
                    nk = (i + 1) * P
                    pool.wait_ge(s_scan, p * NU + n + 1)
                    pool.tensor_tensor(att[n % 3][:, 0:nk], att[n % 3][:, 0:nk], prod[n % 2][:, SEQ - nk + 1:SEQ + 1],
                                       ALU.mult).then_inc(s_att, 1)

        @block.tensor
        def _(pe):
            credit(pe, w_used + [s_pv])
            with pe.Fori(0, PAIRS) as p:
                for u in range(2):
                    pe.wait_ge(ws.lo_ready[u], p + 2)
                    pe.wait_ge(s_sig, p * NU + 1)
                    gemm_rows(pe, zps[u], ws.hi[u], ws.lo[u], g.a_hi, g.a_lo, range(KT), range(KT)).then_inc(w_used[u], 1)

                def scores(n):
                    e, i = units[n]
                    nk = (i + 1) * P
                    if n >= 2:
                        pe.wait_ge(s_sig, p * NU + n)
                    q = qk[0][HD * e:HD * e + HD, i * P:(i + 1) * P]
                    for b in range(0, nk, HALF):
                        b1 = min(nk, b + HALF)
                        pe.matmul(zps[n % 2][:, b:b1], q, qk[1][HD * e:HD * e + HD, b:b1], start=True, stop=True)
                    pe.matmul(zps[n % 2][:, i * P:nk], g.idb[:], g.negb[:], start=False, stop=True, skip_group_check=True).then_inc(s_z, 1)

                def turn(n):
                    e, i = units[n]
                    pe.wait_ge(s_att, p * NU + n + 2)
                    for x in of_unit[n]:
                        _, k0, k1 = groups[x]
                        pe.wait_ge(s_tre[x % 2], p * (NG // 2) + (x // 2 + 1))
                        for kt in range(k0, k1):
                            last = pe.transpose(trps[x % 2][:, (kt - k0) * P:(kt - k0 + 1) * P], att[n % 3][:, kt * P:(kt + 1) * P], g.tile("ident"))
                        last.then_inc(s_tr, 1)

                def values(n):
                    e, i = units[n]
                    for x in of_unit[n]:
                        pe.wait_ge(s_tre[x % 2], p * (NG // 2) + (x // 2 + 2))
                    for kt in range(i + 1):
                        last = pe.matmul(ops[HD * e:HD * e + HD, i * P:(i + 1) * P], vs[:, kt, HD * e:HD * e + HD],
                                         attT[n % 2][:, kt, :], start=(kt == 0), stop=(kt == i))
                    last.then_inc(s_pv, 1)

                pe.wait_ge(s_qk, p * 2 + 2)
                scores(0)
                scores(1)
                pe.wait_ge(s_vs, p + 1)
                pe.wait_ge(s_olo, p + 1)
                for n in range(NU):
                    if n + 2 < NU:
                        scores(n + 2)
                    turn(n)
                    if n >= 1:
                        values(n - 1)
                values(NU - 1)

        def evacuate(eng, p, n, x):
            _, k0, k1 = groups[x]
            eng.wait_ge(s_tr, p * NG + x + 1)
            eng.wait_ge(s_pv, p * NU + max(n, 1))
            dst = attT[n % 2][:, k0:k1, :].rearrange("p a n -> p (a n)")
            src = trps[x % 2][:, 0:(k1 - k0) * P]
            if x % 2:
                eng.activation(dst, src, ACT.Copy).then_inc(s_tre[1], 1)
            else:
                eng.tensor_copy(dst, src).then_inc(s_tre[0], 1)

        @block.scalar
        def _(act):
            def sigmoids(p, n):
                e, i = units[n]
                nk = (i + 1) * P
                act.wait_ge(s_z, p * NU + n + 1)
                if n >= 3:
                    act.wait_ge(s_tr, p * NG + of_unit[n - 3][-1] + 1)
                    act.wait_ge(s_scan, p * NU + n - 2)
                act.activation(att[n % 3][:, 0:nk], zps[n % 2][:, 0:nk], ACT.Sigmoid, scale=HD ** -0.5)
                act.activation(rest[n % 3][:, 0:nk], zps[n % 2][:, 0:nk], ACT.Sigmoid, scale=-HD ** -0.5).then_inc(s_sig, 1)

            credit(act, [s_sig, s_tre[1]])
            with act.Fori(0, PAIRS) as p:
                for u in range(2):
                    ws.split_hi(act, p, u)
                for u in range(2):
                    act.wait_ge(w_used[u], p + 2)
                    act.activation(qk[u][:], zps[u][:], ACT.Copy).then_inc(s_qk, 1)
                sigmoids(p, 0)
                sigmoids(p, 1)
                for n in range(NU):
                    if n + 2 < NU:
                        sigmoids(p, n + 2)
                    for x in of_unit[n]:
                        if x % 2:
                            evacuate(act, p, n, x)
                act.wait_ge(s_pv, p * NU + (NU + 1))
                act.activation(g.c_hi[:, ds(p + PAIRS, 1), :].rearrange("p a n -> p (a n)"), ops[:], ACT.Copy).then_inc(s_ohi, 1)

        @block.vector
        def _(dve):
            for b in range(2):
                dve.memset(prod[b][:, SEQ:SEQ + 1], 1.0).then_inc(s_one, 1)
            dve.wait_ge(s_one, 2)
            credit(dve, [s_tre[0], s_olo])

            def scan(p, n):
                e, i = units[n]
                nk = (i + 1) * P
                dve.wait_ge(s_sig, p * NU + n + 2)
                dve.wait_ge(s_att, p * NU + max(n, 1))
                m = rest[n % 3][:, 0:nk][:, ::-1]
                dve.tensor_tensor_scan(prod[n % 2][:, SEQ - nk:SEQ][:, ::-1], m, m, 1.0, ALU.mult, ALU.bypass).then_inc(s_scan, 1)

            with dve.Fori(0, PAIRS) as p:
                scan(p, 0)
                for n in range(NU):
                    if n + 1 < NU:
                        scan(p, n + 1)
                    for x in of_unit[n]:
                        if x % 2 == 0:
                            evacuate(dve, p, n, x)
                dve.wait_ge(s_ohi, p + 1)
                dve.tensor_tensor(g.c_lo[:, ds(p + PAIRS, 1), :].rearrange("p a n -> p (a n)"), ops[:],
                                  g.c_hi[:, ds(p + PAIRS, 1), :].rearrange("p a n -> p (a n)"), ALU.subtract).then_inc(s_olo, 1)


class Turn:

    def __init__(self, p, dp, f):
        self.p, self.dp, self.f = p, dp, f

    def count(self, k, j):
        return self.p * (2 * k) + ((2 * self.dp + self.f) * k + j)

    def before(self):
        if self.f:
            return Turn(self.p, self.dp, 0)
        return None if isinstance(self.p, int) and self.p + self.dp == 0 else Turn(self.p, self.dp - 1, 1)

    def after(self):
        if not self.f:
            return Turn(self.p, self.dp, 1)
        return None if isinstance(self.p, int) and self.p + self.dp == PAIRS - 1 else Turn(self.p, self.dp + 1, 0)


def phase_recurrence(nc, g, a):
    with ExitStack() as es:
        sb = lambda n, s=(P, HALF), d=F32: es.enter_context(nc.sbuf_tensor(f"rec_{n}", list(s), d))
        sem = lambda n: nc.alloc_semaphore(f"rws_{n}")
        NB, NT, NC = 8, 4, 8
        wa_s, g_s = sb("wa_s", (P, P)), sb("g_s", (P, P))
        pc, pt = sb("pc", (P, 8)), sb("pt", (P, 2))
        th, zgs = g.z[:, NSH - 2, :], g.z[:, NSH - 1, :]
        sg, av, cum, eN, kkr, tmp, k2 = (sb(n) for n in "sg av cum eN kkr tmp k2".split())
        eE, eI = sg, cum
        ar = [sb(f"ar{f}", (P, NT, 2, P)) for f in range(2)]
        rk = [sb(f"rk{f}") for f in range(2)]
        wc = [sb(f"wc{f}", (P, NC)) for f in range(2)]
        bt, kt_, bh, kh, vt = (sb(n) for n in "bt kt bh kh vt".split())
        bn, kn, vn = (sb(n, (P, NT, P)) for n in "bn kn vn".split())
        rhs = sb("rhs", (P, NB, P))
        ma, mk = (t[:, PAIRS:KT, :].rearrange("p a n -> p (a n)").bitcast(F32).rearrange("p (b x n) -> p b x n", x=2, n=P)
                  for t in (g.c_hi, g.c_lo))
        X, T, TTr = sb("X", (P, NB, P)), sb("T", (P, NB, P)), sb("TT", (P, NB, P))
        gt, st, sbd = sb("gt", (P, NC, P)), sb("st", (P, NC + 1, HD)), sb("sbd", (P, NC, P))
        zt, ysb, yc = sb("zt"), sb("ysb"), sb("yc")
        M = [es.enter_context(nc.psum_tensor(f"rw_main{b}", [P, HALF], F32)) for b in range(4)]
        F = [es.enter_context(nc.psum_tensor(f"rw_front{b}", [P, HALF], F32)) for b in range(2)]
        T0, T1 = [es.enter_context(nc.psum_tensor(f"rw_tail{b}", [P, HALF], F32)) for b in range(2)]
        names = ("wa gs th zero pc pt lora sg a kkr sq ss rk cum cumE t k2 ssm rt rn kk kka eI eN eE wc AT RT VT BT KT BhT KhT "
                 "M1 M1e pair TT0 M2 M2e nat natE mv mvE T1 T1e X Xe TX T Tt Tte u ue nu wm tw pq Z ze G ge H Yl S0 S sbd ch Y "
                 "ysb mean yc sqy var sd ri bo bv gm y1 y2 y3 y4 yhi ylo").split()
        s = {n: sem(n) for n in names}
        U, Um, Wm, PQ = rhs, T, X, rhs
        block = es.enter_context(nc.Block())
        c8 = lambda t: t[:].rearrange("p (c n) -> p c n", n=CH)
        c4 = lambda t: t[:].rearrange("p (j n) -> p j n", n=P)
        bank = lambda b: M[b][:].rearrange("p (j n) -> p j n", n=P)
        col = lambda n: pc[:, n:n + 1]
        W0, A0, KK, KA, RK, GG, GB, OMKA = range(8)

        def zs(off, t):
            tile = t.p + (off + t.dp) if not isinstance(t.p, int) else t.p + off + t.dp
            return g.z[:, ds(tile, 1), t.f * HALF:(t.f + 1) * HALF].rearrange("p a n -> p (a n)")

        def wait(eng, t, name, k=1, j=None):
            if t is not None:
                eng.wait_ge(s[name], t.count(k, k if j is None else j))

        def run(eng, prologue, turn, epilogue):
            prologue(Turn(0, 0, 0))
            for f in range(2):
                turn(Turn(0, 0, f))
            with eng.Fori(1, PAIRS - 1) as p:
                for f in range(2):
                    turn(Turn(p, 0, f))
            for f in range(2):
                turn(Turn(PAIRS - 1, 0, f))
            epilogue(Turn(PAIRS - 1, 0, 1))

        @block.sync
        def _(sp):
            for p in range(PAIRS):
                cols = slice(p * P, (p + 1) * P)
                if p:
                    sp.wait_ge(s["lora"], 4 * p)
                sp.dma_start(wa_s[0:LORA_W, :], a["rw_w2"][0][:, cols]).then_inc(s["wa"], 16)
                sp.dma_start(wa_s[LORA_W:P, :], a["rw_a2"][0][:, cols]).then_inc(s["wa"], 16)
                if p:
                    sp.wait_ge(s["gm"], 2 * p)
                sp.dma_start(g_s[:], a["rw_g2"][0][:, cols]).then_inc(s["gs"], 16)

        @block.gpsimd
        def _(pool):
            pool.memset(gt[:], 0.0).then_inc(s["zero"], 1)
            pool.memset(sbd[:], 0.0).then_inc(s["zero"], 1)

            def front(t, main):
                if t is None:
                    return
                wait(pool, main, "nat", 4)
                pool.tensor_copy(vt[:], zs(8, t)).then_inc(s["VT"], 1)
                wait(pool, t, "cum")
                pool.tensor_tensor(sg[:], cum[:], sg[:], ALU.subtract).then_inc(s["cumE"], 1)
                wait(pool, t, "eI")
                pool.tensor_tensor(ar[t.f][:, :, 1, :], zs(0, t).rearrange("p (j n) -> p j n", n=P), c4(eI), ALU.mult).then_inc(s["RT"], 1)

            def tail(t):
                if t is None:
                    return
                wait(pool, t, "yhi")
                out = lambda c: c[:, ds(t.p + t.dp, 1), t.f * HALF:(t.f + 1) * HALF].rearrange("p a n -> p (a n)")
                pool.tensor_tensor(out(g.c_lo), yc[:], out(g.c_hi), ALU.subtract).then_inc(s["ylo"], 1)

            def turn(t):
                front(t.after(), t)
                tail(t.before())

            run(pool, lambda t: front(t, None), turn, tail)

        @block.scalar
        def _(act):
            act.activation(th[0:LORA_W, :], th[0:LORA_W, :], ACT.Tanh).then_inc(s["th"], 1)
            act.activation(zgs, zgs, ACT.Sigmoid).then_inc(s["th"], 1)

            def front1(t):
                if t is None:
                    return
                wait(act, t.before(), "KhT")
                wait(act, t.before(), "RT")
                wait(act, t, "pc")
                wait(act, t, "lora", 2, 1)
                act.activation(sg[:], F[0][:], ACT.Sigmoid, bias=col(W0)).then_inc(s["sg"], 1)
                wait(act, t, "lora", 2)
                act.activation(av[:], F[1][:], ACT.Sigmoid, bias=col(A0)).then_inc(s["a"], 1)

            def front2(t):
                if t is None:
                    return
                wait(act, t, "cum")
                act.activation(eN[:], cum[:], ACT.Exp, scale=DECAY).then_inc(s["eN"], 1)
                wait(act, t, "cumE")
                act.activation(eE[:], sg[:], ACT.Exp, scale=-DECAY).then_inc(s["eE"], 1)
                wait(act, t, "eN")
                act.activation(eI[:], cum[:], ACT.Exp, scale=-DECAY).then_inc(s["eI"], 1)

            def front3(t):
                if t is not None:
                    wait(act, t, "ssm")
                    act.activation(tmp[:], tmp[:], ACT.Sqrt).then_inc(s["rt"], 1)

            def tail1(t):
                if t is None:
                    return
                wait(act, t, "S", NC)
                for e in range(2):
                    r = slice(HD * e, HD * e + HD)
                    act.activation(sbd[r, :, r], st[r, 0:NC, :], ACT.Copy).then_inc(s["sbd"], 1)

            def tail2(t):
                if t is None:
                    return
                wait(act, t.before(), "yhi")
                wait(act, t, "Y")
                act.activation(ysb[:], T1[:], ACT.Copy).then_inc(s["ysb"], 1)

            def tail3(t):
                if t is not None:
                    wait(act, t, "yc")
                    act.activation(ysb[:], yc[:], ACT.Square).then_inc(s["sqy"], 1)

            def tail4(t):
                if t is not None:
                    wait(act, t, "var")
                    act.activation(ysb[:], T0[:], ACT.Sqrt, bias=g.misc(4), scale=1.0 / HD).then_inc(s["sd"], 1)

            def tail5(t):
                if t is not None:
                    wait(act, t, "y4")
                    act.activation(g.c_hi[:, ds(t.p + t.dp, 1), t.f * HALF:(t.f + 1) * HALF].rearrange("p a n -> p (a n)"),
                                   yc[:], ACT.Copy).then_inc(s["yhi"], 1)

            def level(t, lv):
                for h in range(2):
                    wait(act, t, "Tt", 8, 2 * lv + h + 1)
                    act.activation(TTr[:, 4 * h:4 * h + 4, :], bank(h), ACT.Copy).then_inc(s["Tte"], 1)

            def turn(t):
                last, nxt = t.before(), t.after()
                for h in range(2):
                    wait(act, t, "T1", 2, h + 1)
                    act.activation(T[:, 4 * h:4 * h + 4, :], bank(h), ACT.Copy).then_inc(s["T1e"], 1)
                wait(act, t, "nat", 4, 1)
                act.activation(rhs[:].rearrange("p (e j) n -> p e j n", e=2)[:, :, :, 0:HD],
                               M[2][:].rearrange("p (j e n) -> p e j n", e=2, n=HD), ACT.Copy).then_inc(s["natE"], 1)
                for x, (b, dst) in enumerate(((3, bn), (0, kn), (1, vn))):
                    wait(act, t, "nat", 4, x + 2)
                    act.activation(dst[:].rearrange("p j n -> p (j n)"), M[b][:], ACT.Copy).then_inc(s["natE"], 1)
                tail1(last)
                wait(act, t, "mv")
                act.activation(rhs[:, :, HD:P], M[2][:].rearrange("p (b n) -> p b n", n=HD), ACT.Copy).then_inc(s["mvE"], 1)
                front1(nxt)
                tail2(last)
                level(t, 0)
                tail3(last)
                front2(nxt)
                level(t, 1)
                tail4(last)
                front3(nxt)
                level(t, 2)
                level(t, 3)
                for h in range(2):
                    wait(act, t, "u", 2, h + 1)
                    act.activation(U[:, 4 * h:4 * h + 4, :], bank(h), ACT.Copy).then_inc(s["ue"], 1)
                    act.activation(Um[:, 4 * h:4 * h + 4, :], bank(h), ACT.Copy, scale=g.misc(0)).then_inc(s["ue"], 1)
                for h in range(2):
                    wait(act, t, "nu", 2, h + 1)
                    act.activation(Wm[:, 4 * h:4 * h + 4, :], bank(2 + h), ACT.Copy, scale=g.misc(1)).then_inc(s["wm"], 1)
                tail5(last)
                for h in range(2):
                    wait(act, t, "G", 2, h + 1)
                    for e in range(2):
                        r = slice(HD * e, HD * e + HD)
                        act.activation(gt[r, h::2, r], M[3 - 2 * h][r, 0:4 * HD].rearrange("p (j n) -> p j n", n=HD), ACT.Copy).then_inc(s["ge"], 1)

            def prologue(t):
                act.wait_ge(s["th"], 2)
                front1(t)
                front2(t)
                front3(t)

            def epilogue(t):
                for part in (tail1, tail2, tail3, tail4, tail5):
                    part(t)

            run(act, prologue, turn, epilogue)

        @block.vector
        def _(dve):
            at = ROWS["w0"][0]

            def front1(t):
                if t is None:
                    return
                wait(dve, t.before(), "KhT")
                wait(dve, t.before(), "RT")
                dve.tensor_scalar(pc[:], g.cols[:, ds((t.p + t.dp) * 8 + at, 8)], 1.0, None, ALU.mult).then_inc(s["pc"], 1)
                wait(dve, t, "pc")
                dve.tensor_scalar(kkr[:], zs(4, t), col(KK), None, ALU.mult).then_inc(s["kkr"], 1)
                wait(dve, t, "kkr")
                dve.tensor_tensor(tmp[:], kkr[:], kkr[:], ALU.mult).then_inc(s["sq"], 1)

            def front2(t):
                if t is None:
                    return
                wait(dve, t, "sg")
                dve.tensor_tensor_scan(cum[:], g.reset[:], sg[:], 0.0, ALU.mult, ALU.add).then_inc(s["cum"], 1)
                wait(dve, t, "a")
                dve.tensor_scalar(k2[:], av[:], col(KA), col(OMKA), ALU.mult, ALU.add).then_inc(s["t"], 1)
                wait(dve, t, "ss")
                dve.tensor_scalar(tmp[:], F[0][:], 1e-24, None, ALU.max).then_inc(s["ssm"], 1)
                wait(dve, t, "t")
                dve.tensor_tensor(k2[:], k2[:], zs(4, t), ALU.mult).then_inc(s["k2"], 1)

            def front3(t):
                if t is None:
                    return
                wait(dve, t, "rt")
                dve.reciprocal(tmp[:], tmp[:]).then_inc(s["rn"], 1)
                wait(dve, t, "rn")
                dve.tensor_tensor(kkr[:], kkr[:], tmp[:], ALU.mult).then_inc(s["kk"], 1)

            def front4(t):
                if t is None:
                    return
                wait(dve, t, "kk")
                dve.tensor_tensor(tmp[:], kkr[:], av[:], ALU.mult).then_inc(s["kka"], 1)
                wait(dve, t, "kka")
                wait(dve, t, "eN")
                dve.tensor_tensor(bt[:], tmp[:], eN[:], ALU.mult).then_inc(s["BT"], 1)
                wait(dve, t, "eE")
                dve.scalar_tensor_tensor(ar[t.f][:, :, 0, :], c4(kkr), -1.0, c4(eE), ALU.mult, ALU.mult).then_inc(s["AT"], 1)
                wait(dve, t, "k2")
                dve.tensor_tensor(kt_[:], k2[:], eN[:], ALU.mult).then_inc(s["KT"], 1)
                wait(dve, t, "eI")
                dve.tensor_copy(wc[t.f][:], eI[:, CH - 1::CH]).then_inc(s["wc"], 1)

            def front5(t):
                dve.scalar_tensor_tensor(rk[t.f][:], zs(0, t), col(RK), k2[:], ALU.mult, ALU.mult).then_inc(s["rk"], 1)
                wait(dve, t, "wc")
                wcb = wc[t.f][:].unsqueeze(2).to_broadcast([P, NC, CH])
                dve.tensor_tensor(c8(bh), c8(bt), wcb, ALU.mult).then_inc(s["BhT"], 1)
                dve.tensor_tensor(c8(kh), c8(kt_), wcb, ALU.mult).then_inc(s["KhT"], 1)

            def chain0(t):
                if t is None:
                    return
                wait(dve, t.before(), "sbd", 2)
                if t.f:
                    dve.tensor_copy(st[:, 0, :], st[:, NC, :]).then_inc(s["S0"], 1)
                else:
                    dve.memset(st[:, 0, :], 0.0).then_inc(s["S0"], 1)
                wait(dve, t, "S0")

            def chain(t, c):
                if t is None:
                    return
                wait(dve, t, "ch", NC, c + 1)
                dve.scalar_tensor_tensor(st[:, c + 1, :], st[:, c, :], wc[t.f][:, c:c + 1], T0[:, c * HD:(c + 1) * HD],
                                         ALU.mult, ALU.add).then_inc(s["S"], 1)

            def tail1(t):
                if t is None:
                    return
                wait(dve, t.before(), "y2")
                dve.tensor_scalar(pt[:], g.cols[:, ds((t.p + t.dp) * 8 + (at + GG), 2)], 1.0, None, ALU.mult).then_inc(s["pt"], 1)
                wait(dve, t.before(), "ylo")
                wait(dve, t, "mean")
                dve.scalar_tensor_tensor(yc[:], T0[:], -1.0 / HD, ysb[:], ALU.mult, ALU.add).then_inc(s["yc"], 1)

            def tail2(t):
                if t is None:
                    return
                wait(dve, t, "bo")
                dve.tensor_tensor(rk[t.f][:], T1[:], zs(8, t), ALU.mult).then_inc(s["bv"], 1)

            def tail3(t):
                if t is None:
                    return
                wait(dve, t, "sd")
                dve.reciprocal(ysb[:], ysb[:]).then_inc(s["ri"], 1)
                wait(dve, t, "ri")
                dve.tensor_tensor(yc[:], yc[:], ysb[:], ALU.mult).then_inc(s["y1"], 1)
                wait(dve, t, "y1")
                wait(dve, t, "pt")
                dve.tensor_scalar(yc[:], yc[:], pt[:, 0:1], pt[:, 1:2], ALU.mult, ALU.add).then_inc(s["y2"], 1)

            def tail4(t):
                if t is None:
                    return
                wait(dve, t, "y2")
                wait(dve, t, "bv")
                dve.tensor_tensor(yc[:], yc[:], rk[t.f][:], ALU.add).then_inc(s["y3"], 1)
                wait(dve, t, "y3")
                wait(dve, t, "gm")
                dve.tensor_tensor(yc[:], yc[:], T1[:], ALU.mult).then_inc(s["y4"], 1)

            full = lambda n, w: g.tile(n).unsqueeze(1).to_broadcast([P, w, P])
            masks = g.const[:, CT["strictT"]:CT["strictT"] + 2, :].unsqueeze(1).to_broadcast([P, 2, 2, P])

            def masked(t, x, src, dst, done):
                blk = 4 * (x % 2) + 2 * (x // 2)
                wait(dve, t, src, 4, x + 1)
                dve.tensor_tensor(dst[:, blk:blk + 2, :, :], M[x][:].rearrange("p (j x n) -> p j x n", x=2, n=P), masks, ALU.mult).then_inc(s[done], 1)

            def turn(t):
                last, nxt = t.before(), t.after()
                chain0(last)
                for x in range(4):
                    masked(t, x, "M1", ma, "M1e")
                    chain(last, x)
                wait(dve, t, "M1e", 4)
                dve.tensor_tensor(TTr[:], ma[:, :, 0, :], full("pairT", NB), ALU.mult).then_inc(s["pair"], 1)
                masked(t, 0, "M2", mk, "M2e")
                chain(last, 4)
                wait(dve, t, "pair")
                dve.tensor_tensor(TTr[:], TTr[:], full("ident", NB), ALU.add).then_inc(s["TT0"], 1)
                front5(t)
                for x in range(1, 4):
                    masked(t, x, "M2", mk, "M2e")
                    chain(last, 4 + x)
                front1(nxt)
                for lv, size in enumerate(LEVELS):
                    for h in range(2):
                        wait(dve, t, "X", 8, 2 * lv + h + 1)
                        dve.tensor_tensor(X[:, 4 * h:4 * h + 4, :], bank(h), full(f"m{size}", 4), ALU.mult).then_inc(s["Xe"], 1)
                    if lv < 2:
                        (tail1, tail2)[lv](last)
                    for h in range(2):
                        wait(dve, t, "TX", 8, 2 * lv + h + 1)
                        dve.tensor_tensor(T[:, 4 * h:4 * h + 4, :], bank(2 + h), T[:, 4 * h:4 * h + 4, :], ALU.add).then_inc(s["T"], 1)
                    if lv == 0:
                        front2(nxt)
                tail3(last)
                tail4(last)
                for h in range(2):
                    wait(dve, t, "tw", 2, h + 1)
                    dve.tensor_tensor(PQ[:, 4 * h:4 * h + 4, :], bank(h), U[:, 4 * h:4 * h + 4, :], ALU.add).then_inc(s["pq"], 1)
                wait(dve, t, "Z")
                dve.tensor_tensor(c4(zt), bank(2), ar[t.f][:, :, 1, :], ALU.add).then_inc(s["ze"], 1)
                front3(nxt)
                front4(nxt)

            def prologue(t):
                front1(t)
                front2(t)
                front3(t)
                front4(t)

            def epilogue(t):
                chain0(t)
                for c in range(NC):
                    chain(t, c)
                for part in (tail1, tail2, tail3, tail4):
                    part(t)

            run(dve, prologue, turn, epilogue)

        @block.tensor
        def _(pe):
            ident, bones = g.tile("ident"), g.tile("bones")

            def lora(t):
                if t is None:
                    return
                tok = slice(t.f * HALF, (t.f + 1) * HALF)
                if not t.f:
                    pe.wait_ge(s["wa"], (t.p + t.dp) * 32 + 32)
                wait(pe, t.before(), "ssm")
                wait(pe, t.before(), "a")
                pe.matmul(F[0][:], wa_s[0:LORA_W, :], th[0:LORA_W, tok], start=True, stop=True).then_inc(s["lora"], 1)
                pe.matmul(F[1][:], wa_s[LORA_W:P, :], th[LORA_W:P, tok], start=True, stop=True).then_inc(s["lora"], 1)

            def squares(t):
                if t is None:
                    return
                wait(pe, t, "sq")
                wait(pe, t, "sg")
                pe.matmul(F[0][:], bones, tmp[:], start=True, stop=True).then_inc(s["ss"], 1)

            def chain(t, c):
                if t is None:
                    return
                if c == 0:
                    wait(pe, t, "S0")
                    wait(pe, t, "ge", 4)
                else:
                    wait(pe, t, "S", NC, c)
                pe.matmul(T0[:, c * HD:(c + 1) * HD], gt[:, c, :], st[:, c, :], start=False, stop=True, skip_group_check=True).then_inc(s["ch"], 1)

            def outputs(t):
                if t is None:
                    return
                wait(pe, t, "sbd", 2)
                wait(pe, t, "ze")
                for c in range(NC):
                    last = pe.matmul(T1[:, c * CH:(c + 1) * CH], sbd[:, c, :], zt[:, c * CH:(c + 1) * CH], start=False, stop=True,
                                     skip_group_check=True)
                last.then_inc(s["Y"], 1)

            def mean(t):
                if t is not None:
                    wait(pe, t, "ysb")
                    pe.matmul(T0[:], bones, ysb[:], start=True, stop=True).then_inc(s["mean"], 1)

            def bonus(t):
                if t is not None:
                    wait(pe, t, "rk")
                    pe.matmul(T1[:], bones, rk[t.f][:], start=True, stop=True).then_inc(s["bo"], 1)

            def variance(t):
                if t is not None:
                    wait(pe, t, "sqy")
                    pe.matmul(T0[:], bones, ysb[:], start=True, stop=True).then_inc(s["var"], 1)

            def gate(t):
                if t is None:
                    return
                if not t.f:
                    pe.wait_ge(s["gs"], (t.p + t.dp) * 16 + 16)
                wait(pe, t, "bv")
                pe.matmul(T1[:], g_s[:], zgs[:, t.f * HALF:(t.f + 1) * HALF], start=True, stop=True).then_inc(s["gm"], 1)

            def product(left, right, b0, done):
                def half(h):
                    for b in range(4):
                        last = pe.matmul(M[b0 + h][:, b * P:(b + 1) * P], left(4 * h + b), right(4 * h + b), start=True, stop=True)
                    last.then_inc(s[done], 1)
                return half

            nT = lambda b: ma[:, b, 0, :]
            blk = lambda t: lambda b: t[:, b, :]
            jobs = [(jp, e) for jp in range(2) for e in range(2)]

            def turn(t):
                last, nxt = t.before(), t.after()
                art = ar[t.f]
                for n in ("BT", "AT", "RT"):
                    wait(pe, t, n)
                for left, n, done in ((bt, 0, "M1"), (kt_, 4, "M2")):
                    for x, (jp, e) in enumerate(jobs):
                        rows = slice(HD * e, HD * e + HD)
                        if n:
                            if x == 0:
                                wait(pe, t, "KT")
                            wait(pe, t, "M1e", 4, x + 1)
                        elif x == 1:
                            wait(pe, last, "ge", 4)
                        elif x == 2:
                            wait(pe, last, "ze")
                        for j in (2 * jp, 2 * jp + 1):
                            mm = pe.matmul(M[x][:, (j % 2) * 2 * P:(j % 2 + 1) * 2 * P], left[rows, j * P:(j + 1) * P],
                                           art[rows, j, :, :].rearrange("p x n -> p (x n)"), start=True, stop=True)
                        mm.then_inc(s[done], 1)
                        chain(last, n + x)
                wait(pe, t, "TT0")
                for h in range(2):
                    wait(pe, t, "M2e", 4, h + 1)
                    for b in range(4):
                        mm = pe.transpose(M[h][:, b * P:(b + 1) * P], TTr[:, 4 * h + b, :], ident)
                    mm.then_inc(s["T1"], 1)
                wait(pe, t, "M2e", 4)
                for x, (src, n, b) in enumerate(((None, "AT", 2), (bh, "BhT", 3), (kh, "KhT", 0), (vt, "VT", 1))):
                    wait(pe, t, n)
                    if b < 2:
                        wait(pe, t, "T1e", 2, b + 1)
                    for j in range(NT):
                        mm = pe.transpose(M[b][:, j * P:(j + 1) * P], art[:, j, 0, :] if src is None else src[:, j * P:(j + 1) * P], ident)
                    mm.then_inc(s["nat"], 1)
                lora(nxt)
                wait(pe, t, "natE", 4)
                for b in range(NB):
                    mm = pe.matmul(M[2][:, b * HD:(b + 1) * HD], mk[:, b, 0, :], vn[:, b % 4, HD * (b // 4):HD * (b // 4) + HD],
                                   start=True, stop=True)
                mm.then_inc(s["mv"], 1)
                outputs(last)
                for lv in range(len(LEVELS)):
                    x = product(nT, blk(T), 0, "X")
                    for h in range(2):
                        if lv:
                            wait(pe, t, "T", 8, 2 * lv - 1 + h)
                            wait(pe, t, "Tte", 8, 2 * lv - 1 + h)
                        x(h)
                    if lv == 0:
                        mean(last)
                        squares(nxt)
                        wait(pe, t, "mvE")
                    if lv == 1:
                        bonus(last)
                    if lv == 2:
                        variance(last)
                    if lv == 3:
                        gate(last)
                    x = product(blk(TTr), blk(X), 2, "TX")
                    for h in range(2):
                        wait(pe, t, "Xe", 8, 2 * lv + h + 1)
                        x(h)
                    for h in range(2):
                        wait(pe, t, "T", 8, 2 * lv + h + 1)
                        for b in range(4):
                            mm = pe.transpose(M[h][:, b * P:(b + 1) * P], T[:, 4 * h + b, :], ident)
                        mm.then_inc(s["Tt"], 1)
                x = product(blk(TTr), blk(rhs), 0, "u")
                for h in range(2):
                    wait(pe, t, "Tte", 8, 7 + h)
                    x(h)
                x = product(nT, blk(Um), 2, "nu")
                for h in range(2):
                    wait(pe, t, "ue", 4, 2 * h + 2)
                    x(h)
                x = product(blk(TTr), blk(Wm), 0, "tw")
                for h in range(2):
                    wait(pe, t, "wm", 2, h + 1)
                    x(h)
                wait(pe, t, "pq", 2)
                wait(pe, last, "sd")
                wait(pe, last, "y4")
                for b in range(NB):
                    e, j = b // 4, b % 4
                    mm = pe.matmul(M[2][HD * e:HD * e + HD, j * P:(j + 1) * P], PQ[:, b, 0:HD], ma[:, b, 1, :], start=True, stop=True)
                mm.then_inc(s["Z"], 1)
                for h in range(2):
                    rows = slice(CH * h, CH * h + CH)
                    for b in range(NB):
                        e, j = b // 4, b % 4
                        r = slice(HD * e, HD * e + HD)
                        mm = pe.matmul(M[3 - 2 * h][r, j * HD:(j + 1) * HD], PQ[rows, b, 0:HD], bn[rows, j, r], start=True, stop=True)
                    mm.then_inc(s["G"], 1)
                    for b in range(NB):
                        e, j = b // 4, b % 4
                        r = slice(HD * e, HD * e + HD)
                        o = T0[r, (2 * j + h) * HD:(2 * j + h + 1) * HD]
                        pe.matmul(o, bn[rows, j, r], PQ[rows, b, HD:P], start=(j == 0 and h == 0), stop=False, skip_group_check=True)
                        mm = pe.matmul(o, kn[rows, j, r], vn[rows, j, r], start=False, stop=False, skip_group_check=True)
                    if h == 0:
                        mm.then_inc(s["H"], 1)
                    for b in range(4 * h, 4 * h + 4):
                        e, j = b // 4, b % 4
                        r = slice(HD * e, HD * e + HD)
                        o = T1[r, j * P:(j + 1) * P]
                        pe.matmul(o, PQ[:, b, HD:P], ma[:, b, 1, :], start=(j == 0), stop=False, skip_group_check=True)
                        if b == 3:
                            wait(pe, t, "H")
                        pe.matmul(o, vn[:, j, r], mk[:, b, 1, :], start=False, stop=False, skip_group_check=True)

            def prologue(t):
                pe.wait_ge(s["th"], 2)
                pe.wait_ge(s["zero"], 2)
                lora(t)
                squares(t)

            def epilogue(t):
                for c in range(NC):
                    chain(t, c)
                for part in (outputs, mean, bonus, variance, gate):
                    part(t)

            run(pe, prologue, turn, epilogue)


def phase_merge(nc, g, a):
    with ExitStack() as es:
        sb = lambda n, s, d=F32: es.enter_context(nc.sbuf_tensor(f"mg_{n}", s, d))
        sem = lambda n: nc.alloc_semaphore(f"mgs_{n}")
        w = a["w_in"][0].rearrange("(k p) n -> p k n", p=P)
        wa = a["w_branch_a"][0].rearrange("(k p) n -> p k n", p=P)
        wb = a["w_branch_b"][0].rearrange("(k p) n -> p k n", p=P)
        w_used = [sem(f"used{u}") for u in range(3)]
        s_ya, s_sa, s_sb, s_pa, s_pb, s_m, s_hi, s_lo = (sem(n) for n in "ya sa sb pa pb m hi lo".split())
        ga, gb, m = sb("ga", [P, SEQ]), sb("gb", [P, SEQ]), sb("m", [P, SEQ])
        ps = [es.enter_context(nc.psum_tensor(f"mg_ps{u}", [P, SEQ], F32)) for u in range(4)]

        def source(u, i):
            if u < 2:
                return [(slice(0, KT), w[:, :, ds(i + (COL_GA, COL_GB)[u], P)])]
            return [(slice(0, PAIRS), wa[:, :, ds(i, P)]), (slice(PAIRS, KT), wb[:, :, ds(i, P)])]

        ws = split_stream(es, nc, "mg", KT, 3, source, w_used)
        block = es.enter_context(nc.Block())
        block.sync(ws.load)

        @block.gpsimd
        def _(pool):
            credit(pool, ws.lo_ready + [s_lo])
            for u in range(3):
                ws.cut_lo(pool, 0, u)

            def finish(i):
                pool.wait_ge(s_hi, i + 1)
                pool.tensor_tensor(g.b_lo[:, ds(i, 1), :].rearrange("p a n -> p (a n)"), m[:],
                                   g.b_hi[:, ds(i, 1), :].rearrange("p a n -> p (a n)"), ALU.subtract).then_inc(s_lo, 1)

            with pool.Fori(0, KT - 1) as i:
                for u in range(3):
                    ws.cut_lo(pool, i + 1, u)
                finish(i)
            finish(KT - 1)

        @block.tensor
        def _(pe):
            credit(pe, w_used)
            with pe.Fori(0, KT) as i:
                for u in range(2):
                    pe.wait_ge(ws.lo_ready[u], i + 2)
                    pe.wait_ge((s_sa, s_sb)[u], i + 1)
                    gemm_rows(pe, ps[u], ws.hi[u], ws.lo[u], g.a_hi, g.a_lo, range(KT), range(KT)).then_inc(w_used[u], 1)
                pe.wait_ge(ws.lo_ready[2], i + 2)
                pe.wait_ge(s_pa, i + 1)
                gemm_rows(pe, ps[2], ws.hi[2], ws.lo[2], g.c_hi, g.c_lo, range(PAIRS), range(PAIRS)).then_inc(s_ya, 1)
                pe.wait_ge(s_pb, i + 1)
                gemm_rows(pe, ps[3], ws.hi[2], ws.lo[2], g.c_hi, g.c_lo, range(PAIRS, KT), range(PAIRS, KT)).then_inc(w_used[2], 1)

        @block.scalar
        def _(act):
            credit(act, [s_sa, s_sb])
            for u in range(3):
                ws.split_hi(act, 0, u)

            def step(i, last):
                for u, (gate, ready, free) in enumerate(((ga, s_sa, s_pa), (gb, s_sb, s_pb))):
                    act.wait_ge(w_used[u], i + 2)
                    act.wait_ge(free, i + 1)
                    act.activation(gate[:], ps[u][:], ACT.Sigmoid).then_inc(ready, 1)
                    if not last:
                        ws.split_hi(act, i + 1, u)
                act.wait_ge(s_m, i + 1)
                act.activation(g.b_hi[:, ds(i, 1), :].rearrange("p a n -> p (a n)"), m[:], ACT.Copy).then_inc(s_hi, 1)
                if not last:
                    ws.split_hi(act, i + 1, 2)

            with act.Fori(0, KT - 1) as i:
                step(i, False)
            step(KT - 1, True)

        @block.vector
        def _(dve):
            credit(dve, [s_pa, s_pb])
            with dve.Fori(0, KT) as i:
                dve.wait_ge(s_sa, i + 2)
                dve.wait_ge(s_ya, i + 1)
                dve.tensor_tensor(ga[:], ga[:], ps[2][:], ALU.mult).then_inc(s_pa, 1)
                dve.wait_ge(s_sb, i + 2)
                dve.wait_ge(w_used[2], i + 2)
                dve.tensor_tensor(gb[:], gb[:], ps[3][:], ALU.mult).then_inc(s_pb, 1)
                dve.wait_ge(s_pb, i + 2)
                dve.wait_ge(s_pa, i + 2)
                dve.wait_ge(s_lo, i + 1)
                dve.tensor_tensor(m[:], ga[:], gb[:], ALU.add).then_inc(s_m, 1)


def gate_rows(es, nc, g):
    diag = [es.enter_context(nc.sbuf_tensor(f"gr_diag{u}", [P, CPH, P], F32)) for u in range(2)]
    ps = [es.enter_context(nc.psum_tensor(f"gr_ps{u}", [P, HALF], F32)) for u in range(2)]
    s_diag, s_mm, s_row = (nc.alloc_semaphore(f"gr_{n}") for n in "diag mm row".split())
    jobs = [(g.g1, "g1", 0), (g.g1, "g1", 1), (g.g2, "g2", 0), (g.g2, "g2", 1)]

    def diagonals(dve):
        for x, (_, name, h) in enumerate(jobs):
            if x >= 2:
                dve.wait_ge(s_mm, x - 1)
            at = ADA[name] + CPH * h
            dve.tensor_tensor(diag[x % 2][:], g.tile("ident").unsqueeze(1).to_broadcast([P, CPH, P]),
                              g.ada[:, at:at + CPH].unsqueeze(2).to_broadcast([P, CPH, P]), ALU.mult).then_inc(s_diag, 1)

    def spread(pe):
        for x in range(len(jobs)):
            pe.wait_ge(s_diag, x + 1)
            if x >= 2:
                pe.wait_ge(s_row, x - 1)
            pe.matmul(ps[x % 2][:], g.ones[:], diag[x % 2][:].rearrange("p a n -> p (a n)"), start=True, stop=True).then_inc(s_mm, 1)

    def store(act):
        for x, (dst, _, h) in enumerate(jobs):
            act.wait_ge(s_mm, x + 1)
            act.activation(dst[:, h * HALF:(h + 1) * HALF], ps[x % 2][:], ACT.Copy).then_inc(s_row, 1)

    return diagonals, spread, store, (s_row, len(jobs))


def phase_out(nc, g, a):
    with ExitStack() as es:
        sb = lambda n, s, d=F32: es.enter_context(nc.sbuf_tensor(f"ou_{n}", s, d))
        sem = lambda n: nc.alloc_semaphore(f"ous_{n}")
        w = a["w_out"][0].rearrange("(k p) n -> p k n", p=P)
        x = a["x"][0].rearrange("(t p) n -> p t n", p=P)
        stage = sb("stage", [P, KT, HALF])
        hi, lo = sb("whi", [P, KT, HALF], BF16), sb("wlo", [P, KT, HALF], BF16)
        xt = [sb(f"x{u}", [P, HALF]) for u in range(2)]
        gm = [sb(f"gm{u}", [P, HALF]) for u in range(2)]
        ps = [es.enter_context(nc.psum_tensor(f"ou_ps{u}", [P, HALF], F32)) for u in range(2)]
        s_w, s_hi, s_lo = (sem(n) for n in "w hi lo".split())
        s_x, s_mm, s_gm, s_done = ([sem(f"{n}{u}") for u in range(2)] for n in "x mm gm done".split())
        steps = TT // 2
        diagonals, spread, store, (s_row, rows) = gate_rows(es, nc, g)
        block = es.enter_context(nc.Block())

        @block.sync
        def _(sp):
            for n in range(2):
                if n:
                    sp.wait_ge(s_lo, KT)
                sp.dma_start(stage[:], w[:, :, n * HALF:(n + 1) * HALF]).then_inc(s_w, 16)
                with sp.Fori(0, steps) as i:
                    for u in range(2):
                        sp.wait_ge(s_done[u], i + (n * steps + 1))
                        sp.dma_start(xt[u][:], x[:, ds(i * 2 + u, 1), n * HALF:(n + 1) * HALF].rearrange("p a n -> p (a n)")).then_inc(s_x[u], 16)

        @block.scalar
        def _(act):
            store(act)
            for n in range(2):
                act.wait_ge(s_w, 16 * (n + 1))
                if n:
                    for u in range(2):
                        act.wait_ge(s_mm[u], steps)
                for kt in range(KT):
                    act.activation(hi[:, kt, :], stage[:, kt, :], ACT.Copy).then_inc(s_hi, 1)

        @block.gpsimd
        def _(pool):
            for n in range(2 * KT):
                pool.wait_ge(s_hi, n + 1)
                pool.tensor_tensor(lo[:, n % KT, :], stage[:, n % KT, :], hi[:, n % KT, :], ALU.subtract).then_inc(s_lo, 1)

        @block.tensor
        def _(pe):
            spread(pe)
            for n in range(2):
                pe.wait_ge(s_lo, KT * (n + 1))
                with pe.Fori(0, steps) as i:
                    for u in range(2):
                        pe.wait_ge(s_gm[u], i + (n * steps + 1))
                        gemm_tokens(pe, ps[u][:], g.b_hi, g.b_lo, ds(i * (2 * P) + u * P, P), hi, lo,
                                    slice(0, HALF), range(KT)).then_inc(s_mm[u], 1)

        @block.vector
        def _(dve):
            credit(dve, s_gm + s_done)
            diagonals(dve)
            dve.wait_ge(s_row, rows)
            for n in range(2):
                with dve.Fori(0, steps) as i:
                    for u in range(2):
                        at = n * steps
                        dve.wait_ge(s_mm[u], i + (at + 1))
                        dve.wait_ge(s_done[u], i + (at + 1))
                        dve.tensor_tensor(gm[u][:], ps[u][:], g.g1[:, n * HALF:(n + 1) * HALF], ALU.mult).then_inc(s_gm[u], 1)
                        dve.wait_ge(s_gm[u], i + (at + 2))
                        dve.wait_ge(s_x[u], i * 16 + 16 * (at + 1))
                        dve.scalar_tensor_tensor(g.x1[:, ds(i * 2 + u, 1), n * HALF:(n + 1) * HALF].rearrange("p a n -> p (a n)"),
                                                 xt[u][:], ALPHA, gm[u][:], ALU.mult, ALU.add).then_inc(s_done[u], 1)


def norm_affine(nc, g, tag, gain, bias, to_dram):
    with ExitStack() as es:
        sb = lambda n, s, d=F32: es.enter_context(nc.sbuf_tensor(f"{tag}_{n}", s, d))
        sem = lambda n: nc.alloc_semaphore(f"{tag}s_{n}")
        rows = sb("rows", [P, 2, D])
        st, mv, rs = sb("st", [P, TT, 2, 6]), sb("mv", [P, TT, 2]), sb("rs", [P, TT])
        s_in, s_st, s_mv, s_sd, s_rs, s_xn, s_g, s_b, s_out = (sem(n) for n in "in st mv sd rs xn g b out".split())
        block = es.enter_context(nc.Block())

        @block.sync
        def _(sp):
            for x, v in enumerate((gain, bias)):
                sp.dma_start(rows[:, x, :], v.partition_broadcast(P)).then_inc(s_in, 16)
            if to_dram is not None:
                for t in range(TT):
                    sp.wait_ge(s_b, t + 1)
                    sp.dma_start(to_dram[t * P:(t + 1) * P, :], g.x1[:, t, :]).then_inc(s_out, 16)
                sp.wait_ge(s_out, 16 * TT)

        @block.vector
        def _(dve):
            for t in range(TT):
                for h in range(2):
                    dve.bn_stats(st[:, t, h, :], g.x1[:, t, h * HALF:(h + 1) * HALF]).then_inc(s_st, 1)
                dve.wait_ge(s_st, 2 * t + 2)
                dve.bn_aggr(mv[:, t, :], st[:, t, :, :].rearrange("p a b -> p (a b)")).then_inc(s_mv, 1)
            dve.wait_ge(s_sd, 1)
            dve.reciprocal(rs[:], rs[:]).then_inc(s_rs, 1)
            dve.wait_ge(s_rs, 1)
            dve.wait_ge(s_in, 32)
            for t in range(TT):
                dve.tensor_scalar(g.x1[:, t, :], g.x1[:, t, :], mv[:, t, 0:1], rs[:, t:t + 1], ALU.subtract, ALU.mult).then_inc(s_xn, 1)
                if t:
                    dve.wait_ge(s_xn, t)
                    dve.tensor_tensor(g.x1[:, t - 1, :], g.x1[:, t - 1, :], rows[:, 0, :], ALU.mult).then_inc(s_g, 1)
            dve.wait_ge(s_xn, TT)
            dve.tensor_tensor(g.x1[:, TT - 1, :], g.x1[:, TT - 1, :], rows[:, 0, :], ALU.mult).then_inc(s_g, 1)

        @block.scalar
        def _(act):
            act.wait_ge(s_mv, TT)
            act.activation(rs[:], mv[:, :, 1], ACT.Sqrt, bias=g.misc(3)).then_inc(s_sd, 1)

        @block.gpsimd
        def _(pool):
            for t in range(TT):
                pool.wait_ge(s_g, t + 1)
                pool.tensor_tensor(g.x1[:, t, :], g.x1[:, t, :], rows[:, 1, :], ALU.add).then_inc(s_b, 1)


def phase_mlp(nc, g, a):
    with ExitStack() as es:
        sb = lambda n, s, d=F32: es.enter_context(nc.sbuf_tensor(f"ff_{n}", s, d))
        sem = lambda n: nc.alloc_semaphore(f"ffs_{n}")
        GT = 4
        NGR = DFF // P // GT
        w1 = a["w_ff1"][0].rearrange("(k p) n -> p k n", p=P)
        w2 = a["w_ff2"][0].rearrange("(g k p) n -> p (g k) n", p=P, k=GT)
        st1 = [sb(f"st1_{u}", [P, KT, P]) for u in range(2)]
        hi1 = [sb(f"hi1_{u}", [P, KT, P], BF16) for u in range(2)]
        lo1 = [sb(f"lo1_{u}", [P, KT, P], BF16) for u in range(2)]
        st2, hi2, lo2 = sb("st2", [P, GT, D]), sb("hi2", [P, GT, D], BF16), sb("lo2", [P, GT, D], BF16)
        r = [sb(f"r{u}", [P, SEQ]) for u in range(2)]
        brow = sb("brow", [P, D])
        ps1 = [es.enter_context(nc.psum_tensor(f"ff_ps1_{u}", [P, SEQ], F32)) for u in range(2)]
        ps2 = [es.enter_context(nc.psum_tensor(f"ff_ps2_{u}", [P, HALF], F32)) for u in range(4)]
        s_l1, s_h1, s_o1, s_used1, s_relu, s_sq, s_uhi, s_ulo = (
            [sem(f"{n}{u}") for u in range(2)] for n in "l1 h1 o1 used1 relu sq uhi ulo".split())
        s_l2, s_m2, s_h2, s_o2, s_mm2, s_acc, s_b, s_bg, s_init = (sem(n) for n in "l2 m2 h2 o2 mm2 acc b bg init".split())
        NO = 2 * TT
        block = es.enter_context(nc.Block())

        def steps(eng, first, step):
            first()
            with eng.Fori(0, (NGR - 2) // 2) as r_:
                for par in range(2):
                    step(r_ * 2 + par, par, False)
            step(NGR - 2, 0, False)
            step(NGR - 1, 1, True)

        @block.sync
        def _(sp):
            sp.dma_start(brow[:], a["b_ff2"][0].partition_broadcast(P)).then_inc(s_b, 16)
            with sp.Fori(0, NGR) as gr:
                for t in range(GT):
                    sp.wait_ge(s_o1[t % 2], gr * 2 + (t // 2 + 1))
                    sp.dma_start(st1[t % 2][:], w1[:, :, ds(gr * (GT * P) + t * P, P)]).then_inc(s_l1[t % 2], 16)
                sp.wait_ge(s_o2, gr * GT + 1)
                sp.dma_start(st2[:], w2[:, ds(gr * GT, GT), :]).then_inc(s_l2, 16)

        @block.scalar
        def _(act):
            b1 = ROWS["bff1"][0]

            def split1(m, u):
                act.wait_ge(s_l1[u], m * 16 + 16)
                act.wait_ge(s_used1[u], m + 1)
                act.activation(hi1[u][:], st1[u][:], ACT.Copy).then_inc(s_h1[u], 1)

            def group(gr, par, last):
                for t in range(GT):
                    u, m = t % 2, gr * 2 + t // 2
                    act.wait_ge(s_used1[u], m + 2)
                    act.wait_ge(s_ulo[u], m + 1)
                    act.activation(r[u][:], ps1[u][:], ACT.Relu, bias=g.cols[:, ds(gr * GT + (b1 + t), 1)]).then_inc(s_relu[u], 1)
                    if not (last and t >= 2):
                        split1(m + 1, u)
                    act.wait_ge(s_sq[u], m + 1)
                    act.activation(g.c_hi[:, GT * par + t, :], r[u][:], ACT.Copy).then_inc(s_uhi[u], 1)

            def split2(gr):
                act.wait_ge(s_m2, gr * GT + GT)
                for k in range(GT):
                    act.activation(hi2[:, k, :], st2[:, k, :], ACT.Copy).then_inc(s_h2, 1)

            def first():
                for u in range(2):
                    split1(0, u)
                group(0, 0, False)
                split2(0)

            def step(i, par, last):
                if not last:
                    group(i + 1, 1 - par, isinstance(i, int))
                    act.wait_ge(s_mm2, i * NO + NO)
                    split2(i + 1)

            credit(act, s_relu)
            steps(act, first, step)

        @block.gpsimd
        def _(pool):
            credit(pool, s_o1 + s_ulo + [s_o2])

            def split1(m, u):
                pool.wait_ge(s_h1[u], m + 1)
                pool.tensor_tensor(lo1[u][:], st1[u][:], hi1[u][:], ALU.subtract).then_inc(s_o1[u], 1)

            def group(gr, par, last):
                for t in range(GT):
                    u, m = t % 2, gr * 2 + t // 2
                    if not (last and t >= 2):
                        split1(m + 1, u)
                    pool.wait_ge(s_uhi[u], m + 1)
                    pool.tensor_tensor(g.c_lo[:, GT * par + t, :], r[u][:], g.c_hi[:, GT * par + t, :], ALU.subtract).then_inc(s_ulo[u], 1)

            def split2(gr):
                for k in range(GT):
                    pool.wait_ge(s_h2, gr * GT + k + 1)
                    pool.tensor_tensor(lo2[:, k, :], st2[:, k, :], hi2[:, k, :], ALU.subtract).then_inc(s_o2, 1)

            def first():
                for u in range(2):
                    split1(0, u)
                group(0, 0, False)
                split2(0)

            def step(i, par, last):
                if not last:
                    group(i + 1, 1 - par, isinstance(i, int))
                    split2(i + 1)

            steps(pool, first, step)

        @block.vector
        def _(dve):
            dve.wait_ge(s_b, 16)
            dve.tensor_tensor(brow[:], brow[:], g.g2[:], ALU.mult).then_inc(s_bg, 1)
            dve.wait_ge(s_bg, 1)
            for t in range(TT):
                dve.scalar_tensor_tensor(g.x1[:, t, :], g.x1[:, t, :], ALPHA, brow[:], ALU.mult, ALU.add).then_inc(s_init, 1)
            dve.wait_ge(s_init, TT)
            credit(dve, [s_acc])

            def scale2(gr):
                dve.wait_ge(s_l2, gr * 16 + 16)
                for k in range(GT):
                    dve.tensor_tensor(st2[:, k, :], st2[:, k, :], g.g2[:], ALU.mult).then_inc(s_m2, 1)

            def group(gr):
                for t in range(GT):
                    u, m = t % 2, gr * 2 + t // 2
                    dve.wait_ge(s_relu[u], m + 2)
                    dve.tensor_tensor(r[u][:], r[u][:], r[u][:], ALU.mult).then_inc(s_sq[u], 1)

            def first():
                scale2(0)
                group(0)

            def step(i, par, last):
                if not last:
                    scale2(i + 1)
                    group(i + 1)
                for x in range(NO):
                    t, h = x // 2, x % 2
                    dve.wait_ge(s_mm2, i * NO + x + 1)
                    acc = g.x1[:, t, h * HALF:(h + 1) * HALF]
                    dve.tensor_tensor(acc, ps2[x % 4][:], acc, ALU.add).then_inc(s_acc, 1)

            steps(dve, first, step)

        @block.tensor
        def _(pe):
            credit(pe, s_used1)

            def group(gr):
                for t in range(GT):
                    u, m = t % 2, gr * 2 + t // 2
                    pe.wait_ge(s_o1[u], m + 2)
                    pe.wait_ge(s_relu[u], m + 1)
                    gemm_rows(pe, ps1[u], hi1[u], lo1[u], g.a_hi, g.a_lo, range(KT), range(KT)).then_inc(s_used1[u], 1)

            def second(i, par):
                pe.wait_ge(s_o2, i * GT + GT + 1)
                for u in range(2):
                    pe.wait_ge(s_ulo[u], i * 2 + 3)
                for x in range(NO):
                    t, h = x // 2, x % 2
                    pe.wait_ge(s_acc, i * NO + (x - 3 if x > 3 else 0) + 1)
                    gemm_tokens(pe, ps2[x % 4][:], g.c_hi, g.c_lo, slice(t * P, (t + 1) * P), hi2, lo2,
                                slice(h * HALF, (h + 1) * HALF), range(GT * par, GT * par + GT)).then_inc(s_mm2, 1)

            def step(i, par, last):
                if not last:
                    group(i + 1)
                second(i, par)

            steps(pe, lambda: group(0), step)


def setup(nc, es):
    g = Net()
    sb = lambda n, s, d=F32: es.enter_context(nc.sbuf_tensor(n, s, d))
    g.const = sb("const", [P, len(CT), P])
    g.tile = lambda n: g.const[:, CT[n], :]
    g.misc = lambda n: g.const[:, CT["misc"], n:n + 1]
    g.reset = sb("reset", [P, HALF])
    g.cols = sb("cols", [P, P + KT])
    g.idb = sb("idb", [P, P], BF16)
    g.negb = sb("negb", [P, P], BF16)
    g.ada = sb("ada", [P, 6 * KT])
    g.csil = sb("csil", [P, KT])
    g.ones = sb("ones", [P, P])
    g.a_hi = sb("a_hi", [P, KT, SEQ], BF16)
    g.a_lo = sb("a_lo", [P, KT, SEQ], BF16)
    g.c_hi = sb("c_hi", [P, KT, SEQ], BF16)
    g.c_lo = sb("c_lo", [P, KT, SEQ], BF16)
    return g


def build(nc, a, out):
    with ExitStack() as es:
        g = setup(nc, es)
        with ExitStack() as shifted:
            g.z = shifted.enter_context(nc.sbuf_tensor("z", [P, NSH, SEQ], F32))
            with nc.cleanup_on_exit():
                phase_start(nc, g, a)
            with nc.cleanup_on_exit():
                phase_recurrence(nc, g, a)
        with nc.cleanup_on_exit(), ExitStack() as scope:
            g.v = scope.enter_context(nc.sbuf_tensor("v", [P, TT, DR], F32))
            phase_values(nc, g, a)
            phase_stick(nc, g, a)
        g.g1, g.g2 = (es.enter_context(nc.sbuf_tensor(n, [P, D], F32)) for n in ("g1", "g2"))
        g.x1 = es.enter_context(nc.sbuf_tensor("x1", [P, TT, D], F32))
        with nc.cleanup_on_exit():
            with ExitStack() as scope:
                g.b_hi, g.b_lo = (scope.enter_context(nc.sbuf_tensor(n, [P, KT, SEQ], BF16)) for n in ("b_hi", "b_lo"))
                phase_merge(nc, g, a)
                phase_out(nc, g, a)
            norm_affine(nc, g, "n1", a["ln1_g"][0], a["ln1_b"][0], None)
            modulate(nc, g, "m2", g.x1, None, ADA["sc2"], ADA["sh2"], g.a_hi, g.a_lo)
            phase_mlp(nc, g, a)
            norm_affine(nc, g, "n2", a["ln2_g"][0], a["ln2_b"][0], out[0])


_INS = ["x", "c", "w_ada", "b_ada", "w_in", "mu_shift", "rw_w0", "rw_w2", "rw_a0", "rw_a2", "rw_g2", "rw_kk", "rw_ka", "rw_rk",
        "rw_gn_g", "rw_gn_b", "w_branch_a", "w_branch_b", "w_out", "ln1_g", "ln1_b", "w_ff1", "b_ff1", "w_ff2", "b_ff2",
        "ln2_g", "ln2_b"]


def kernel(**inputs):
    import concourse.bacc as bacc
    from concourse.bass_utils import run_bass_kernel_spmd

    nc = bacc.Bacc("TRN2", target_bir_lowering=False, num_devices=1)
    tiles, reset = constants()
    arrays = {n: np.ascontiguousarray(inputs[n]) for n in _INS} | {"const_tiles": tiles, "const_reset": reset}
    aps = {n: nc.dram_tensor(n, v.shape, mybir.dt.from_np(v.dtype), kind="ExternalInput").ap() for n, v in arrays.items()}
    out = nc.dram_tensor("out", [1, SEQ, D], F32, kind="ExternalOutput").ap()
    build(nc, aps, out)
    r = run_bass_kernel_spmd(nc, [arrays], core_ids=[0])
    return r.results[0]["out"]
```

```python
from contextlib import ExitStack

import numpy as np

import concourse.bass as bass
from concourse import mybir

F32 = mybir.dt.float32
BF16 = mybir.dt.bfloat16
ALU = mybir.AluOpType
ACT = mybir.ActivationFunctionType
ds = bass.ds

P = 128
SEQ = 1024
D = 1024
KT = D // P
TT = SEQ // P
HALF = 512
DR = 512
PAIRS = DR // P
HD = 64
DFF = 4 * D
LORA_W, LORA_A, LORA_G = 64, 64, 128
D_SHIFT = 3 * DR + LORA_W + LORA_A + LORA_G
NSH = D_SHIFT // P
COL_Q, COL_K, COL_V = D_SHIFT, D_SHIFT + DR, D_SHIFT + 2 * DR
COL_GA, COL_GB = D_SHIFT + 3 * DR, D_SHIFT + 3 * DR + D
CH = 64
ALPHA = 2.0 ** 0.25
LN_EPS, ADALN_EPS, GN_EPS = 1e-5, 1e-6, 64e-5
DECAY = float(np.exp(-0.5))
LEVELS = (2, 4, 8, 16)

ROWS = {}
_at = 0
for _name, _n in (("mu", NSH), ("w0", 8 * PAIRS), ("bff1", DFF // P), ("bada", 6 * KT)):
    ROWS[_name] = (_at, _n)
    _at += _n
ROWS["c"] = (P, KT)
PAIR_ROWS = ("w0", "a0", "kk", "ka", "rk", "gng", "gnb")

CT = {n: i for i, n in enumerate(("ident", "strictT", "inclT", "pairT", "m2", "m4", "m8", "m16", "bones", "neg", "misc"))}


def constants():
    i, j = np.meshgrid(np.arange(P), np.arange(P), indexing="ij")
    same = i // CH == j // CH
    t = np.zeros((P, len(CT), P), np.float32)
    t[:, CT["ident"]] = i == j
    t[:, CT["strictT"]] = same & (i < j)
    t[:, CT["inclT"]] = same & (i <= j)
    t[:, CT["pairT"]] = (i // 2 == j // 2) & (i < j)
    for s in LEVELS:
        t[:, CT[f"m{s}"]] = (i // (2 * s) == j // (2 * s)) & (i % (2 * s) >= s) & (j % (2 * s) < s)
    t[:, CT["bones"]] = i // HD == j // HD
    t[:, CT["neg"]] = np.where(j >= i, np.float32(-1e30), 0)
    t[:, CT["misc"], 0] = i[:, 0] % CH < CH // 2
    t[:, CT["misc"], 1] = i[:, 0] % CH >= CH // 2
    t[:, CT["misc"], 2] = ADALN_EPS
    t[:, CT["misc"], 3] = LN_EPS
    t[:, CT["misc"], 4] = GN_EPS
    reset = np.ones((P, HALF), np.float32)
    reset[:, ::CH] = 0
    return t, reset


def credit(eng, sems):
    for s in sems:
        eng.sem_inc(s, 1)


class Turn:

    def __init__(self, p, dp, f, n):
        self.p, self.dp, self.f, self.n = p, dp, f, n

    def count(self, k, j):
        return self.p * (2 * k) + ((2 * self.dp + self.f) * k + j)

    def before(self):
        if self.f:
            return Turn(self.p, self.dp, 0, self.n)
        return None if isinstance(self.p, int) and self.p + self.dp == 0 else Turn(self.p, self.dp - 1, 1, self.n)

    def after(self):
        if not self.f:
            return Turn(self.p, self.dp, 1, self.n)
        return None if isinstance(self.p, int) and self.p + self.dp == self.n - 1 else Turn(self.p, self.dp + 1, 0, self.n)


def turns(eng, n, prologue, turn, epilogue):
    prologue(Turn(0, 0, 0, n))
    for f in range(2):
        turn(Turn(0, 0, f, n))
    with eng.Fori(1, n - 1) as p:
        for f in range(2):
            turn(Turn(p, 0, f, n))
    for f in range(2):
        turn(Turn(n - 1, 0, f, n))
    epilogue(Turn(n - 1, 0, 1, n))


class Net:
    pass


def split_stream(es, nc, tag, count, units, source, w_used):
    stage = [es.enter_context(nc.sbuf_tensor(f"{tag}_stage{u}", [P, KT, P], F32)) for u in range(units)]
    hi = [es.enter_context(nc.sbuf_tensor(f"{tag}_whi{u}", [P, KT, P], BF16)) for u in range(units)]
    lo = [es.enter_context(nc.sbuf_tensor(f"{tag}_wlo{u}", [P, KT, P], BF16)) for u in range(units)]
    loaded = [nc.alloc_semaphore(f"{tag}_loaded{u}") for u in range(units)]
    hi_ready = [nc.alloc_semaphore(f"{tag}_hi_ready{u}") for u in range(units)]
    lo_ready = [nc.alloc_semaphore(f"{tag}_lo_ready{u}") for u in range(units)]

    def load_step(sp, i):
        col = i * P if isinstance(i, int) else sp.snap(i * P)
        for u in range(units):
            for w in {0: (0,), 1: range(1, units)}.get(u, ()):
                sp.wait_ge(lo_ready[w], i + 1)
            parts = source(u, col)
            for dst, src in parts:
                sp.dma_start(stage[u][:, dst, :], src).then_inc(loaded[u], 16)

    def load(sp):
        with sp.Fori(0, count) as i:
            load_step(sp, i)

    def split_hi(act, i, u):
        act.wait_ge(loaded[u], (i + 1) * (16 * len(source(u, 0))))
        act.wait_ge(w_used[u], i + 1)
        act.activation(hi[u][:], stage[u][:], ACT.Copy).then_inc(hi_ready[u], 1)

    def cut_lo(pool, i, u):
        pool.wait_ge(hi_ready[u], i + 1)
        pool.tensor_tensor(lo[u][:], stage[u][:], hi[u][:], ALU.subtract).then_inc(lo_ready[u], 1)

    def split_lo(pool, first=True):
        if first:
            credit(pool, lo_ready)
        with pool.Fori(0, count) as i:
            for u in range(units):
                cut_lo(pool, i, u)

    st = Net()
    st.stage, st.hi, st.lo, st.loaded, st.hi_ready, st.lo_ready = stage, hi, lo, loaded, hi_ready, lo_ready
    st.load_step = load_step
    st.load, st.split_hi, st.split_lo, st.cut_lo = load, split_hi, split_lo, cut_lo
    return st


def gemm_rows(pe, out, whi, wlo, act_hi, act_lo, kts, slots, halfway=None):
    n = len(kts)
    for x, (kt, slot) in enumerate(zip(kts, slots)):
        if halfway is not None and x == n // 2:
            halfway()
        for y, (w, a) in enumerate(((whi, act_hi), (whi, act_lo), (wlo, act_hi))):
            for h in range(2):
                last = pe.matmul(out[:, h * HALF:(h + 1) * HALF], w[:, kt, :], a[:, slot, h * HALF:(h + 1) * HALF],
                                 start=(x == 0 and y == 0), stop=(x == n - 1 and y == 2))
    return last


ADA = {n: i * KT for i, n in enumerate(("sh1", "sc1", "g1", "sh2", "sc2", "g2"))}
ADA_PARTS = 6 * D // HALF
CPH = HALF // P


def phase_start(nc, g, a):
    with ExitStack() as es:
        sb = lambda n, s, d=F32: es.enter_context(nc.sbuf_tensor(n, s, d))
        psum = lambda n, w=HALF: es.enter_context(nc.psum_tensor(n, [P, w], F32))
        sem = lambda n: nc.alloc_semaphore(n)
        rows, crows = sb("rows", [P, P]), sb("crows", [KT, P])
        s_in, s_tr, s_zero, s_one, s_cols, s_tab = (sem(f"par_{n}") for n in "in tr zero one cols tab".split())
        pair_vecs = {"w0": a["rw_w0"][0], "a0": a["rw_a0"][0], "kk": a["rw_kk"][0], "ka": a["rw_ka"][0],
                     "rk": a["rw_rk"][0].rearrange("h d -> (h d)"), "gng": a["rw_gn_g"][0], "gnb": a["rw_gn_b"][0]}
        vecs = {"mu": a["mu_shift"][0], "bff1": a["b_ff1"][0], "bada": a["b_ada"][0]}
        n_in = 16 * (len(vecs) + len(pair_vecs) + 2)
        at8 = ROWS["w0"][0]
        s_const = sem("par_const")
        steps = NSH // 2
        early = ADA_PARTS - steps
        csig = sb("csig", [P, KT])
        wst = [g.z[:, 4 * n:4 * n + 4, :].rearrange("p a n -> p (a n)").rearrange("p (k n) -> p k n", n=HALF) for n in range(early - 2)]
        wst += [sb(f"ada_w{u}", [P, KT, HALF])[:] for u in range(2)]
        acc = [sb(f"ada_acc{u}", [P, HALF]) for u in range(2)]
        ada_ps = [psum(f"ada_ps{u}") for u in range(2)]
        s_wada = [sem(f"ada_in{n}") for n in range(early)]
        s_acc, s_sum = ([sem(f"ada_{n}{u}") for u in range(2)] for n in "acc sum".split())
        s_sig, s_sil, s_step, s_ada, s_wlate, s_late, s_lstep, s_lsum, s_lada = (
            sem(f"ada_{n}") for n in "sig sil step ada wlate late lstep lsum lada".split())
        order = [0, 2, 1, 3, 4]
        w_ada = a["w_ada"][0].rearrange("(k p) n -> p k n", p=P)
        b_at = ROWS["bada"][0]
        NB = 4
        x = [(g.c_hi, g.c_lo)[t // 4][:].rearrange("p a n -> p (a n)").bitcast(F32)[:, (t % 4) * D:(t % 4 + 1) * D] for t in range(TT)]
        st, mv, rs = sb("st", [P, TT, 2, 6]), sb("mv", [P, TT, 2]), sb("rs", [P, TT, 2])
        hf = [sb(f"hf{u}", [P, HALF]) for u in range(NB)]
        s_x = [sem(f"h_x{t}") for t in range(TT)]
        s_st, s_mv, s_sd, s_rs, s_xn, s_turn, s_hf, s_hi, s_lo0, s_lo1 = (
            sem(f"h_{n}") for n in "st mv sd rs xn turn hf hi lo0 lo1".split())
        pieces = [(kt, h) for k0 in (0, KT // 2) for h in range(2) for kt in range(k0, k0 + KT // 2)]
        NH = len(pieces)
        w_used, s_raw, s_diff, s_shift = ([sem(f"zs_{n}{u}") for u in range(2)] for n in "used raw diff shift".split())
        s_pad = sem("zs_pad")
        raw = [sb(f"zs_rawt{u}", [P, SEQ + 1]) for u in range(2)]
        diff = [sb(f"zs_dift{u}", [P, SEQ]) for u in range(2)]
        ps = [psum(f"zs_ps{u}", SEQ) for u in range(2)]
        h_ps = [psum(f"h_ps{u}")[:] for u in range(2)] + [ps[1][:, h * HALF:(h + 1) * HALF] for h in range(2)]
        w = a["w_in"][0].rearrange("(k p) n -> p k n", p=P)
        ws = split_stream(
            es, nc, "zs", steps, 2, lambda u, i: [(slice(0, KT), w[:, :, ds(i * 2 + u * P, P)])], w_used)
        block = es.enter_context(nc.Block())

        @block.sync
        def _(sp):
            sp.dma_start(g.const[:], a["const_tiles"]).then_inc(s_const, 16)
            sp.dma_start(g.reset[:], a["const_reset"]).then_inc(s_in, 16)
            sp.dma_start(crows[:], a["c"][0].rearrange("(t p) -> t p", p=P)).then_inc(s_in, 16)
            for t in range(TT):
                sp.dma_start(x[t], a["x"][0][t * P:(t + 1) * P, :]).then_inc(s_x[t], 16)
            sp.wait_ge(s_zero, 1)
            for name, v in vecs.items():
                at, n = ROWS[name]
                sp.dma_start(rows[at:at + n, :], v.rearrange("(t p) -> t p", p=P)).then_inc(s_in, 16)
            for y, name in enumerate(PAIR_ROWS):
                sp.dma_start(rows[at8 + y:at8 + 8 * PAIRS:8, :], pair_vecs[name].rearrange("(t p) -> t p", p=P)).then_inc(s_in, 16)

            def chunk(n):
                at = order[n] * HALF
                sp.dma_start(wst[n], w_ada[:, :, at:at + HALF]).then_inc(s_wada[n], 16)

            for n in range(early - 1):
                chunk(n)

            def late(i):
                sp.wait_ge(s_late, i + 1)
                sp.dma_start(wst[early - 2], w_ada[:, :, ds(i * HALF + early * HALF, HALF)]).then_inc(s_wlate, 16)

            ws.load_step(sp, 0)
            chunk(early - 1)
            sp.wait_ge(s_acc[early % 2], early // 2)
            late(0)
            with sp.Fori(1, steps) as i:
                ws.load_step(sp, i)
                late(i)

        @block.tensor
        def _(pe):
            pe.wait_ge(s_const, 16)
            pe.wait_ge(s_in, n_in)
            pe.transpose(ps[0][:, 0:P], rows[:], g.tile("ident"))
            pe.transpose(ps[0][:, P:P + KT], crows[:], g.const[0:KT, CT["ident"], 0:KT]).then_inc(s_tr, 1)

            def columns(u):
                for c in range(CPH):
                    last = pe.matmul(ada_ps[u][:, c:c + 1], acc[u][:, c * P:(c + 1) * P], g.ones[:, 0:1], start=True, stop=True)
                return last

            def turn(n):
                kt, h = pieces[n]
                pe.wait_ge(s_xn, 4 * h + 4)
                if n >= NB:
                    pe.wait_ge(s_hf, n - NB + 1)
                for j in range(4):
                    last = pe.transpose(h_ps[n % NB][:, j * P:(j + 1) * P], x[4 * h + j][:, kt * P:(kt + 1) * P], g.tile("ident"))
                last.then_inc(s_turn, 1)

            pe.wait_ge(s_one, 1)
            credit(pe, w_used)

            def early_columns(n):
                pe.wait_ge(s_acc[n % 2], n // 2 + 1)
                if n >= 2:
                    pe.wait_ge(s_ada, n - 1)
                columns(n % 2).then_inc(s_sum[n % 2], 1)

            for n in range(NB):
                turn(n)
            early_columns(0)
            early_columns(1)
            for n in range(NB, KT + NB):
                turn(n)
            early_columns(2)
            early_columns(3)
            for n in range(KT + NB, NH):
                turn(n)
            for lo in (s_lo0, s_lo1):
                pe.wait_ge(lo, KT // 2)
            late = early % 2
            pe.wait_ge(s_cols, 1)

            def rest():
                for lo in (s_lo0, s_lo1):
                    pe.wait_ge(lo, KT)

            with pe.Fori(0, steps) as i:
                for u in range(2):
                    pe.wait_ge(ws.lo_ready[u], i + 2)
                    pe.wait_ge(s_raw[u], i + 1)
                    gemm_rows(pe, ps[u], ws.hi[u], ws.lo[u], g.a_hi, g.a_lo, range(KT), range(KT), rest).then_inc(w_used[u], 1)
                    if u == 0:
                        pe.wait_ge(s_late, i + 2)
                        pe.wait_ge(s_lada, i + 1)
                        columns(late).then_inc(s_lsum, 1)
            early_columns(early - 1)

        @block.scalar
        def _(act):
            cc = ROWS["c"][0]

            def normalise(t):
                act.wait_ge(s_rs, 2 * t + 2)
                act.activation(x[t], x[t], ACT.Identity, bias=rs[:, t, 1:2], scale=rs[:, t, 0:1]).then_inc(s_xn, 1)

            act.wait_ge(s_const, 16)
            for t in range(TT):
                act.wait_ge(s_mv, t + 1)
                act.activation(rs[:, t, 0:1], mv[:, t, 1:2], ACT.Sqrt, bias=g.misc(2)).then_inc(s_sd, 1)
                if t:
                    normalise(t - 1)
            normalise(TT - 1)
            act.wait_ge(s_cols, 1)
            act.activation(csig[:], g.cols[:, cc:cc + KT], ACT.Sigmoid).then_inc(s_sig, 1)
            credit(act, s_raw)
            for n in range(NH):
                kt, h = pieces[n]
                if n % KT == 0:
                    act.wait_ge(s_ada, 2 * (n // KT) + 2)
                act.wait_ge(s_turn, n + 1)
                if n >= NB:
                    act.wait_ge((s_lo0, s_lo1)[n % 2], n // 2 - 1)
                act.activation(hf[n % NB][:], h_ps[n % NB], ACT.Identity, bias=g.ada[:, ADA["sh1"] + kt:ADA["sh1"] + kt + 1],
                               scale=g.ada[:, ADA["sc1"] + kt:ADA["sc1"] + kt + 1]).then_inc(s_hf, 1)
            for u in range(2):
                ws.split_hi(act, 0, u)
            act.wait_ge(s_pad, 2)
            with act.Fori(0, steps - 1) as i:
                for u in range(2):
                    act.wait_ge(w_used[u], i + 2)
                    act.wait_ge(s_shift[u], i + 1)
                    act.activation(raw[u][:, 1:SEQ + 1], ps[u][:], ACT.Copy).then_inc(s_raw[u], 1)
                    ws.split_hi(act, i + 1, u)
            for u in range(2):
                act.wait_ge(w_used[u], steps + 1)
                act.wait_ge(s_shift[u], steps)
                act.activation(raw[u][:, 1:SEQ + 1], ps[u][:], ACT.Copy).then_inc(s_raw[u], 1)

        @block.vector
        def _(dve):
            dve.memset(rows[:], 0.0).then_inc(s_zero, 1)
            dve.memset(g.ones[:], 1.0).then_inc(s_one, 1)
            credit(dve, s_shift + [s_late, s_lada])
            for u in range(2):
                dve.memset(raw[u][:, 0:1], 0.0).then_inc(s_pad, 1)
            def accumulate(buf, u, step, before, done):
                for kt in range(KT):
                    src, c = wst[buf][:, kt, :], g.csil[:, kt:kt + 1]
                    if kt:
                        dve.wait_ge(step, before + kt)
                        op = dve.scalar_tensor_tensor(acc[u][:], src, c, acc[u][:], ALU.mult, ALU.add)
                    else:
                        op = dve.tensor_scalar(acc[u][:], src, c, None, ALU.mult)
                    op.then_inc(done if kt == KT - 1 else step, 1)

            def chunk(n):
                dve.wait_ge(s_wada[n], 16)
                if n >= 2:
                    dve.wait_ge(s_sum[n % 2], n // 2)
                accumulate(n, n % 2, s_step, n * (KT - 1), s_acc[n % 2])

            def finish(n):
                dve.wait_ge(s_sum[n % 2], n // 2 + 1)
                at = order[n] * CPH
                one = 1.0 if ADA["sc1"] <= at < ADA["g1"] else 0.0
                dve.scalar_tensor_tensor(g.ada[:, at:at + CPH], ada_ps[n % 2][:, 0:CPH], one,
                                         g.cols[:, b_at + at:b_at + at + CPH], ALU.add, ALU.add).then_inc(s_ada, 1)

            def normalise(t):
                dve.wait_ge(s_sd, t + 1)
                dve.reciprocal(rs[:, t, 0:1], rs[:, t, 0:1]).then_inc(s_rs, 1)
                dve.wait_ge(s_rs, 2 * t + 1)
                dve.scalar_tensor_tensor(rs[:, t, 1:2], mv[:, t, 0:1], -1.0, rs[:, t, 0:1], ALU.mult, ALU.mult).then_inc(s_rs, 1)

            for t in range(TT):
                dve.wait_ge(s_x[t], 16)
                for h in range(2):
                    dve.bn_stats(st[:, t, h, :], x[t][:, h * HALF:(h + 1) * HALF]).then_inc(s_st, 1)
                dve.wait_ge(s_st, 2 * t + 2)
                dve.bn_aggr(mv[:, t, :], st[:, t, :, :].rearrange("p a b -> p (a b)")).then_inc(s_mv, 1)
                if t:
                    normalise(t - 1)
            normalise(TT - 1)
            dve.wait_ge(s_tr, 1)
            dve.tensor_copy(g.cols[:], ps[0][:, 0:P + KT]).then_inc(s_cols, 1)
            dve.wait_ge(s_cols, 1)
            ka, cc = at8 + PAIR_ROWS.index("ka"), ROWS["c"][0]
            dve.tensor_scalar(g.cols[:, at8 + 7:at8 + 8 * PAIRS:8], g.cols[:, ka:at8 + 8 * PAIRS:8], -1.0, 1.0, ALU.mult, ALU.add).then_inc(s_tab, 1)
            dve.tensor_copy(g.idb[:], g.tile("ident")).then_inc(s_tab, 1)
            dve.tensor_copy(g.negb[:], g.tile("neg")).then_inc(s_tab, 1)
            dve.wait_ge(s_sig, 1)
            dve.tensor_tensor(g.csil[:], csig[:], g.cols[:, cc:cc + KT], ALU.mult).then_inc(s_sil, 1)
            dve.wait_ge(s_sil, 1)

            def low(n):
                kt, h = pieces[n]
                dve.wait_ge(s_hi, n + 1)
                at = slice(h * HALF, (h + 1) * HALF)
                dve.tensor_tensor(g.a_lo[:, kt, at], hf[n % NB][:], g.a_hi[:, kt, at], ALU.subtract).then_inc(s_lo1, 1)

            for n in range(NH):
                kt, h = pieces[n]
                if n % KT == 0:
                    for x_ in range(2):
                        chunk(2 * (n // KT) + x_)
                    for x_ in range(2):
                        finish(2 * (n // KT) + x_)
                dve.wait_ge(s_hf, n + 1)
                dve.tensor_copy(g.a_hi[:, kt, h * HALF:(h + 1) * HALF], hf[n % NB][:]).then_inc(s_hi, 1)
                if n % 2:
                    low(n)
            chunk(early - 1)
            mu = ROWS["mu"][0]
            with dve.Fori(0, steps) as i:
                dve.wait_ge(s_wlate, i * 16 + 16)
                dve.wait_ge(s_lada, i + 1)
                accumulate(early - 2, early % 2, s_lstep, i * (KT - 1), s_late)
                for u in range(2):
                    dve.wait_ge(s_raw[u], i + 2)
                    dve.tensor_tensor(diff[u][:], raw[u][:, 0:SEQ], raw[u][:, 1:SEQ + 1], ALU.subtract).then_inc(s_diff[u], 1)
                    if u == 0:
                        dve.wait_ge(s_lsum, i + 1)
                        dve.tensor_tensor(g.ada[:, ds(i * CPH + early * CPH, CPH)], ada_ps[early % 2][:, 0:CPH],
                                          g.cols[:, ds(i * CPH + (b_at + early * CPH), CPH)], ALU.add).then_inc(s_lada, 1)
                    dve.wait_ge(s_diff[u], i + 1)
                    dve.scalar_tensor_tensor(g.z[:, ds(i * 2 + u, 1), :].rearrange("p a n -> p (a n)"), diff[u][:],
                                             g.cols[:, ds(i * 2 + (mu + u), 1)],
                                             raw[u][:, 1:SEQ + 1], ALU.mult, ALU.add).then_inc(s_shift[u], 1)
            finish(early - 1)
            dve.wait_ge(s_lada, steps + 1)
            v = g.ada[:, ADA["sc2"]:ADA["sc2"] + KT]
            dve.tensor_scalar(v, v, 1.0, None, ALU.add).then_inc(s_ada, 1)

        @block.gpsimd
        def _(pool):
            credit(pool, ws.lo_ready)
            for n in range(0, NH, 2):
                kt, h = pieces[n]
                pool.wait_ge(s_hi, n + 1)
                at = slice(h * HALF, (h + 1) * HALF)
                pool.tensor_tensor(g.a_lo[:, kt, at], hf[n % NB][:], g.a_hi[:, kt, at], ALU.subtract).then_inc(s_lo0, 1)
            ws.split_lo(pool, False)


def gemm_tokens(pe, out, act_hi, act_lo, at, whi, wlo, n, slots):
    k = len(slots)
    for x, slot in enumerate(slots):
        for y, (a, w) in enumerate(((act_hi, whi), (act_hi, wlo), (act_lo, whi))):
            last = pe.matmul(out, a[:, slot, at], w[:, x, n], start=(x == 0 and y == 0), stop=(x == k - 1 and y == 2))
    return last


def value_weights(g):
    stage = g.z[:, 0:4, :].rearrange("p a n -> p (a n)").rearrange("p (k n) -> p k n", n=DR)
    hi, lo = (g.z[:, at:at + 2, :].rearrange("p a n -> p (a n)").bitcast(BF16).rearrange("p (k n) -> p k n", n=DR) for at in (4, 6))
    return stage, hi, lo


def values(g):
    return [c[:, PAIRS:KT, :].rearrange("p a n -> p (a n)").bitcast(F32).rearrange("p (a n) -> p a n", a=PAIRS)
            for c in (g.c_hi, g.c_lo)]


def phase_stick(nc, g, a):
    with ExitStack() as es:
        sb = lambda n, s, d=F32: es.enter_context(nc.sbuf_tensor(n, s, d))
        sem = lambda n: nc.alloc_semaphore(n)
        w = a["w_in"][0].rearrange("(k p) n -> p k n", p=P)
        v = values(g)
        qk = [g.z[:, 4 + b, :] for b in range(2)]
        vs = sb("vs", [P, TT, P])
        att = [g.z[:, 6 + b, :] for b in range(3)]
        rest = [g.z[:, 9 + b, :] for b in range(3)]
        prod = [sb(f"prod{b}", [P, SEQ + 1]) for b in range(2)]
        attT = [g.z[:, 12 + b, :].rearrange("p (a n) -> p a n", n=P) for b in range(2)]
        zps = [es.enter_context(nc.psum_tensor(f"z_ps{b}", [P, SEQ], F32)) for b in range(2)]
        trps = [es.enter_context(nc.psum_tensor(f"tr_ps{b}", [P, HALF], F32)) for b in range(2)]
        ops = es.enter_context(nc.psum_tensor("o_ps", [P, SEQ], F32))
        w_used = [sem(f"sb_used{u}") for u in range(2)]
        s_one, s_qk, s_vs, s_z, s_sig, s_scan, s_att, s_tr, s_pv, s_ohi, s_olo = (
            sem(f"sb_{n}") for n in "one qk vs z sig scan att tr pv ohi olo".split())
        s_tre = [sem(f"sb_tre{b}") for b in range(2)]
        units = [(e, i) for i in range(TT) for e in range(2)]
        NU = len(units)
        LAST = NU - 1
        s_half = sem("sb_half")
        halves = [(1, 0), (0, 0), (1, 1), (0, 1)]
        groups = [(n, k0, min(k0 + 4, units[n][1] + 1)) for n in range(NU) for k0 in range(0, units[n][1] + 1, 4)]
        NG = len(groups)
        assert NG % 2 == 0
        of_unit = [[x for x, gr in enumerate(groups) if gr[0] == n] for n in range(NU)]
        ws = split_stream(
            es, nc, "sb", PAIRS, 2, lambda u, i: [(slice(0, KT), w[:, :, ds(i + (COL_Q, COL_K)[u], P)])], w_used)
        block = es.enter_context(nc.Block())
        block.sync(ws.load)

        def pairs(eng, pair):
            pair(0, True, False)
            with eng.Fori(1, PAIRS - 1) as p:
                pair(p, False, False)
            pair(PAIRS - 1, False, True)

        @block.gpsimd
        def _(pool):
            credit(pool, [s_att])

            def pair(p, first, last):
                pool.wait_ge(s_pv, p * NU + 1)
                for x in range(2):
                    pool.tensor_copy(vs[:, 4 * x:4 * x + 4, :].rearrange("p a n -> p (a n)"),
                                     v[x][:, ds(p, 1), :].rearrange("p a n -> p (a n)")).then_inc(s_vs, 1)
                for n, (e, i) in enumerate(units):
                    nk = (i + 1) * P
                    pool.wait_ge(s_scan, p * NU + n + 1)
                    pool.tensor_tensor(att[n % 3][:, 0:nk], att[n % 3][:, 0:nk], prod[n % 2][:, SEQ - nk + 1:SEQ + 1],
                                       ALU.mult).then_inc(s_att, 1)

            pairs(pool, pair)

        @block.tensor
        def _(pe):
            credit(pe, w_used + [s_pv])

            def half(p, x):
                u, h = halves[x]
                if h == 0:
                    pe.wait_ge(ws.lo_ready[u], p + 2)
                    pe.wait_ge(s_sig, p * NU + 1)
                at = slice(h * HALF, (h + 1) * HALF)
                for kt in range(KT):
                    for y, (w_part, a_part) in enumerate(((ws.hi[u], g.a_hi), (ws.hi[u], g.a_lo), (ws.lo[u], g.a_hi))):
                        mm = pe.matmul(zps[u][:, at], w_part[:, kt, :], a_part[:, kt, at], start=(kt == 0 and y == 0),
                                       stop=(kt == KT - 1 and y == 2))
                mm.then_inc(s_half if h == 0 else w_used[u], 1)

            def scores(p, n):
                e, i = units[n]
                nk = (i + 1) * P
                if n == 0 or nk == HALF + P and e == 0:
                    pe.wait_ge(s_qk, p * 4 + (4 if n else 2))
                if n >= 2:
                    pe.wait_ge(s_sig, p * NU + n)
                q = qk[0][HD * e:HD * e + HD, i * P:(i + 1) * P]
                for b in range(0, nk, HALF):
                    b1 = min(nk, b + HALF)
                    pe.matmul(zps[n % 2][:, b:b1], q, qk[1][HD * e:HD * e + HD, b:b1], start=True, stop=True)
                pe.matmul(zps[n % 2][:, i * P:nk], g.idb[:], g.negb[:], start=False, stop=True, skip_group_check=True).then_inc(s_z, 1)

            def turn(p, n):
                e, i = units[n]
                pe.wait_ge(s_att, p * NU + n + 2)
                for x in of_unit[n]:
                    _, k0, k1 = groups[x]
                    pe.wait_ge(s_tre[x % 2], p * (NG // 2) + (x // 2 + 1))
                    for kt in range(k0, k1):
                        last = pe.transpose(trps[x % 2][:, (kt - k0) * P:(kt - k0 + 1) * P], att[n % 3][:, kt * P:(kt + 1) * P], g.tile("ident"))
                    last.then_inc(s_tr, 1)

            def values(p, n):
                e, i = units[n]
                for x in of_unit[n]:
                    pe.wait_ge(s_tre[x % 2], p * (NG // 2) + (x // 2 + 2))
                for kt in range(i + 1):
                    last = pe.matmul(ops[HD * e:HD * e + HD, i * P:(i + 1) * P], vs[:, kt, HD * e:HD * e + HD],
                                     attT[n % 2][:, kt, :], start=(kt == 0), stop=(kt == i))
                last.then_inc(s_pv, 1)

            def before(p):
                return p - 1 if isinstance(p, int) else p + (-1)

            def pair(p, first, last):
                half(p, 0)
                if not first:
                    turn(before(p), LAST)
                    values(before(p), LAST - 1)
                half(p, 1)
                if not first:
                    values(before(p), LAST)
                scores(p, 0)
                scores(p, 1)
                half(p, 2)
                half(p, 3)
                pe.wait_ge(s_vs, p * 2 + 2)
                pe.wait_ge(s_olo, p + 1)
                for n in range(LAST):
                    if n + 2 < NU:
                        scores(p, n + 2)
                    turn(p, n)
                    if n >= 1:
                        values(p, n - 1)

            pairs(pe, pair)
            turn(PAIRS - 1, LAST)
            values(PAIRS - 1, LAST - 1)
            values(PAIRS - 1, LAST)

        def evacuate(eng, p, n, x):
            _, k0, k1 = groups[x]
            eng.wait_ge(s_tr, p * NG + x + 1)
            eng.wait_ge(s_pv, p * NU + max(n, 1))
            dst = attT[n % 2][:, k0:k1, :].rearrange("p a n -> p (a n)")
            src = trps[x % 2][:, 0:(k1 - k0) * P]
            if x % 2:
                eng.activation(dst, src, ACT.Copy).then_inc(s_tre[1], 1)
            else:
                eng.tensor_copy(dst, src).then_inc(s_tre[0], 1)

        @block.scalar
        def _(act):
            def sigmoids(p, n, first=False):
                e, i = units[n]
                nk = (i + 1) * P
                act.wait_ge(s_z, p * NU + n + 1)
                if n >= 3:
                    act.wait_ge(s_tr, p * NG + of_unit[n - 3][-1] + 1)
                    act.wait_ge(s_scan, p * NU + n - 2)
                elif not first:
                    act.wait_ge(s_tr, p * NG)
                act.activation(att[n % 3][:, 0:nk], zps[n % 2][:, 0:nk], ACT.Sigmoid, scale=HD ** -0.5)
                act.activation(rest[n % 3][:, 0:nk], zps[n % 2][:, 0:nk], ACT.Sigmoid, scale=-HD ** -0.5).then_inc(s_sig, 1)

            credit(act, [s_sig, s_tre[1]])
            for u in range(2):
                ws.split_hi(act, 0, u)

            def before(p):
                return p - 1 if isinstance(p, int) else p + (-1)

            def half(p, x):
                u, h = halves[x]
                if h == 0:
                    act.wait_ge(s_half, p * 2 + x + 1)
                else:
                    act.wait_ge(w_used[u], p + 2)
                at = slice(h * HALF, (h + 1) * HALF)
                act.activation(qk[u][:, at], zps[u][:, at], ACT.Copy).then_inc(s_qk, 1)

            def evacuated(p, n):
                for x in of_unit[n]:
                    if x % 2:
                        evacuate(act, p, n, x)

            def output(p):
                act.wait_ge(s_pv, p * NU + (NU + 1))
                act.activation(g.c_hi[:, ds(p + PAIRS, 1), :].rearrange("p a n -> p (a n)"), ops[:], ACT.Copy).then_inc(s_ohi, 1)

            def pair(p, first, last):
                half(p, 0)
                if not first:
                    evacuated(before(p), LAST)
                half(p, 1)
                if not first:
                    output(before(p))
                sigmoids(p, 0, first)
                sigmoids(p, 1, first)
                for x in (2, 3):
                    half(p, x)
                    if not last:
                        ws.split_hi(act, p + 1, halves[x][0])
                for n in range(LAST):
                    if n + 2 < NU:
                        sigmoids(p, n + 2, first)
                    evacuated(p, n)

            pairs(act, pair)
            evacuated(PAIRS - 1, LAST)
            output(PAIRS - 1)

        @block.vector
        def _(dve):
            for b in range(2):
                dve.memset(prod[b][:, SEQ:SEQ + 1], 1.0).then_inc(s_one, 1)
            dve.wait_ge(s_one, 2)
            credit(dve, ws.lo_ready + [s_tre[0], s_olo])
            for u in range(2):
                ws.cut_lo(dve, 0, u)

            def scan(p, n):
                e, i = units[n]
                nk = (i + 1) * P
                dve.wait_ge(s_sig, p * NU + n + 2)
                dve.wait_ge(s_att, p * NU + max(n, 1))
                m = rest[n % 3][:, 0:nk][:, ::-1]
                dve.tensor_tensor_scan(prod[n % 2][:, SEQ - nk:SEQ][:, ::-1], m, m, 1.0, ALU.mult, ALU.bypass).then_inc(s_scan, 1)

            def evacuated(p, n):
                for x in of_unit[n]:
                    if x % 2 == 0:
                        evacuate(dve, p, n, x)

            def output(p):
                dve.wait_ge(s_ohi, p + 1)
                dve.tensor_tensor(g.c_lo[:, ds(p + PAIRS, 1), :].rearrange("p a n -> p (a n)"), ops[:],
                                  g.c_hi[:, ds(p + PAIRS, 1), :].rearrange("p a n -> p (a n)"), ALU.subtract).then_inc(s_olo, 1)

            def pair(p, first, last):
                if not first:
                    p_ = p - 1 if isinstance(p, int) else p + (-1)
                    evacuated(p_, LAST)
                    output(p_)
                scan(p, 0)
                for n in range(LAST):
                    scan(p, n + 1)
                    evacuated(p, n)
                    if n < 2 and not last:
                        ws.cut_lo(dve, p + 1, 1 - n)

            pairs(dve, pair)
            evacuated(PAIRS - 1, LAST)
            output(PAIRS - 1)


def phase_recurrence(nc, g, a):
    with ExitStack() as es:
        sb = lambda n, s=(P, HALF), d=F32: es.enter_context(nc.sbuf_tensor(f"rec_{n}", list(s), d))
        sem = lambda n: nc.alloc_semaphore(f"rws_{n}")
        NB, NT, NC = 8, 4, 8
        wa_s, g_s = sb("wa_s", (P, P)), sb("g_s", (P, P))
        pc, pt = sb("pc", (P, 8)), sb("pt", (P, 2))
        th, zgs = g.z[:, NSH - 2, :], g.z[:, NSH - 1, :]
        sg, av, cum, eN, kkr, tmp, k2 = (sb(n) for n in "sg av cum eN kkr tmp k2".split())
        eE, eI = sg, cum
        ar = [sb(f"ar{f}", (P, NT, 2, P)) for f in range(2)]
        rk = [sb(f"rk{f}") for f in range(2)]
        wc = [sb(f"wc{f}", (P, NC)) for f in range(2)]
        bt, kt_, bh, kh, vt = (sb(n) for n in "bt kt bh kh vt".split())
        bn, kn, vn = (sb(n, (P, NT, P)) for n in "bn kn vn".split())
        rhs = sb("rhs", (P, NB, P))
        ma, mk = (t[:, PAIRS:KT, :].rearrange("p a n -> p (a n)").bitcast(F32).rearrange("p (b x n) -> p b x n", x=2, n=P)
                  for t in (g.c_hi, g.c_lo))
        X, T, TTr = sb("X", (P, NB, P)), sb("T", (P, NB, P)), sb("TT", (P, NB, P))
        gt, st, sbd = sb("gt", (P, NC, P)), sb("st", (P, NC + 1, HD)), sb("sbd", (P, NC, P))
        zt, ysb, yc = sb("zt"), sb("ysb"), sb("yc")
        M = [es.enter_context(nc.psum_tensor(f"rw_main{b}", [P, HALF], F32)) for b in range(4)]
        F = [es.enter_context(nc.psum_tensor(f"rw_front{b}", [P, HALF], F32)) for b in range(2)]
        T0, T1 = [es.enter_context(nc.psum_tensor(f"rw_tail{b}", [P, HALF], F32)) for b in range(2)]
        names = ("wa gs th zero pc pt lora sg a kkr sq ss rk cum cumE t k2 ssm rt rn kk kka eI eN eE wc AT RT VT BT KT BhT KhT "
                 "M1 M1e pair TT0 M2 M2e nat natE mv mvE T1 T1e X Xe TX T Tt Tte u ue nu wm tw pq Z ze G ge H Yl S0 S sbd ch Y "
                 "vw vhi vlo vmm vout ysb mean yc sqy var sd ri bo bv gm y1 y2 y3 y4 yhi ylo").split()
        s = {n: sem(n) for n in names}
        U, Um, Wm, PQ = rhs, T, X, rhs
        v_stage, v_hi, v_lo = value_weights(g)
        v = values(g)
        block = es.enter_context(nc.Block())
        c8 = lambda t: t[:].rearrange("p (c n) -> p c n", n=CH)
        c4 = lambda t: t[:].rearrange("p (j n) -> p j n", n=P)
        bank = lambda b: M[b][:].rearrange("p (j n) -> p j n", n=P)
        col = lambda n: pc[:, n:n + 1]
        W0, A0, KK, KA, RK, GG, GB, OMKA = range(8)

        def zs(off, t):
            tile = t.p + (off + t.dp) if not isinstance(t.p, int) else t.p + off + t.dp
            return g.z[:, ds(tile, 1), t.f * HALF:(t.f + 1) * HALF].rearrange("p a n -> p (a n)")

        def wait(eng, t, name, k=1, j=None):
            if t is not None:
                eng.wait_ge(s[name], t.count(k, k if j is None else j))

        run = lambda eng, *parts: turns(eng, PAIRS, *parts)

        @block.sync
        def _(sp):
            for p in range(PAIRS):
                cols = slice(p * P, (p + 1) * P)
                if p:
                    sp.wait_ge(s["lora"], 4 * p)
                sp.dma_start(wa_s[0:LORA_W, :], a["rw_w2"][0][:, cols]).then_inc(s["wa"], 16)
                sp.dma_start(wa_s[LORA_W:P, :], a["rw_a2"][0][:, cols]).then_inc(s["wa"], 16)
                if p:
                    sp.wait_ge(s["gm"], 2 * p)
                sp.dma_start(g_s[:], a["rw_g2"][0][:, cols]).then_inc(s["gs"], 16)
            sp.wait_ge(s["rk"], 2 * PAIRS)
            sp.wait_ge(s["RT"], 2 * PAIRS)
            sp.dma_start(v_stage, a["w_in"][0].rearrange("(k p) n -> p k n", p=P)[:, :, COL_V:COL_V + DR]).then_inc(s["vw"], 16)

        @block.gpsimd
        def _(pool):
            pool.memset(gt[:], 0.0).then_inc(s["zero"], 1)
            pool.memset(sbd[:], 0.0).then_inc(s["zero"], 1)

            def front(t, main):
                if t is None:
                    for kt in range(KT):
                        pool.wait_ge(s["vhi"], kt + 1)
                        pool.tensor_tensor(v_lo[:, kt, :], v_stage[:, kt, :], v_hi[:, kt, :], ALU.subtract).then_inc(s["vlo"], 1)
                    return
                wait(pool, main, "nat", 4)
                pool.tensor_copy(vt[:], zs(8, t)).then_inc(s["VT"], 1)
                wait(pool, t, "cum")
                pool.tensor_tensor(sg[:], cum[:], sg[:], ALU.subtract).then_inc(s["cumE"], 1)
                wait(pool, t, "eI")
                pool.tensor_tensor(ar[t.f][:, :, 1, :], zs(0, t).rearrange("p (j n) -> p j n", n=P), c4(eI), ALU.mult).then_inc(s["RT"], 1)

            def tail(t):
                if t is None:
                    return
                wait(pool, t, "yhi")
                out = lambda c: c[:, ds(t.p + t.dp, 1), t.f * HALF:(t.f + 1) * HALF].rearrange("p a n -> p (a n)")
                pool.tensor_tensor(out(g.c_lo), yc[:], out(g.c_hi), ALU.subtract).then_inc(s["ylo"], 1)

            def turn(t):
                front(t.after(), t)
                tail(t.before())

            run(pool, lambda t: front(t, None), turn, tail)

        @block.scalar
        def _(act):
            act.activation(th[0:LORA_W, :], th[0:LORA_W, :], ACT.Tanh).then_inc(s["th"], 1)
            act.activation(zgs, zgs, ACT.Sigmoid).then_inc(s["th"], 1)

            def front1(t):
                if t is None:
                    return
                wait(act, t.before(), "KhT")
                wait(act, t.before(), "RT")
                wait(act, t, "pc")
                wait(act, t, "lora", 2, 1)
                act.activation(sg[:], F[0][:], ACT.Sigmoid, bias=col(W0)).then_inc(s["sg"], 1)
                wait(act, t, "lora", 2)
                act.activation(av[:], F[1][:], ACT.Sigmoid, bias=col(A0)).then_inc(s["a"], 1)

            def front2(t):
                if t is None:
                    return
                wait(act, t, "cum")
                act.activation(eN[:], cum[:], ACT.Exp, scale=DECAY).then_inc(s["eN"], 1)
                wait(act, t, "cumE")
                act.activation(eE[:], sg[:], ACT.Exp, scale=-DECAY).then_inc(s["eE"], 1)
                wait(act, t, "eN")
                act.activation(eI[:], cum[:], ACT.Exp, scale=-DECAY).then_inc(s["eI"], 1)

            def front3(t):
                if t is None:
                    act.wait_ge(s["vw"], 16)
                    for kt in range(KT):
                        act.activation(v_hi[:, kt, :], v_stage[:, kt, :], ACT.Copy).then_inc(s["vhi"], 1)
                    return
                wait(act, t, "ssm")
                act.activation(tmp[:], tmp[:], ACT.Sqrt).then_inc(s["rt"], 1)

            def tail1(t):
                if t is None:
                    return
                wait(act, t, "S", NC)
                for e in range(2):
                    r = slice(HD * e, HD * e + HD)
                    act.activation(sbd[r, :, r], st[r, 0:NC, :], ACT.Copy).then_inc(s["sbd"], 1)

            def tail2(t):
                if t is None:
                    return
                wait(act, t.before(), "yhi")
                wait(act, t, "Y")
                act.activation(ysb[:], T1[:], ACT.Copy).then_inc(s["ysb"], 1)

            def tail3(t):
                if t is not None:
                    wait(act, t, "yc")
                    act.activation(ysb[:], yc[:], ACT.Square).then_inc(s["sqy"], 1)

            def tail4(t):
                if t is not None:
                    wait(act, t, "var")
                    act.activation(ysb[:], T0[:], ACT.Sqrt, bias=g.misc(4), scale=1.0 / HD).then_inc(s["sd"], 1)

            def tail5(t):
                if t is not None:
                    wait(act, t, "y4")
                    act.activation(g.c_hi[:, ds(t.p + t.dp, 1), t.f * HALF:(t.f + 1) * HALF].rearrange("p a n -> p (a n)"),
                                   yc[:], ACT.Copy).then_inc(s["yhi"], 1)

            def level(t, lv):
                for h in range(2):
                    wait(act, t, "Tt", 8, 2 * lv + h + 1)
                    act.activation(TTr[:, 4 * h:4 * h + 4, :], bank(h), ACT.Copy).then_inc(s["Tte"], 1)

            def turn(t):
                last, nxt = t.before(), t.after()
                for h in range(2):
                    wait(act, t, "T1", 2, h + 1)
                    act.activation(T[:, 4 * h:4 * h + 4, :], bank(h), ACT.Copy).then_inc(s["T1e"], 1)
                wait(act, t, "nat", 4, 1)
                act.activation(rhs[:].rearrange("p (e j) n -> p e j n", e=2)[:, :, :, 0:HD],
                               M[2][:].rearrange("p (j e n) -> p e j n", e=2, n=HD), ACT.Copy).then_inc(s["natE"], 1)
                for x, (b, dst) in enumerate(((3, bn), (0, kn), (1, vn))):
                    wait(act, t, "nat", 4, x + 2)
                    act.activation(dst[:].rearrange("p j n -> p (j n)"), M[b][:], ACT.Copy).then_inc(s["natE"], 1)
                tail1(last)
                wait(act, t, "mv")
                act.activation(rhs[:, :, HD:P], M[2][:].rearrange("p (b n) -> p b n", n=HD), ACT.Copy).then_inc(s["mvE"], 1)
                front1(nxt)
                tail2(last)
                level(t, 0)
                tail3(last)
                front2(nxt)
                level(t, 1)
                tail4(last)
                front3(nxt)
                level(t, 2)
                level(t, 3)
                for h in range(2):
                    wait(act, t, "u", 2, h + 1)
                    act.activation(U[:, 4 * h:4 * h + 4, :], bank(h), ACT.Copy).then_inc(s["ue"], 1)
                    act.activation(Um[:, 4 * h:4 * h + 4, :], bank(h), ACT.Copy, scale=g.misc(0)).then_inc(s["ue"], 1)
                for h in range(2):
                    wait(act, t, "nu", 2, h + 1)
                    act.activation(Wm[:, 4 * h:4 * h + 4, :], bank(2 + h), ACT.Copy, scale=g.misc(1)).then_inc(s["wm"], 1)
                tail5(last)
                for h in range(2):
                    wait(act, t, "G", 2, h + 1)
                    for e in range(2):
                        r = slice(HD * e, HD * e + HD)
                        act.activation(gt[r, h::2, r], M[3 - 2 * h][r, 0:4 * HD].rearrange("p (j n) -> p j n", n=HD), ACT.Copy).then_inc(s["ge"], 1)

            def prologue(t):
                act.wait_ge(s["th"], 2)
                front1(t)
                front2(t)
                front3(t)

            def epilogue(t):
                for tt in range(TT):
                    if 2 <= tt < 7:
                        (tail1, tail2, tail3, tail4, tail5)[tt - 2](t)
                    act.wait_ge(s["vmm"], tt + 1)
                    act.activation(v[tt // 4][:, :, tt % 4 * P:tt % 4 * P + P], M[tt % 4][:].rearrange("p (a n) -> p a n", n=P),
                                   ACT.Copy).then_inc(s["vout"], 1)

            run(act, prologue, turn, epilogue)

        @block.vector
        def _(dve):
            at = ROWS["w0"][0]

            def front1(t):
                if t is None:
                    return
                wait(dve, t.before(), "KhT")
                wait(dve, t.before(), "RT")
                dve.tensor_scalar(pc[:], g.cols[:, ds((t.p + t.dp) * 8 + at, 8)], 1.0, None, ALU.mult).then_inc(s["pc"], 1)
                wait(dve, t, "pc")
                dve.tensor_scalar(kkr[:], zs(4, t), col(KK), None, ALU.mult).then_inc(s["kkr"], 1)
                wait(dve, t, "kkr")
                dve.tensor_tensor(tmp[:], kkr[:], kkr[:], ALU.mult).then_inc(s["sq"], 1)

            def front2(t):
                if t is None:
                    return
                wait(dve, t, "sg")
                dve.tensor_tensor_scan(cum[:], g.reset[:], sg[:], 0.0, ALU.mult, ALU.add).then_inc(s["cum"], 1)
                wait(dve, t, "a")
                dve.tensor_scalar(k2[:], av[:], col(KA), col(OMKA), ALU.mult, ALU.add).then_inc(s["t"], 1)
                wait(dve, t, "ss")
                dve.tensor_scalar(tmp[:], F[0][:], 1e-24, None, ALU.max).then_inc(s["ssm"], 1)
                wait(dve, t, "t")
                dve.tensor_tensor(k2[:], k2[:], zs(4, t), ALU.mult).then_inc(s["k2"], 1)

            def front3(t):
                if t is None:
                    return
                wait(dve, t, "rt")
                dve.reciprocal(tmp[:], tmp[:]).then_inc(s["rn"], 1)
                wait(dve, t, "rn")
                dve.tensor_tensor(kkr[:], kkr[:], tmp[:], ALU.mult).then_inc(s["kk"], 1)

            def front4(t):
                if t is None:
                    return
                wait(dve, t, "kk")
                dve.tensor_tensor(tmp[:], kkr[:], av[:], ALU.mult).then_inc(s["kka"], 1)
                wait(dve, t, "kka")
                wait(dve, t, "eN")
                dve.tensor_tensor(bt[:], tmp[:], eN[:], ALU.mult).then_inc(s["BT"], 1)
                wait(dve, t, "eE")
                dve.scalar_tensor_tensor(ar[t.f][:, :, 0, :], c4(kkr), -1.0, c4(eE), ALU.mult, ALU.mult).then_inc(s["AT"], 1)
                wait(dve, t, "k2")
                dve.tensor_tensor(kt_[:], k2[:], eN[:], ALU.mult).then_inc(s["KT"], 1)
                wait(dve, t, "eI")
                dve.tensor_copy(wc[t.f][:], eI[:, CH - 1::CH]).then_inc(s["wc"], 1)

            def front5(t):
                dve.scalar_tensor_tensor(rk[t.f][:], zs(0, t), col(RK), k2[:], ALU.mult, ALU.mult).then_inc(s["rk"], 1)
                wait(dve, t, "wc")
                wcb = wc[t.f][:].unsqueeze(2).to_broadcast([P, NC, CH])
                dve.tensor_tensor(c8(bh), c8(bt), wcb, ALU.mult).then_inc(s["BhT"], 1)
                dve.tensor_tensor(c8(kh), c8(kt_), wcb, ALU.mult).then_inc(s["KhT"], 1)

            def chain0(t):
                if t is None:
                    return
                wait(dve, t.before(), "sbd", 2)
                if t.f:
                    dve.tensor_copy(st[:, 0, :], st[:, NC, :]).then_inc(s["S0"], 1)
                else:
                    dve.memset(st[:, 0, :], 0.0).then_inc(s["S0"], 1)
                wait(dve, t, "S0")

            def chain(t, c):
                if t is None:
                    return
                wait(dve, t, "ch", NC, c + 1)
                dve.scalar_tensor_tensor(st[:, c + 1, :], st[:, c, :], wc[t.f][:, c:c + 1], T0[:, c * HD:(c + 1) * HD],
                                         ALU.mult, ALU.add).then_inc(s["S"], 1)

            def tail1(t):
                if t is None:
                    return
                wait(dve, t.before(), "y2")
                dve.tensor_scalar(pt[:], g.cols[:, ds((t.p + t.dp) * 8 + (at + GG), 2)], 1.0, None, ALU.mult).then_inc(s["pt"], 1)
                wait(dve, t.before(), "ylo")
                wait(dve, t, "mean")
                dve.scalar_tensor_tensor(yc[:], T0[:], -1.0 / HD, ysb[:], ALU.mult, ALU.add).then_inc(s["yc"], 1)

            def tail2(t):
                if t is None:
                    return
                wait(dve, t, "bo")
                dve.tensor_tensor(rk[t.f][:], T1[:], zs(8, t), ALU.mult).then_inc(s["bv"], 1)

            def tail3(t):
                if t is None:
                    return
                wait(dve, t, "sd")
                dve.reciprocal(ysb[:], ysb[:]).then_inc(s["ri"], 1)
                wait(dve, t, "ri")
                dve.tensor_tensor(yc[:], yc[:], ysb[:], ALU.mult).then_inc(s["y1"], 1)
                wait(dve, t, "y1")
                wait(dve, t, "pt")
                dve.tensor_scalar(yc[:], yc[:], pt[:, 0:1], pt[:, 1:2], ALU.mult, ALU.add).then_inc(s["y2"], 1)

            def tail4(t):
                if t is None:
                    return
                wait(dve, t, "y2")
                wait(dve, t, "bv")
                dve.tensor_tensor(yc[:], yc[:], rk[t.f][:], ALU.add).then_inc(s["y3"], 1)
                wait(dve, t, "y3")
                wait(dve, t, "gm")
                dve.tensor_tensor(yc[:], yc[:], T1[:], ALU.mult).then_inc(s["y4"], 1)

            full = lambda n, w: g.tile(n).unsqueeze(1).to_broadcast([P, w, P])
            masks = g.const[:, CT["strictT"]:CT["strictT"] + 2, :].unsqueeze(1).to_broadcast([P, 2, 2, P])

            def masked(t, x, src, dst, done):
                blk = 4 * (x % 2) + 2 * (x // 2)
                wait(dve, t, src, 4, x + 1)
                dve.tensor_tensor(dst[:, blk:blk + 2, :, :], M[x][:].rearrange("p (j x n) -> p j x n", x=2, n=P), masks, ALU.mult).then_inc(s[done], 1)

            def turn(t):
                last, nxt = t.before(), t.after()
                chain0(last)
                for x in range(4):
                    masked(t, x, "M1", ma, "M1e")
                    chain(last, x)
                wait(dve, t, "M1e", 4)
                dve.tensor_tensor(TTr[:], ma[:, :, 0, :], full("pairT", NB), ALU.mult).then_inc(s["pair"], 1)
                masked(t, 0, "M2", mk, "M2e")
                chain(last, 4)
                wait(dve, t, "pair")
                dve.tensor_tensor(TTr[:], TTr[:], full("ident", NB), ALU.add).then_inc(s["TT0"], 1)
                front5(t)
                for x in range(1, 4):
                    masked(t, x, "M2", mk, "M2e")
                    chain(last, 4 + x)
                front1(nxt)
                for lv, size in enumerate(LEVELS):
                    for h in range(2):
                        wait(dve, t, "X", 8, 2 * lv + h + 1)
                        dve.tensor_tensor(X[:, 4 * h:4 * h + 4, :], bank(h), full(f"m{size}", 4), ALU.mult).then_inc(s["Xe"], 1)
                    if lv < 2:
                        (tail1, tail2)[lv](last)
                    for h in range(2):
                        wait(dve, t, "TX", 8, 2 * lv + h + 1)
                        dve.tensor_tensor(T[:, 4 * h:4 * h + 4, :], bank(2 + h), T[:, 4 * h:4 * h + 4, :], ALU.add).then_inc(s["T"], 1)
                    if lv == 0:
                        front2(nxt)
                tail3(last)
                tail4(last)
                for h in range(2):
                    wait(dve, t, "tw", 2, h + 1)
                    dve.tensor_tensor(PQ[:, 4 * h:4 * h + 4, :], bank(h), U[:, 4 * h:4 * h + 4, :], ALU.add).then_inc(s["pq"], 1)
                wait(dve, t, "Z")
                dve.tensor_tensor(c4(zt), bank(2), ar[t.f][:, :, 1, :], ALU.add).then_inc(s["ze"], 1)
                front3(nxt)
                front4(nxt)

            def prologue(t):
                front1(t)
                front2(t)
                front3(t)
                front4(t)

            def epilogue(t):
                chain0(t)
                for c in range(NC):
                    chain(t, c)
                for part in (tail1, tail2, tail3, tail4):
                    part(t)

            run(dve, prologue, turn, epilogue)

        @block.tensor
        def _(pe):
            ident, bones = g.tile("ident"), g.tile("bones")

            def lora(t):
                if t is None:
                    return
                tok = slice(t.f * HALF, (t.f + 1) * HALF)
                if not t.f:
                    pe.wait_ge(s["wa"], (t.p + t.dp) * 32 + 32)
                wait(pe, t.before(), "ssm")
                wait(pe, t.before(), "a")
                pe.matmul(F[0][:], wa_s[0:LORA_W, :], th[0:LORA_W, tok], start=True, stop=True).then_inc(s["lora"], 1)
                pe.matmul(F[1][:], wa_s[LORA_W:P, :], th[LORA_W:P, tok], start=True, stop=True).then_inc(s["lora"], 1)

            def squares(t):
                if t is None:
                    return
                wait(pe, t, "sq")
                wait(pe, t, "sg")
                pe.matmul(F[0][:], bones, tmp[:], start=True, stop=True).then_inc(s["ss"], 1)

            def chain(t, c):
                if t is None:
                    return
                if c == 0:
                    wait(pe, t, "S0")
                    wait(pe, t, "ge", 4)
                else:
                    wait(pe, t, "S", NC, c)
                pe.matmul(T0[:, c * HD:(c + 1) * HD], gt[:, c, :], st[:, c, :], start=False, stop=True, skip_group_check=True).then_inc(s["ch"], 1)

            def outputs(t):
                if t is None:
                    return
                wait(pe, t, "sbd", 2)
                wait(pe, t, "ze")
                for c in range(NC):
                    last = pe.matmul(T1[:, c * CH:(c + 1) * CH], sbd[:, c, :], zt[:, c * CH:(c + 1) * CH], start=False, stop=True,
                                     skip_group_check=True)
                last.then_inc(s["Y"], 1)

            def mean(t):
                if t is not None:
                    wait(pe, t, "ysb")
                    pe.matmul(T0[:], bones, ysb[:], start=True, stop=True).then_inc(s["mean"], 1)

            def bonus(t):
                if t is not None:
                    wait(pe, t, "rk")
                    pe.matmul(T1[:], bones, rk[t.f][:], start=True, stop=True).then_inc(s["bo"], 1)

            def variance(t):
                if t is not None:
                    wait(pe, t, "sqy")
                    pe.matmul(T0[:], bones, ysb[:], start=True, stop=True).then_inc(s["var"], 1)

            def gate(t):
                if t is None:
                    return
                if not t.f:
                    pe.wait_ge(s["gs"], (t.p + t.dp) * 16 + 16)
                wait(pe, t, "bv")
                pe.matmul(T1[:], g_s[:], zgs[:, t.f * HALF:(t.f + 1) * HALF], start=True, stop=True).then_inc(s["gm"], 1)

            def product(left, right, b0, done):
                def half(h):
                    for b in range(4):
                        last = pe.matmul(M[b0 + h][:, b * P:(b + 1) * P], left(4 * h + b), right(4 * h + b), start=True, stop=True)
                    last.then_inc(s[done], 1)
                return half

            nT = lambda b: ma[:, b, 0, :]
            blk = lambda t: lambda b: t[:, b, :]
            jobs = [(jp, e) for jp in range(2) for e in range(2)]

            def turn(t):
                last, nxt = t.before(), t.after()
                art = ar[t.f]
                for n in ("BT", "AT", "RT"):
                    wait(pe, t, n)
                for left, n, done in ((bt, 0, "M1"), (kt_, 4, "M2")):
                    for x, (jp, e) in enumerate(jobs):
                        rows = slice(HD * e, HD * e + HD)
                        if n:
                            if x == 0:
                                wait(pe, t, "KT")
                            wait(pe, t, "M1e", 4, x + 1)
                        elif x == 1:
                            wait(pe, last, "ge", 4)
                        elif x == 2:
                            wait(pe, last, "ze")
                        for j in (2 * jp, 2 * jp + 1):
                            mm = pe.matmul(M[x][:, (j % 2) * 2 * P:(j % 2 + 1) * 2 * P], left[rows, j * P:(j + 1) * P],
                                           art[rows, j, :, :].rearrange("p x n -> p (x n)"), start=True, stop=True)
                        mm.then_inc(s[done], 1)
                        chain(last, n + x)
                wait(pe, t, "TT0")
                for h in range(2):
                    wait(pe, t, "M2e", 4, h + 1)
                    for b in range(4):
                        mm = pe.transpose(M[h][:, b * P:(b + 1) * P], TTr[:, 4 * h + b, :], ident)
                    mm.then_inc(s["T1"], 1)
                wait(pe, t, "M2e", 4)
                for x, (src, n, b) in enumerate(((None, "AT", 2), (bh, "BhT", 3), (kh, "KhT", 0), (vt, "VT", 1))):
                    wait(pe, t, n)
                    if b < 2:
                        wait(pe, t, "T1e", 2, b + 1)
                    for j in range(NT):
                        mm = pe.transpose(M[b][:, j * P:(j + 1) * P], art[:, j, 0, :] if src is None else src[:, j * P:(j + 1) * P], ident)
                    mm.then_inc(s["nat"], 1)
                lora(nxt)
                wait(pe, t, "natE", 4)
                for b in range(NB):
                    mm = pe.matmul(M[2][:, b * HD:(b + 1) * HD], mk[:, b, 0, :], vn[:, b % 4, HD * (b // 4):HD * (b // 4) + HD],
                                   start=True, stop=True)
                mm.then_inc(s["mv"], 1)
                outputs(last)
                for lv in range(len(LEVELS)):
                    x = product(nT, blk(T), 0, "X")
                    for h in range(2):
                        if lv:
                            wait(pe, t, "T", 8, 2 * lv - 1 + h)
                            wait(pe, t, "Tte", 8, 2 * lv - 1 + h)
                        x(h)
                    if lv == 0:
                        mean(last)
                        squares(nxt)
                        wait(pe, t, "mvE")
                    if lv == 1:
                        bonus(last)
                    if lv == 2:
                        variance(last)
                    if lv == 3:
                        gate(last)
                    x = product(blk(TTr), blk(X), 2, "TX")
                    for h in range(2):
                        wait(pe, t, "Xe", 8, 2 * lv + h + 1)
                        x(h)
                    for h in range(2):
                        wait(pe, t, "T", 8, 2 * lv + h + 1)
                        for b in range(4):
                            mm = pe.transpose(M[h][:, b * P:(b + 1) * P], T[:, 4 * h + b, :], ident)
                        mm.then_inc(s["Tt"], 1)
                x = product(blk(TTr), blk(rhs), 0, "u")
                for h in range(2):
                    wait(pe, t, "Tte", 8, 7 + h)
                    x(h)
                x = product(nT, blk(Um), 2, "nu")
                for h in range(2):
                    wait(pe, t, "ue", 4, 2 * h + 2)
                    x(h)
                x = product(blk(TTr), blk(Wm), 0, "tw")
                for h in range(2):
                    wait(pe, t, "wm", 2, h + 1)
                    x(h)
                wait(pe, t, "pq", 2)
                wait(pe, last, "sd")
                wait(pe, last, "y4")
                for b in range(NB):
                    e, j = b // 4, b % 4
                    mm = pe.matmul(M[2][HD * e:HD * e + HD, j * P:(j + 1) * P], PQ[:, b, 0:HD], ma[:, b, 1, :], start=True, stop=True)
                mm.then_inc(s["Z"], 1)
                for h in range(2):
                    rows = slice(CH * h, CH * h + CH)
                    for b in range(NB):
                        e, j = b // 4, b % 4
                        r = slice(HD * e, HD * e + HD)
                        mm = pe.matmul(M[3 - 2 * h][r, j * HD:(j + 1) * HD], PQ[rows, b, 0:HD], bn[rows, j, r], start=True, stop=True)
                    mm.then_inc(s["G"], 1)
                    for b in range(NB):
                        e, j = b // 4, b % 4
                        r = slice(HD * e, HD * e + HD)
                        o = T0[r, (2 * j + h) * HD:(2 * j + h + 1) * HD]
                        pe.matmul(o, bn[rows, j, r], PQ[rows, b, HD:P], start=(j == 0 and h == 0), stop=False, skip_group_check=True)
                        mm = pe.matmul(o, kn[rows, j, r], vn[rows, j, r], start=False, stop=False, skip_group_check=True)
                    if h == 0:
                        mm.then_inc(s["H"], 1)
                    for b in range(4 * h, 4 * h + 4):
                        e, j = b // 4, b % 4
                        r = slice(HD * e, HD * e + HD)
                        o = T1[r, j * P:(j + 1) * P]
                        pe.matmul(o, PQ[:, b, HD:P], ma[:, b, 1, :], start=(j == 0), stop=False, skip_group_check=True)
                        if b == 3:
                            wait(pe, t, "H")
                        pe.matmul(o, vn[:, j, r], mk[:, b, 1, :], start=False, stop=False, skip_group_check=True)

            def prologue(t):
                pe.wait_ge(s["th"], 2)
                pe.wait_ge(s["zero"], 2)
                lora(t)
                squares(t)

            def epilogue(t):
                pe.wait_ge(s["vlo"], KT)
                wait(pe, t, "ge", 4)
                wait(pe, t, "ze")
                steps = {n: (lambda n=n: chain(t, n)) for n in range(NC)}
                for n, part in zip((8, 10, 11, 13, 15), (outputs, mean, bonus, variance, gate)):
                    steps[n] = lambda part=part: part(t)
                for tt in range(TT):
                    if tt >= 4:
                        pe.wait_ge(s["vout"], tt - 3)
                    for third in range(3):
                        if 3 * tt + third in steps:
                            steps[3 * tt + third]()
                        for n in range(KT * third, KT * third + KT):
                            kt, (act_part, w_part) = n // 3, ((g.a_hi, v_hi), (g.a_hi, v_lo), (g.a_lo, v_hi))[n % 3]
                            mm = pe.matmul(M[tt % 4][:], act_part[:, kt, tt * P:(tt + 1) * P], w_part[:, kt, :],
                                           start=(n == 0), stop=(n == 3 * KT - 1))
                    mm.then_inc(s["vmm"], 1)

            run(pe, prologue, turn, epilogue)


def phase_merge(nc, g, a):
    with ExitStack() as es:
        sb = lambda n, s, d=F32: es.enter_context(nc.sbuf_tensor(f"mg_{n}", s, d))
        sem = lambda n: nc.alloc_semaphore(f"mgs_{n}")
        w = a["w_in"][0].rearrange("(k p) n -> p k n", p=P)
        wa = a["w_branch_a"][0].rearrange("(k p) n -> p k n", p=P)
        wb = a["w_branch_b"][0].rearrange("(k p) n -> p k n", p=P)
        w_used = [sem(f"used{u}") for u in range(3)]
        s_ya, s_sa, s_sb, s_pa, s_pb, s_m, s_hi, s_lo = (sem(n) for n in "ya sa sb pa pb m hi lo".split())
        ga, gb, m = sb("ga", [P, SEQ]), sb("gb", [P, SEQ]), sb("m", [P, SEQ])
        ps = [es.enter_context(nc.psum_tensor(f"mg_ps{u}", [P, SEQ], F32)) for u in range(4)]

        def source(u, i):
            if u < 2:
                return [(slice(0, KT), w[:, :, ds(i + (COL_GA, COL_GB)[u], P)])]
            return [(slice(0, PAIRS), wa[:, :, ds(i, P)]), (slice(PAIRS, KT), wb[:, :, ds(i, P)])]

        ws = split_stream(es, nc, "mg", KT, 3, source, w_used)
        block = es.enter_context(nc.Block())

        @block.sync
        def _(sp):
            ws.load(sp)
            sp.dma_start(g.x1[:], a["w_out"][0].rearrange("(k p) n -> p k n", p=P)).then_inc(g.s_wout, 16)

        @block.gpsimd
        def _(pool):
            credit(pool, ws.lo_ready + [s_lo])
            for u in range(3):
                ws.cut_lo(pool, 0, u)

            def finish(i):
                pool.wait_ge(s_hi, i + 1)
                pool.tensor_tensor(g.b_lo[:, ds(i, 1), :].rearrange("p a n -> p (a n)"), m[:],
                                   g.b_hi[:, ds(i, 1), :].rearrange("p a n -> p (a n)"), ALU.subtract).then_inc(s_lo, 1)

            with pool.Fori(0, KT - 1) as i:
                for u in range(3):
                    ws.cut_lo(pool, i + 1, u)
                finish(i)
            finish(KT - 1)

        @block.tensor
        def _(pe):
            credit(pe, w_used)
            with pe.Fori(0, KT) as i:
                for u in range(2):
                    pe.wait_ge(ws.lo_ready[u], i + 2)
                    pe.wait_ge((s_sa, s_sb)[u], i + 1)
                    gemm_rows(pe, ps[u], ws.hi[u], ws.lo[u], g.a_hi, g.a_lo, range(KT), range(KT)).then_inc(w_used[u], 1)
                pe.wait_ge(ws.lo_ready[2], i + 2)
                pe.wait_ge(s_pa, i + 1)
                gemm_rows(pe, ps[2], ws.hi[2], ws.lo[2], g.c_hi, g.c_lo, range(PAIRS), range(PAIRS)).then_inc(s_ya, 1)
                pe.wait_ge(s_pb, i + 1)
                gemm_rows(pe, ps[3], ws.hi[2], ws.lo[2], g.c_hi, g.c_lo, range(PAIRS, KT), range(PAIRS, KT)).then_inc(w_used[2], 1)

        @block.scalar
        def _(act):
            credit(act, [s_sa, s_sb])
            for u in range(3):
                ws.split_hi(act, 0, u)

            def step(i, last):
                for u, (gate, ready, free) in enumerate(((ga, s_sa, s_pa), (gb, s_sb, s_pb))):
                    act.wait_ge(w_used[u], i + 2)
                    act.wait_ge(free, i + 1)
                    act.activation(gate[:], ps[u][:], ACT.Sigmoid).then_inc(ready, 1)
                    if not last:
                        ws.split_hi(act, i + 1, u)
                act.wait_ge(s_m, i + 1)
                act.activation(g.b_hi[:, ds(i, 1), :].rearrange("p a n -> p (a n)"), m[:], ACT.Copy).then_inc(s_hi, 1)
                if not last:
                    ws.split_hi(act, i + 1, 2)

            with act.Fori(0, KT - 1) as i:
                step(i, False)
            step(KT - 1, True)

        @block.vector
        def _(dve):
            credit(dve, [s_pa, s_pb])
            with dve.Fori(0, KT) as i:
                dve.wait_ge(s_sa, i + 2)
                dve.wait_ge(s_ya, i + 1)
                dve.tensor_tensor(ga[:], ga[:], ps[2][:], ALU.mult).then_inc(s_pa, 1)
                dve.wait_ge(s_sb, i + 2)
                dve.wait_ge(w_used[2], i + 2)
                dve.tensor_tensor(gb[:], gb[:], ps[3][:], ALU.mult).then_inc(s_pb, 1)
                dve.wait_ge(s_pb, i + 2)
                dve.wait_ge(s_pa, i + 2)
                dve.wait_ge(s_lo, i + 1)
                dve.tensor_tensor(m[:], ga[:], gb[:], ALU.add).then_inc(s_m, 1)


def gate_rows(es, nc, g):
    diag = [es.enter_context(nc.sbuf_tensor(f"gr_diag{u}", [P, CPH, P], F32)) for u in range(2)]
    ps = [es.enter_context(nc.psum_tensor(f"gr_ps{u}", [P, HALF], F32)) for u in range(2)]
    s_diag, s_mm, s_row = (nc.alloc_semaphore(f"gr_{n}") for n in "diag mm row".split())
    jobs = [(g.g1, "g1", 0), (g.g1, "g1", 1), (g.g2, "g2", 0), (g.g2, "g2", 1)]

    def diagonals(dve):
        for x, (_, name, h) in enumerate(jobs):
            if x >= 2:
                dve.wait_ge(s_mm, x - 1)
            at = ADA[name] + CPH * h
            dve.tensor_tensor(diag[x % 2][:], g.tile("ident").unsqueeze(1).to_broadcast([P, CPH, P]),
                              g.ada[:, at:at + CPH].unsqueeze(2).to_broadcast([P, CPH, P]), ALU.mult).then_inc(s_diag, 1)

    def spread(pe):
        for x in range(len(jobs)):
            pe.wait_ge(s_diag, x + 1)
            if x >= 2:
                pe.wait_ge(s_row, x - 1)
            pe.matmul(ps[x % 2][:], g.ones[:], diag[x % 2][:].rearrange("p a n -> p (a n)"), start=True, stop=True).then_inc(s_mm, 1)

    def store(act):
        for x, (dst, _, h) in enumerate(jobs):
            act.wait_ge(s_mm, x + 1)
            act.activation(dst[:, h * HALF:(h + 1) * HALF], ps[x % 2][:], ACT.Copy).then_inc(s_row, 1)

    return diagonals, spread, store, (s_row, len(jobs))


def phase_out(nc, g, a):
    with ExitStack() as es:
        sb = lambda n, s=(P, D), d=F32: es.enter_context(nc.sbuf_tensor(f"ou_{n}", list(s), d))
        psum = lambda n: es.enter_context(nc.psum_tensor(f"ou_{n}", [P, D], F32))
        names = "seen vec brow mm gm y s1 v1 sd1 r1 n1 gain bias keep s2 v2 sd2 r2 n2 turn hf hi lo whi wlo".split()
        s = {n: nc.alloc_semaphore(f"ous_{n}") for n in names}
        s_x = [nc.alloc_semaphore(f"ous_x{u}") for u in range(2)]
        xt, y, yn = ([sb(f"{n}{u}") for u in range(2)] for n in ("x", "y", "yn"))
        hf = sb("hf", (P, KT, P))
        vec = sb("vec", (P, 3, D))
        st = [sb(f"st{x}", (P, 2, 6)) for x in range(2)]
        mv = [[sb(f"mv{x}{u}", (P, 2)) for u in range(2)] for x in range(2)]
        rs = [[sb(f"rs{x}{u}", (P, 2)) for u in range(2)] for x in range(2)]
        ps, turned = [psum(f"ps{u}") for u in range(2)], psum("turned")
        diagonals, spread, store, (s_row, rows) = gate_rows(es, nc, g)
        block = es.enter_context(nc.Block())
        whi, wlo = g.c_hi, g.c_lo
        row = lambda t: t.p * (2 * P) + (2 * t.dp + t.f) * P
        tok = lambda t: ds(row(t), P)
        tile = lambda t: g.x1[:, ds(t.p * 2 + (2 * t.dp + t.f), 1), :].rearrange("p a n -> p (a n)")

        def wait(eng, t, name, k=1, j=None):
            if t is not None:
                eng.wait_ge(s[name], t.count(k, k if j is None else j))

        def low(eng, t):
            if t is not None:
                wait(eng, t, "hi")
                eng.tensor_tensor(g.a_lo[:, :, tok(t)], hf[:], g.a_hi[:, :, tok(t)], ALU.subtract).then_inc(s["lo"], 1)

        two = lambda t: t and t.before() and t.before().before()
        run = lambda eng, turn, epilogue: turns(eng, TT // 2, lambda t: None, turn, epilogue)

        @block.sync
        def _(sp):
            for v, src in enumerate((a["ln1_g"][0], a["ln1_b"][0], a["b_ff2"][0])):
                sp.dma_start(vec[:, v, :], src.partition_broadcast(P)).then_inc(s["vec"], 16)

            def turn(t):
                wait(sp, two(t), "y", 2)
                sp.dma_start(xt[t.f][:], a["x"][0][tok(t), :]).then_inc(s_x[t.f], 16)

            run(sp, turn, lambda t: None)
            for u in range(2):
                g.ff.load(sp, 0, u, u * P)

        @block.scalar
        def _(act):
            act.wait_ge(g.s_wout, 16)
            for kt in range(KT):
                act.activation(whi[:, kt, :], g.x1[:, kt, :], ACT.Copy).then_inc(s["whi"], 1)
            store(act)

            def piece(t):
                if t is None:
                    return
                wait(act, t, "turn")
                wait(act, t.before(), "lo")
                for kt in range(KT):
                    act.activation(hf[:, kt, :], turned[:, kt * P:(kt + 1) * P], ACT.Identity,
                                   bias=g.ada[:, ADA["sh2"] + kt:ADA["sh2"] + kt + 1],
                                   scale=g.ada[:, ADA["sc2"] + kt:ADA["sc2"] + kt + 1]).then_inc(s["hf"], 1)
                wait(act, t, "hf", KT)
                act.activation(g.a_hi[:, :, tok(t)], hf[:], ACT.Copy).then_inc(s["hi"], 1)

            def second(t):
                wait(act, t, "r2", 2)
                wait(act, two(t), "turn")
                act.activation(yn[t.f][:], y[t.f][:], ACT.Identity, bias=rs[1][t.f][:, 1:2], scale=rs[1][t.f][:, 0:1]).then_inc(s["n2"], 1)

            def root(t, x):
                wait(act, t, ("v1", "v2")[x])
                act.activation(rs[x][t.f][:, 0:1], mv[x][t.f][:, 1:2], ACT.Sqrt, bias=g.misc((3, 2)[x])).then_inc(s[("sd1", "sd2")[x]], 1)

            def turn(t):
                piece(two(t))
                root(t, 0)
                wait(act, t, "r1", 2)
                act.activation(y[t.f][:], y[t.f][:], ACT.Identity, bias=rs[0][t.f][:, 1:2], scale=rs[0][t.f][:, 0:1]).then_inc(s["n1"], 1)
                if t.after() is None:
                    piece(t.before())
                root(t, 1)
                second(t)

            def epilogue(t):
                for u in range(2):
                    g.ff.split_hi(act, 0, u)
                piece(t)

            run(act, turn, epilogue)

        @block.gpsimd
        def _(pool):
            credit(pool, g.ff.lo_ready)
            for kt in range(0, KT, 3):
                pool.wait_ge(s["whi"], kt + 1)
                pool.tensor_tensor(wlo[:, kt, :], g.x1[:, kt, :], whi[:, kt, :], ALU.subtract).then_inc(s["wlo"], 1)

            def turn(t):
                low(pool, two(t))

            def epilogue(t):
                low(pool, t.before())
                for u in range(2):
                    g.ff.split_lo(pool, 0, u)

            run(pool, turn, epilogue)

        @block.vector
        def _(dve):
            for kt in range(KT):
                if kt % 3:
                    dve.wait_ge(s["whi"], kt + 1)
                    dve.tensor_tensor(wlo[:, kt, :], g.x1[:, kt, :], whi[:, kt, :], ALU.subtract).then_inc(s["wlo"], 1)
            diagonals(dve)
            dve.wait_ge(s_row, rows)
            dve.wait_ge(s["vec"], 48)
            dve.tensor_tensor(vec[:, 2, :], vec[:, 2, :], g.g2[:], ALU.mult).then_inc(s["brow"], 1)

            def statistics(t, x):
                for h in range(2):
                    dve.bn_stats(st[x][:, h, :], y[t.f][:, h * HALF:(h + 1) * HALF]).then_inc(s[("s1", "s2")[x]], 1)
                wait(dve, t, ("s1", "s2")[x], 2)
                dve.sem_inc(s["seen"], 1)
                dve.bn_aggr(mv[x][t.f][:], st[x][:].rearrange("p a b -> p (a b)")).then_inc(s[("v1", "v2")[x]], 1)

            def scale(t, x):
                r, n = rs[x][t.f], ("r1", "r2")[x]
                wait(dve, t, ("sd1", "sd2")[x])
                dve.reciprocal(r[:, 0:1], r[:, 0:1]).then_inc(s[n], 1)
                wait(dve, t, n, 2, 1)
                dve.scalar_tensor_tensor(r[:, 1:2], mv[x][t.f][:, 0:1], -1.0, r[:, 0:1], ALU.mult, ALU.mult).then_inc(s[n], 1)

            def keep(t):
                if t is not None:
                    dve.scalar_tensor_tensor(tile(t), y[t.f][:], ALPHA, vec[:, 2, :], ALU.mult, ALU.add).then_inc(s["keep"], 1)

            def turn(t):
                wait(dve, two(t), "n2")
                for h in range(2):
                    at = slice(h * HALF, (h + 1) * HALF)
                    wait(dve, t, "mm", 2, h + 1)
                    dve.tensor_tensor(y[t.f][:, at], ps[t.f][:, at], g.g1[:, at], ALU.mult).then_inc(s["gm"], 1)
                if t.f == 0:
                    dve.wait_ge(s_x[0], (t.p + t.dp) * 16 + 16)
                else:
                    dve.wait_ge(s_x[1], (t.p + t.dp) * 16 + 16)
                for h in range(2):
                    at = slice(h * HALF, (h + 1) * HALF)
                    wait(dve, t, "gm", 2, h + 1)
                    dve.scalar_tensor_tensor(y[t.f][:, at], xt[t.f][:, at], ALPHA, y[t.f][:, at], ALU.mult, ALU.add).then_inc(s["y"], 1)
                wait(dve, t, "y", 2)
                wait(dve, t.before(), "v1")
                statistics(t, 0)
                keep(t.before())
                scale(t, 0)
                wait(dve, t, "n1")
                dve.tensor_tensor(y[t.f][:], y[t.f][:], vec[:, 0, :], ALU.mult).then_inc(s["gain"], 1)
                wait(dve, t, "gain")
                dve.tensor_tensor(y[t.f][:], y[t.f][:], vec[:, 1, :], ALU.add).then_inc(s["bias"], 1)
                wait(dve, t, "bias")
                wait(dve, t.before(), "v2")
                statistics(t, 1)
                scale(t, 1)

            def epilogue(t):
                keep(t)
                low(dve, t)

            run(dve, turn, epilogue)

        @block.tensor
        def _(pe):
            credit(pe, g.ff.used)
            pe.wait_ge(s["wlo"], KT)

            def turned_tile(t):
                if t is None:
                    return
                wait(pe, t, "n2")
                wait(pe, t.before(), "hf", KT)
                for kt in range(KT):
                    last = pe.transpose(turned[:, kt * P:(kt + 1) * P], yn[t.f][:, kt * P:(kt + 1) * P], g.tile("ident"))
                last.then_inc(s["turn"], 1)

            def turn(t):
                wait(pe, two(t), "gm", 2)
                for h in range(2):
                    gemm_tokens(pe, ps[t.f][:, h * HALF:(h + 1) * HALF], g.b_hi, g.b_lo, tok(t), whi, wlo,
                                slice(h * HALF, (h + 1) * HALF), range(KT)).then_inc(s["mm"], 1)
                    if h == 0:
                        if t.before() is None:
                            spread(pe)
                        turned_tile(two(t))

            def epilogue(t):
                turned_tile(t.before())
                turned_tile(t)

            run(pe, turn, epilogue)


def ff_weights(nc, es, a):
    ff = Net()
    w1 = a["w_ff1"][0].rearrange("(k p) n -> p k n", p=P)
    stage, ff.hi, ff.lo = ([es.enter_context(nc.sbuf_tensor(f"ff1_{n}{u}", [P, KT, P], d)) for u in range(2)]
                           for n, d in (("stage", F32), ("hi", BF16), ("lo", BF16)))
    loaded, hi_ready, ff.lo_ready, ff.used = ([nc.alloc_semaphore(f"ff1_{n}{u}") for u in range(2)] for n in "in hi lo used".split())

    def load(sp, m, u, col):
        sp.wait_ge(ff.lo_ready[u], m + 1)
        sp.dma_start(stage[u][:], w1[:, :, ds(col, P)]).then_inc(loaded[u], 16)

    def split_hi(act, m, u):
        act.wait_ge(loaded[u], m * 16 + 16)
        act.wait_ge(ff.used[u], m + 1)
        act.activation(ff.hi[u][:], stage[u][:], ACT.Copy).then_inc(hi_ready[u], 1)

    def split_lo(pool, m, u):
        pool.wait_ge(hi_ready[u], m + 1)
        pool.tensor_tensor(ff.lo[u][:], stage[u][:], ff.hi[u][:], ALU.subtract).then_inc(ff.lo_ready[u], 1)

    ff.load, ff.split_hi, ff.split_lo = load, split_hi, split_lo
    return ff


def phase_mlp(nc, g, a, out):
    with ExitStack() as es:
        sb = lambda n, s, d=F32: es.enter_context(nc.sbuf_tensor(f"ff_{n}", s, d))
        sem = lambda n: nc.alloc_semaphore(f"ffs_{n}")
        GT = 4
        NGR = DFF // P // GT
        w2 = a["w_ff2"][0].rearrange("(g k p) n -> p (g k) n", p=P, k=GT)
        st2, hi2, lo2 = sb("st2", [P, GT, D]), sb("hi2", [P, GT, D], BF16), sb("lo2", [P, GT, D], BF16)
        r = [sb(f"r{u}", [P, SEQ]) for u in range(2)]
        ps1 = [es.enter_context(nc.psum_tensor(f"ff_ps1_{u}", [P, SEQ], F32)) for u in range(2)]
        ps2 = [es.enter_context(nc.psum_tensor(f"ff_ps2_{u}", [P, HALF], F32)) for u in range(4)]
        ff, s_used1 = g.ff, g.ff.used
        s_relu, s_sq, s_uhi, s_ulo = ([sem(f"{n}{u}") for u in range(2)] for n in "relu sq uhi ulo".split())
        s_l2, s_m2, s_h2, s_o2, s_mm2, s_acc = (sem(n) for n in "l2 m2 h2 o2 mm2 acc".split())
        NO = 2 * TT
        vec = sb("vec", [P, 2, D])
        st, mv, rs = sb("st", [P, TT, 2, 6]), sb("mv", [P, TT, 2]), sb("rs", [P, TT, 2])
        s_vec, s_st, s_mv, s_sd, s_rs, s_xn, s_gain, s_bias, s_out = (sem(n) for n in "vec st mv sd rs xn gain bias out".split())
        block = es.enter_context(nc.Block())

        def steps(eng, first, step):
            first()
            with eng.Fori(0, (NGR - 2) // 2) as r_:
                for par in range(2):
                    step(r_ * 2 + par, par, False)
            step(NGR - 2, 0, False)
            step(NGR - 1, 1, True)

        @block.sync
        def _(sp):
            def group(gr, first):
                for t in range(first, GT):
                    ff.load(sp, gr * 2 + t // 2, t % 2, gr * (GT * P) + t * P)
                sp.wait_ge(s_o2, gr * GT + 1)
                sp.dma_start(st2[:], w2[:, ds(gr * GT, GT), :]).then_inc(s_l2, 16)

            group(0, 2)
            with sp.Fori(1, NGR) as gr:
                group(gr, 0)
            for x, v in enumerate((a["ln2_g"][0], a["ln2_b"][0])):
                sp.dma_start(vec[:, x, :], v.partition_broadcast(P)).then_inc(s_vec, 16)
            for t in range(TT):
                sp.wait_ge(s_bias, t + 1)
                sp.dma_start(out[t * P:(t + 1) * P, :], g.x1[:, t, :]).then_inc(s_out, 16)
            sp.wait_ge(s_out, 16 * TT)

        @block.scalar
        def _(act):
            b1 = ROWS["bff1"][0]

            def group(gr, par, last):
                for t in range(GT):
                    u, m = t % 2, gr * 2 + t // 2
                    act.wait_ge(s_used1[u], m + 2)
                    act.wait_ge(s_ulo[u], m + 1)
                    act.activation(r[u][:], ps1[u][:], ACT.Relu, bias=g.cols[:, ds(gr * GT + (b1 + t), 1)]).then_inc(s_relu[u], 1)
                    if not (last and t >= 2):
                        ff.split_hi(act, m + 1, u)
                    act.wait_ge(s_sq[u], m + 1)
                    act.activation(g.c_hi[:, GT * par + t, :], r[u][:], ACT.Copy).then_inc(s_uhi[u], 1)

            def split2(gr):
                act.wait_ge(s_m2, gr * GT + GT)
                for k in range(GT):
                    act.activation(hi2[:, k, :], st2[:, k, :], ACT.Copy).then_inc(s_h2, 1)

            def first():
                group(0, 0, False)
                split2(0)

            def step(i, par, last):
                if not last:
                    group(i + 1, 1 - par, isinstance(i, int))
                    act.wait_ge(s_mm2, i * NO + NO)
                    split2(i + 1)

            credit(act, s_relu)
            steps(act, first, step)
            for t in range(TT):
                act.wait_ge(s_mv, t + 1)
                act.activation(rs[:, t, 0:1], mv[:, t, 1:2], ACT.Sqrt, bias=g.misc(3)).then_inc(s_sd, 1)
                act.wait_ge(s_rs, 2 * t + 2)
                act.activation(g.x1[:, t, :], g.x1[:, t, :], ACT.Identity, bias=rs[:, t, 1:2], scale=rs[:, t, 0:1]).then_inc(s_xn, 1)

        @block.gpsimd
        def _(pool):
            credit(pool, s_ulo + [s_o2])

            def group(gr, par, last):
                for t in range(GT):
                    u, m = t % 2, gr * 2 + t // 2
                    if not (last and t >= 2):
                        ff.split_lo(pool, m + 1, u)
                    pool.wait_ge(s_uhi[u], m + 1)
                    pool.tensor_tensor(g.c_lo[:, GT * par + t, :], r[u][:], g.c_hi[:, GT * par + t, :], ALU.subtract).then_inc(s_ulo[u], 1)

            def split2(gr):
                for k in range(GT):
                    pool.wait_ge(s_h2, gr * GT + k + 1)
                    pool.tensor_tensor(lo2[:, k, :], st2[:, k, :], hi2[:, k, :], ALU.subtract).then_inc(s_o2, 1)

            def first():
                group(0, 0, False)
                split2(0)

            def step(i, par, last):
                if not last:
                    group(i + 1, 1 - par, isinstance(i, int))
                    split2(i + 1)

            steps(pool, first, step)
            for t in range(TT):
                pool.wait_ge(s_gain, t + 1)
                pool.tensor_tensor(g.x1[:, t, :], g.x1[:, t, :], vec[:, 1, :], ALU.add).then_inc(s_bias, 1)

        @block.vector
        def _(dve):
            credit(dve, [s_acc])

            def norm(t, done):
                dve.wait_ge(s_acc, done)
                for h in range(2):
                    dve.bn_stats(st[:, t, h, :], g.x1[:, t, h * HALF:(h + 1) * HALF]).then_inc(s_st, 1)
                dve.wait_ge(s_st, 2 * t + 2)
                dve.bn_aggr(mv[:, t, :], st[:, t, :, :].rearrange("p a b -> p (a b)")).then_inc(s_mv, 1)
                if t:
                    gain(t - 1)
                dve.wait_ge(s_sd, t + 1)
                dve.reciprocal(rs[:, t, 0:1], rs[:, t, 0:1]).then_inc(s_rs, 1)
                dve.wait_ge(s_rs, 2 * t + 1)
                dve.scalar_tensor_tensor(rs[:, t, 1:2], mv[:, t, 0:1], -1.0, rs[:, t, 0:1], ALU.mult, ALU.mult).then_inc(s_rs, 1)

            def gain(t):
                dve.wait_ge(s_vec, 32)
                dve.wait_ge(s_xn, t + 1)
                dve.tensor_tensor(g.x1[:, t, :], g.x1[:, t, :], vec[:, 0, :], ALU.mult).then_inc(s_gain, 1)

            def scale2(gr):
                dve.wait_ge(s_l2, gr * 16 + 16)
                for k in range(GT):
                    dve.tensor_tensor(st2[:, k, :], st2[:, k, :], g.g2[:], ALU.mult).then_inc(s_m2, 1)

            def group(gr):
                for t in range(GT):
                    u, m = t % 2, gr * 2 + t // 2
                    dve.wait_ge(s_relu[u], m + 2)
                    dve.tensor_tensor(r[u][:], r[u][:], r[u][:], ALU.mult).then_inc(s_sq[u], 1)

            def first():
                scale2(0)
                group(0)

            def step(i, par, last):
                if not last:
                    scale2(i + 1)
                    group(i + 1)
                for x in range(NO):
                    t, h = x // 2, x % 2
                    dve.wait_ge(s_mm2, i * NO + x + 1)
                    acc = g.x1[:, t, h * HALF:(h + 1) * HALF]
                    dve.tensor_tensor(acc, ps2[x % 4][:], acc, ALU.add).then_inc(s_acc, 1)
                    if last and h:
                        norm(t, i * NO + x + 2)
                if last:
                    gain(TT - 1)

            steps(dve, first, step)

        @block.tensor
        def _(pe):
            def group(gr):
                for t in range(GT):
                    u, m = t % 2, gr * 2 + t // 2
                    pe.wait_ge(ff.lo_ready[u], m + 2)
                    pe.wait_ge(s_relu[u], m + 1)
                    gemm_rows(pe, ps1[u], ff.hi[u], ff.lo[u], g.a_hi, g.a_lo, range(KT), range(KT)).then_inc(s_used1[u], 1)

            def second(i, par):
                pe.wait_ge(s_o2, i * GT + GT + 1)
                for u in range(2):
                    pe.wait_ge(s_ulo[u], i * 2 + 3)
                for x in range(NO):
                    t, h = x // 2, x % 2
                    pe.wait_ge(s_acc, i * NO + (x - 3 if x > 3 else 0) + 1)
                    gemm_tokens(pe, ps2[x % 4][:], g.c_hi, g.c_lo, slice(t * P, (t + 1) * P), hi2, lo2,
                                slice(h * HALF, (h + 1) * HALF), range(GT * par, GT * par + GT)).then_inc(s_mm2, 1)

            def step(i, par, last):
                if not last:
                    group(i + 1)
                second(i, par)

            steps(pe, lambda: group(0), step)


def setup(nc, es):
    g = Net()
    sb = lambda n, s, d=F32: es.enter_context(nc.sbuf_tensor(n, s, d))
    g.const = sb("const", [P, len(CT), P])
    g.tile = lambda n: g.const[:, CT[n], :]
    g.misc = lambda n: g.const[:, CT["misc"], n:n + 1]
    g.reset = sb("reset", [P, HALF])
    g.cols = sb("cols", [P, P + KT])
    g.idb = sb("idb", [P, P], BF16)
    g.negb = sb("negb", [P, P], BF16)
    g.ada = sb("ada", [P, 6 * KT])
    g.csil = sb("csil", [P, KT])
    g.ones = sb("ones", [P, P])
    g.a_hi = sb("a_hi", [P, KT, SEQ], BF16)
    g.a_lo = sb("a_lo", [P, KT, SEQ], BF16)
    g.c_hi = sb("c_hi", [P, KT, SEQ], BF16)
    g.c_lo = sb("c_lo", [P, KT, SEQ], BF16)
    return g


def build(nc, a, out):
    with ExitStack() as es:
        g = setup(nc, es)
        with ExitStack() as shifted:
            g.z = shifted.enter_context(nc.sbuf_tensor("z", [P, NSH, SEQ], F32))
            with nc.cleanup_on_exit():
                phase_start(nc, g, a)
            with nc.cleanup_on_exit():
                phase_recurrence(nc, g, a)
            with nc.cleanup_on_exit():
                phase_stick(nc, g, a)
        g.g1, g.g2 = (es.enter_context(nc.sbuf_tensor(n, [P, D], F32)) for n in ("g1", "g2"))
        g.x1 = es.enter_context(nc.sbuf_tensor("x1", [P, TT, D], F32))
        with nc.cleanup_on_exit(), ExitStack() as weights:
            g.s_wout = nc.alloc_semaphore("w_out_in")
            g.ff = ff_weights(nc, weights, a)
            with ExitStack() as scope:
                g.b_hi, g.b_lo = (scope.enter_context(nc.sbuf_tensor(n, [P, KT, SEQ], BF16)) for n in ("b_hi", "b_lo"))
                phase_merge(nc, g, a)
                phase_out(nc, g, a)
            phase_mlp(nc, g, a, out[0])


_INS = ["x", "c", "w_ada", "b_ada", "w_in", "mu_shift", "rw_w0", "rw_w2", "rw_a0", "rw_a2", "rw_g2", "rw_kk", "rw_ka", "rw_rk",
        "rw_gn_g", "rw_gn_b", "w_branch_a", "w_branch_b", "w_out", "ln1_g", "ln1_b", "w_ff1", "b_ff1", "w_ff2", "b_ff2",
        "ln2_g", "ln2_b"]


def kernel(**inputs):
    import concourse.bacc as bacc
    from concourse.bass_utils import run_bass_kernel_spmd

    nc = bacc.Bacc("TRN2", target_bir_lowering=False, num_devices=1)
    tiles, reset = constants()
    arrays = {n: np.ascontiguousarray(inputs[n]) for n in _INS} | {"const_tiles": tiles, "const_reset": reset}
    aps = {n: nc.dram_tensor(n, v.shape, mybir.dt.from_np(v.dtype), kind="ExternalInput").ap() for n, v in arrays.items()}
    out = nc.dram_tensor("out", [1, SEQ, D], F32, kind="ExternalOutput").ap()
    build(nc, aps, out)
    r = run_bass_kernel_spmd(nc, [arrays], core_ids=[0])
    return r.results[0]["out"]
```
